# Optimizing a Trainium2 kernel written in Bass

```python
import math
import jax
import jax.numpy as jnp
from jax import lax
import numpy as np

D_MODEL = 1024
BATCH = 1
SEQ = 256
DEPTH = 2
DEC_BATCH = 8
DEC_SEQ = 4
PAST_LEN = 256
PAGE_SIZE = 128

HEAD_DIM = 64
H_A = 8
H_B = 8
KV_B = 2
G_B = H_B // KV_B
H_IDX = 8
D_IDX = 64
MOBA_BLOCK = 256
MOBA_TOPK = 3
DSA_TOPK = 256
NUM_BUCKETS = 32
MAX_DISTANCE = 128
D_CONV = D_MODEL
CONV_W = 3
N_GROUPS = 4
EXPERTS_PER_GROUP = 8
N_EXPERTS = N_GROUPS * EXPERTS_PER_GROUP
EXPERT_TOPK = 2
D_EXPERT = D_MODEL // 2
EXPERT_ROWS = 128
MOBA_Q_CHUNK = 32
DSA_Q_CHUNK = 128
LN_EPS = 1e-5
N_ATTN_LAYERS = (DEPTH + 1) // 2
N_CONV_LAYERS = DEPTH // 2
ATTN_COLS = (H_A * HEAD_DIM, H_A * HEAD_DIM, H_A * HEAD_DIM,
             H_B * HEAD_DIM, KV_B * HEAD_DIM, KV_B * HEAD_DIM,
             H_IDX * D_IDX, D_IDX, H_IDX)
ATTN_SPLITS = tuple(int(s) for s in np.cumsum(ATTN_COLS)[:-1])
ATTN_IN = sum(ATTN_COLS)
ATTN_OUT = (H_A + H_B) * HEAD_DIM

kernel_name = 'hybrid_moba_dsa_shortconv_hmoe_step'

F32 = jnp.float32

def layer_norm(x, g, b):
    xf = x.astype(F32)
    mu = jnp.mean(xf, axis=-1, keepdims=True)
    var = jnp.mean(jnp.square(xf - mu), axis=-1, keepdims=True)
    return ((xf - mu) * lax.rsqrt(var + LN_EPS) * g + b).astype(x.dtype)

def rel_bucket(dist):
    n = jnp.maximum(dist, 0)
    max_exact = NUM_BUCKETS // 2
    nf = jnp.maximum(n, 1).astype(F32)
    large = max_exact + (jnp.log(nf / max_exact) / math.log(MAX_DISTANCE / max_exact)
                         * (NUM_BUCKETS - max_exact)).astype(jnp.int32)
    large = jnp.minimum(large, NUM_BUCKETS - 1)
    return jnp.where(n < max_exact, n, large)

def to_chunks(a, c):
    b, t = a.shape[:2]
    return jnp.moveaxis(a.reshape((b, t // c, c) + a.shape[2:]), 1, 0)

def from_chunks(a):
    n, b, c, f = a.shape
    return jnp.moveaxis(a, 0, 1).reshape(b, n * c, f)

def gather_pages(pool, page_table):
    rows = pool[page_table]
    return rows.reshape((page_table.shape[0], -1) + pool.shape[2:])

def moba_attend(q, k, v, q_pos, bias_a, q_chunk):
    b, t, h, dh = q.shape
    l = k.shape[1]
    nb = -(-l // MOBA_BLOCK)
    pad = ((0, 0), (0, nb * MOBA_BLOCK - l), (0, 0), (0, 0))
    kb = jnp.pad(k, pad).reshape(b, nb, MOBA_BLOCK, h, dh).transpose(0, 3, 1, 2, 4)
    vb = jnp.pad(v, pad).reshape(b, nb, MOBA_BLOCK, h, dh).transpose(0, 3, 1, 2, 4)
    k_mean = jnp.mean(kb.astype(F32), axis=3)
    top = min(MOBA_TOPK, nb)
    blk = jnp.arange(MOBA_BLOCK, dtype=jnp.int32)
    b_ix = jnp.arange(b)[:, None, None, None]
    h_ix = jnp.arange(h)[None, None, :, None]
    h_ix5 = h_ix[..., None]
    scale = 1.0 / math.sqrt(dh)

    def chunk(args):
        qc, pc = args
        c = qc.shape[1]
        own = pc // MOBA_BLOCK
        gate = jnp.einsum('bchd,bhnd->bchn', qc.astype(F32), k_mean)
        past = jnp.arange(nb)[None, :] < own[:, None]
        gate = jnp.where(past[None, :, None, :], gate, -jnp.inf)
        _, sel = lax.top_k(gate, top)
        sel_ok = sel < own[None, :, None, None]
        ks = kb[b_ix, h_ix, sel]
        vs = vb[b_ix, h_ix, sel]
        ko = kb[:, :, own].transpose(0, 2, 1, 3, 4)
        vo = vb[:, :, own].transpose(0, 2, 1, 3, 4)
        dist_sel = pc[None, :, None, None, None] - (sel[..., None] * MOBA_BLOCK + blk)
        s_sel = (jnp.einsum('bchd,bchkld->bchkl', qc, ks).astype(F32) * scale
                 + bias_a[rel_bucket(dist_sel), h_ix5].astype(F32))
        s_sel = jnp.where(sel_ok[..., None], s_sel, -jnp.inf)
        dist_own = pc[:, None] - (own[:, None] * MOBA_BLOCK + blk[None, :])
        s_own = (jnp.einsum('bchd,bchld->bchl', qc, ko).astype(F32) * scale
                 + bias_a[rel_bucket(dist_own)].transpose(0, 2, 1)[None].astype(F32))
        s_own = jnp.where((dist_own >= 0)[None, :, None, :], s_own, -jnp.inf)
        s = jnp.concatenate([s_sel.reshape(b, c, h, top * MOBA_BLOCK), s_own], axis=-1)
        p = jax.nn.softmax(s, axis=-1).astype(v.dtype)
        p_sel = p[..., :top * MOBA_BLOCK].reshape(s_sel.shape)
        p_own = p[..., top * MOBA_BLOCK:]
        o = (jnp.einsum('bchkl,bchkld->bchd', p_sel, vs)
             + jnp.einsum('bchl,bchld->bchd', p_own, vo))
        return o.reshape(b, c, h * dh)

    out = lax.map(chunk, (to_chunks(q, q_chunk), q_pos.reshape(-1, q_chunk)))
    return from_chunks(out)

def dsa_attend(q, k, v, q_idx, w_idx, k_idx, q_pos, bias_b, k_sel, q_chunk):
    b, t, h, dh = q.shape
    l = k.shape[1]
    k_pos = jnp.arange(l, dtype=jnp.int32)
    kif = k_idx.astype(F32)
    b_ix = jnp.arange(b)[:, None, None]
    scale = 1.0 / math.sqrt(dh)
    idx_scale = 1.0 / math.sqrt(D_IDX * H_IDX)

    def chunk(args):
        qc, qic, wc, pc = args
        c = qc.shape[1]
        s_idx = jnp.einsum('bchd,bld->bchl', qic.astype(F32), kif)
        score = jnp.einsum('bchl,bch->bcl', jax.nn.relu(s_idx), wc.astype(F32)) * idx_scale
        score = jnp.where((k_pos[None, :] <= pc[:, None])[None], score, -jnp.inf)
        _, idx = lax.top_k(score, k_sel)
        dist = pc[None, :, None] - idx
        ks = k[b_ix, idx]
        vs = v[b_ix, idx]
        qg = qc.reshape(b, c, KV_B, G_B, dh)
        s = jnp.einsum('bcngd,bcknd->bcngk', qg, ks).astype(F32) * scale
        bias = bias_b[rel_bucket(dist)].reshape(b, c, k_sel, KV_B, G_B).transpose(0, 1, 3, 4, 2)
        s = jnp.where((dist >= 0)[:, :, None, None, :], s + bias.astype(F32), -jnp.inf)
        p = jax.nn.softmax(s, axis=-1).astype(v.dtype)
        o = jnp.einsum('bcngk,bcknd->bcngd', p, vs)
        return o.reshape(b, c, h * dh)

    out = lax.map(chunk, (to_chunks(q, q_chunk), to_chunks(q_idx, q_chunk),
                          to_chunks(w_idx, q_chunk), q_pos.reshape(-1, q_chunk)))
    return from_chunks(out)

def attn_mixer(x, q_pos, past, w_in, w_out, rel_bias, moba_chunk, dsa_chunk):
    b, t, _ = x.shape
    qa, ka, va, qb, kb, vb, qi, ki, wi = jnp.split(x @ w_in, ATTN_SPLITS, axis=-1)
    qa = qa.reshape(b, t, H_A, HEAD_DIM)
    ka = ka.reshape(b, t, H_A, HEAD_DIM)
    va = va.reshape(b, t, H_A, HEAD_DIM)
    qb = qb.reshape(b, t, H_B, HEAD_DIM)
    kb = kb.reshape(b, t, KV_B, HEAD_DIM)
    vb = vb.reshape(b, t, KV_B, HEAD_DIM)
    qi = qi.reshape(b, t, H_IDX, D_IDX)
    new_rows = (ka, va, kb, vb, ki)
    if past is None:
        full = new_rows
    else:
        full = tuple(jnp.concatenate([p.astype(n.dtype), n], axis=1) for p, n in zip(past, new_rows))
    ka_f, va_f, kb_f, vb_f, ki_f = full
    k_sel = min(DSA_TOPK, ka_f.shape[1] // 4)
    ya = moba_attend(qa, ka_f, va_f, q_pos, rel_bias[:, :H_A], moba_chunk)
    yb = dsa_attend(qb, kb_f, vb_f, qi, wi, ki_f, q_pos, rel_bias[:, H_A:], k_sel, dsa_chunk)
    y = jnp.concatenate([ya, yb], axis=-1) @ w_out
    return y, new_rows

def conv_mixer(x, past_u, w_in, conv_w, w_out):
    b, t, _ = x.shape
    h, gate_b, gate_c = jnp.split(x @ w_in, 3, axis=-1)
    u = gate_c * h
    if past_u is None:
        past_u = jnp.zeros((b, CONV_W - 1, D_CONV), u.dtype)
    up = jnp.concatenate([past_u.astype(u.dtype), u], axis=1)
    c = sum(up[:, j:j + t] * conv_w[j] for j in range(CONV_W))
    y = (gate_b * c) @ w_out
    return y, up[:, t:]

def routed_experts(x2, e_idx, gates, w_gate, w_up, w_down):
    n, d = x2.shape
    a = n * EXPERT_TOPK
    e_flat = e_idx.reshape(a)
    tok_flat = jnp.repeat(jnp.arange(n, dtype=jnp.int32), EXPERT_TOPK)
    g_flat = gates.reshape(a)
    order = jnp.argsort(e_flat).astype(jnp.int32)
    e_sorted = e_flat[order]
    counts = jnp.bincount(e_flat, length=N_EXPERTS)
    padded = (counts + EXPERT_ROWS - 1) // EXPERT_ROWS * EXPERT_ROWS
    end_pad = jnp.cumsum(padded)
    start_pad = end_pad - padded
    start = jnp.cumsum(counts) - counts
    dest = start_pad[e_sorted] + jnp.arange(a, dtype=jnp.int32) - start[e_sorted]
    n_blocks = -(-a // EXPERT_ROWS) + N_EXPERTS
    row_src = jnp.full((n_blocks * EXPERT_ROWS,), a, jnp.int32).at[dest].set(order)
    valid = row_src < a
    src = jnp.minimum(row_src, a - 1)
    tok_rows = tok_flat[src]
    g_rows = jnp.where(valid, g_flat[src], 0).astype(x2.dtype)
    block_expert = jnp.minimum(
        jnp.searchsorted(end_pad, jnp.arange(n_blocks, dtype=jnp.int32) * EXPERT_ROWS, side='right'),
        N_EXPERTS - 1)
    xr = x2[tok_rows].reshape(n_blocks, EXPERT_ROWS, d)

    def block_ffn(args):
        xb, e = args
        hdn = jax.nn.silu(xb @ w_gate[e]) * (xb @ w_up[e])
        return hdn @ w_down[e]

    yr = lax.map(block_ffn, (xr, block_expert)).reshape(-1, d)
    return jnp.zeros_like(x2).at[tok_rows].add(yr * g_rows[:, None])

def hier_moe(x, w_rg, b_rg, w_re, b_re, w_gate, w_up, w_down):
    b, t, d = x.shape
    x2 = x.reshape(b * t, d)
    p_group = jax.nn.softmax((x2 @ w_rg + b_rg).astype(F32), axis=-1)
    g_val, g_idx = lax.top_k(p_group, 1)
    logit_e = (x2 @ w_re + b_re).astype(F32).reshape(-1, N_GROUPS, EXPERTS_PER_GROUP)
    logit_e = jnp.take_along_axis(logit_e, g_idx[:, :, None], axis=1)[:, 0]
    p_exp = jax.nn.softmax(logit_e, axis=-1)
    e_val, e_loc = lax.top_k(p_exp, EXPERT_TOPK)
    gates = g_val * e_val / jnp.sum(e_val, axis=-1, keepdims=True)
    e_idx = g_idx * EXPERTS_PER_GROUP + e_loc
    y = routed_experts(x2, e_idx, gates.astype(x.dtype), w_gate, w_up, w_down)
    return y.reshape(b, t, d)

def stack_rows(rows, j):
    return jnp.stack([r[j] for r in rows])

def setup_inputs(seed: int = 0) -> dict:
    key = jax.random.key(seed)
    ks = jax.random.split(key, 24)
    n_pages = PAST_LEN // PAGE_SIZE
    n_phys = (DEC_BATCH * n_pages * 5) // 4
    beta = (8 * DEPTH) ** -0.25

    def nrm(k, shape, s):
        return jax.random.normal(k, shape, F32) * s

    col_scale = np.concatenate([np.full((c,), beta if i in (2, 5) else 1.0, np.float32)
                                for i, c in enumerate(ATTN_COLS)])
    page_table = jax.random.permutation(ks[8], n_phys)[:DEC_BATCH * n_pages]
    page_table = page_table.reshape(DEC_BATCH, n_pages).astype(jnp.int32)
    return {
        'x_prompt': nrm(ks[0], (BATCH, SEQ, D_MODEL), 1.0),
        'x_sample': nrm(ks[1], (DEC_BATCH, DEC_SEQ, D_MODEL), 1.0),
        'cache_k_a': nrm(ks[2], (N_ATTN_LAYERS, n_phys, PAGE_SIZE, H_A, HEAD_DIM), 1.0),
        'cache_v_a': nrm(ks[3], (N_ATTN_LAYERS, n_phys, PAGE_SIZE, H_A, HEAD_DIM), 1.0),
        'cache_k_b': nrm(ks[4], (N_ATTN_LAYERS, n_phys, PAGE_SIZE, KV_B, HEAD_DIM), 1.0),
        'cache_v_b': nrm(ks[5], (N_ATTN_LAYERS, n_phys, PAGE_SIZE, KV_B, HEAD_DIM), 1.0),
        'cache_k_idx': nrm(ks[6], (N_ATTN_LAYERS, n_phys, PAGE_SIZE, D_IDX), 1.0),
        'state_conv': nrm(ks[7], (N_CONV_LAYERS, DEC_BATCH, CONV_W - 1, D_CONV), 1.0),
        'page_table': page_table,
        'rel_bias': nrm(ks[9], (NUM_BUCKETS, H_A + H_B), 0.5),
        'w_attn_in': nrm(ks[10], (N_ATTN_LAYERS, D_MODEL, ATTN_IN), D_MODEL ** -0.5) * col_scale,
        'w_attn_out': nrm(ks[11], (N_ATTN_LAYERS, ATTN_OUT, D_MODEL), ATTN_OUT ** -0.5 * beta),
        'w_conv_in': nrm(ks[12], (N_CONV_LAYERS, D_MODEL, 3 * D_CONV), D_MODEL ** -0.5),
        'conv_w': nrm(ks[13], (N_CONV_LAYERS, CONV_W, D_CONV), CONV_W ** -0.5),
        'w_conv_out': nrm(ks[14], (N_CONV_LAYERS, D_CONV, D_MODEL), D_CONV ** -0.5 * beta),
        'w_router_group': nrm(ks[15], (DEPTH, D_MODEL, N_GROUPS), D_MODEL ** -0.5),
        'b_router_group': nrm(ks[16], (DEPTH, N_GROUPS), 0.01),
        'w_router_expert': nrm(ks[17], (DEPTH, D_MODEL, N_EXPERTS), D_MODEL ** -0.5),
        'b_router_expert': nrm(ks[18], (DEPTH, N_EXPERTS), 0.01),
        'w_exp_gate': nrm(ks[19], (DEPTH, N_EXPERTS, D_MODEL, D_EXPERT), D_MODEL ** -0.5),
        'w_exp_up': nrm(ks[20], (DEPTH, N_EXPERTS, D_MODEL, D_EXPERT), D_MODEL ** -0.5 * beta),
        'w_exp_down': nrm(ks[21], (DEPTH, N_EXPERTS, D_EXPERT, D_MODEL), D_EXPERT ** -0.5 * beta),
        'ln_g': 1.0 + nrm(ks[22], (DEPTH, 2, D_MODEL), 0.02),
        'ln_b': nrm(ks[23], (DEPTH, 2, D_MODEL), 0.02),
    }

def reference(x_prompt, x_sample, cache_k_a, cache_v_a, cache_k_b, cache_v_b, cache_k_idx,
              state_conv, page_table, rel_bias, w_attn_in, w_attn_out, w_conv_in, conv_w,
              w_conv_out, w_router_group, b_router_group, w_router_expert, b_router_expert,
              w_exp_gate, w_exp_up, w_exp_down, ln_g, ln_b):
    alpha = (2 * DEPTH) ** 0.25
    t_p = x_prompt.shape[1]
    t_s = x_sample.shape[1]
    past_len = page_table.shape[1] * cache_k_a.shape[2]
    pos_p = jnp.arange(t_p, dtype=jnp.int32)
    pos_s = past_len + jnp.arange(t_s, dtype=jnp.int32)
    xp, xs = x_prompt, x_sample
    attn_p, attn_s, conv_p, conv_s = [], [], [], []
    for layer in range(DEPTH):
        i = layer // 2
        if layer % 2 == 0:
            past = tuple(gather_pages(c[i], page_table)
                         for c in (cache_k_a, cache_v_a, cache_k_b, cache_v_b, cache_k_idx))
            hp, rows_p = attn_mixer(xp, pos_p, None, w_attn_in[i], w_attn_out[i], rel_bias,
                                    min(MOBA_Q_CHUNK, t_p), min(DSA_Q_CHUNK, t_p))
            hs, rows_s = attn_mixer(xs, pos_s, past, w_attn_in[i], w_attn_out[i], rel_bias, 1, t_s)
            attn_p.append(rows_p)
            attn_s.append(rows_s)
        else:
            hp, st_p = conv_mixer(xp, None, w_conv_in[i], conv_w[i], w_conv_out[i])
            hs, st_s = conv_mixer(xs, state_conv[i], w_conv_in[i], conv_w[i], w_conv_out[i])
            conv_p.append(st_p)
            conv_s.append(st_s)
        xp = layer_norm(alpha * xp + hp, ln_g[layer, 0], ln_b[layer, 0])
        xs = layer_norm(alpha * xs + hs, ln_g[layer, 0], ln_b[layer, 0])
        moe_w = (w_router_group[layer], b_router_group[layer], w_router_expert[layer],
                 b_router_expert[layer], w_exp_gate[layer], w_exp_up[layer], w_exp_down[layer])
        xp = layer_norm(alpha * xp + hier_moe(xp, *moe_w), ln_g[layer, 1], ln_b[layer, 1])
        xs = layer_norm(alpha * xs + hier_moe(xs, *moe_w), ln_g[layer, 1], ln_b[layer, 1])
    return (xp, xs,
            stack_rows(attn_p, 0), stack_rows(attn_p, 1), stack_rows(attn_p, 2),
            stack_rows(attn_p, 3), stack_rows(attn_p, 4), jnp.stack(conv_p),
            stack_rows(attn_s, 0), stack_rows(attn_s, 1), stack_rows(attn_s, 2),
            stack_rows(attn_s, 3), stack_rows(attn_s, 4), jnp.stack(conv_s))


_drawn_inputs = setup_inputs


def setup_inputs(seed=0):
    import zlib

    import numpy as np

    out = dict(_drawn_inputs(seed))
    spreads = {}
    factors = {'b_router_group': 37.207, 'b_router_expert': 8.0}
    for name, (base, spread) in spreads.items():
        noise = np.random.default_rng([zlib.crc32(name.encode()), seed]).standard_normal(out[name].shape)
        drawn = base * np.exp(spread * noise) if base else spread * noise
        out[name] = jnp.asarray(drawn.astype(out[name].dtype))
    for name, factor in factors.items():
        out[name] = (out[name] * factor).astype(out[name].dtype)
    return out
```

```python
import math
from contextlib import ExitStack

import numpy as np
import concourse.bass as bass
from concourse import mybir

F32 = mybir.dt.float32
I32 = mybir.dt.int32
U32 = mybir.dt.uint32
ALU = mybir.AluOpType
ACT = mybir.ActivationFunctionType
AX = mybir.AxisListType

D = 1024
DC = D // 128
SEQ = 256
DEC_B, DEC_T = 8, 4
NS = DEC_B * DEC_T
NTOK = SEQ + NS
TILES = [(0, 128), (128, 128), (256, NS)]
DEPTH = 2
ALPHA = (2 * DEPTH) ** 0.25
EPS = 1e-5
PAST, PAGE = 256, 128
N_PAGES = PAST // PAGE
NK_S = PAST + DEC_T
HD, HA, HB, KVB, HI = 64, 8, 8, 2, 8
HEADS = HA + HB
TOPK_P = 64
TOPK_S = 65
ROUNDS_P = TOPK_P // 8
ROUNDS_S = -(-TOPK_S // 8)
PADS_S = ROUNDS_S * 8 - TOPK_S
IDX_SCALE = 1.0 / math.sqrt(64 * HI)
QK_SCALE = 1.0 / math.sqrt(HD)
NEG, TAKEN = -1e30, -3e38
ATTN_IN = 2888
NE, NG, EPG, FE = 32, 4, 8, 512
FC = FE // 128
CAP = 64
PASSES = -(-NTOK // CAP)
SLOTS = PASSES * NE * CAP
DIST0 = PAST + DEC_T - 1
TABLE_W = 388
W_BLOCKS = [(0, 512), (512, 512), (1024, 512), (1536, 512), (2048, 256), (2304, 512), (2816, 72)]
QA, KA, QB, KB, QI, KI, KBS = 0, 4, 8, 12, 13, 17, 18
PROJ = ([(0, 128 * c, 128, QA + c, None, None) for c in range(4)]
        + [(1, 128 * c, 128, KA + c, None, None) for c in range(4)]
        + [(2, 0, 512, None, t, 0) for t in range(3)]
        + [(3, 128 * c, 128, QB + c, None, None) for c in range(4)]
        + [(4, 0, 128, KB, None, None)] + [(4, 128, 128, None, t, 512) for t in range(3)]
        + [(5, 128 * c, 128, QI + c, None, None) for c in range(4)]
        + [(6, 0, 64, KI, None, None)] + [(6, 64, 8, None, t, 640) for t in range(3)])
PROJ_END = [sum(1 for p in PROJ if p[0] <= k) for k in range(len(W_BLOCKS))]
C_ID, C_TRI, C_ONE, C_IOTA, C_TOK, C_STAY = 0, 128, 256, 384, 416, 419
C_REP, C_PAT, C_HM, C_NEW, C_OH = 419, 675, 739, 747, 811
C_END = C_OH + TABLE_W


def constants():
    c = np.zeros((128, C_END), np.float32)
    i = np.arange(128)
    c[:, C_ID:C_ID + 128] = np.eye(128)
    c[:, C_TRI:C_TRI + 128] = i[:, None] < i[None, :]
    c[:, C_ONE:C_ONE + 128] = 1.0
    b, h, q = i // 32, (i // 4) % 8, i % 4
    for g in range(2):
        tok = (4 * g + b) * DEC_T + q
        c[tok, C_REP + 128 * g + i] = 1.0
        c[i, C_PAT + 32 * g + tok] = 1.0
        for j in range(DEC_T):
            c[i, C_NEW + 32 * g + (4 * g + b) * DEC_T + j] = 1.0
    c[i, C_HM + h] = 1.0
    c[:, C_IOTA:C_IOTA + 32] = np.arange(32)
    c[:, C_TOK:C_TOK + 3] = i[:, None] + 128 * np.arange(3)[None, :]
    dist = DIST0 - np.arange(TABLE_W)
    n = np.maximum(dist, 0)
    nf = np.maximum(n, 1).astype(np.float32)
    large = 16 + (np.log(nf / np.float32(16)) / np.float32(math.log(8.0)) * np.float32(16)).astype(np.int32)
    bucket = np.where(n < 16, n, np.minimum(large, 31))
    for k in range(TABLE_W):
        if dist[k] >= 0:
            c[bucket[k], C_OH + k] = 1.0 / QK_SCALE
        else:
            c[32, C_OH + k] = 1.0
    return c



def build(nc, t, stage=99):
    with ExitStack() as ctx:
        build_in(nc, t, ctx, stage)


def build_in(nc, t, ctx, stage):
    def sem(name):
        return ctx.enter_context(nc.semaphore(name))

    TOTAL = 53200
    mem = ctx.enter_context(nc.sbuf_tensor("mem", [128, TOTAL], F32))

    def region(lo, hi):
        at = [lo]

        def take(*dims):
            n = int(np.prod(dims))
            a = mem[:, at[0]:at[0] + n]
            at[0] += n + n % 2
            assert at[0] <= hi, (lo, hi, at[0])
            names = "abcd"[:len(dims)]
            if len(dims) > 1:
                sizes = {x: d for x, d in zip(names[:-1], dims)}
                a = a.rearrange("p (" + " ".join(names) + ") -> p " + " ".join(names), **sizes)
            return a
        return take

    SLOT = 3 * DC * FE
    S0 = TOTAL - 3 * SLOT
    WORK = 9350
    common = region(0, WORK)
    CST = common(C_STAY)
    X = common(3, D)
    XT = common(DC, NTOK)
    LNP = common(2, D)
    WR = common(DEPTH, DC, NG + NE)
    RBI = common(DEPTH, NG + NE)
    SLOTI, SLOTM, TOKI, IDXI, IDXC, FLAG = common(6), common(6), common(3), common(NE), common(2), common(2)
    ZERO = common(SLOTS // 128)
    NEGH, L8, GT, GATE, EF, RK, QQ, SLOTF = common(1), common(8), common(6), common(6), common(6), common(6), common(6), common(6)
    TOP8, GIX, EIX, GSUM, RR, DEN = common(8), common(8), common(8), common(3), common(3), common(3)
    HOT, HOTK, LG, PEN, RANKT, TKI, TKF = common(3, NE), common(6, NE), common(NG + NE), common(NG), common(NE), common(CAP), common(CAP)
    STATS, MV, VE, RSTD = common(12), common(3, 2), common(3), common(3)
    ID, TRI, ONE = CST[:, C_ID:C_ID + 128], CST[:, C_TRI:C_TRI + 128], CST[:, C_ONE:C_ONE + 128]
    IOTA = CST[:, C_IOTA:C_IOTA + NE]

    slots = [mem[:, S0 + k * SLOT:S0 + (k + 1) * SLOT] for k in range(3)]
    WG = [s[:, 0:4096].rearrange("p (c f) -> p c f", c=DC) for s in slots]
    WU = [s[:, 4096:8192].rearrange("p (c f) -> p c f", c=DC) for s in slots]
    WD = [s[:, 8192:12288].rearrange("p (c n) -> p c n", c=FC) for s in slots]

    slot0 = region(S0, S0 + SLOT)
    WOUT, V, KTOK = slot0(DC, D), slot0(3, 648), slot0(3, 704)
    att = region(S0 + SLOT, TOTAL)
    WIN = [att(DC, 512) for _ in range(3)]
    QKVT, YT, BM = att(19, NTOK), att(DC, NTOK), att(17, 256)
    sample = region(S0 + SLOT, S0 + SLOT + 3 * 4096)
    KRAW = [sample(N_PAGES, 704) for _ in range(2)]
    KTB = [sample(6, NK_S) for _ in range(2)]
    VRAW = [sample(N_PAGES, 640) for _ in range(2)]
    QAS, QBS, QIS, PT = sample(4, DEC_B, 32), sample(DEC_B, 32), sample(DEC_B, 32), sample(4, 3, 128)
    RIS = [sample(NK_S) for _ in range(2)]
    work = region(WORK, S0)
    PB, PTB, COMB, SELM, ACC, RELU = work(3, 256), work(2, 2, 128), work(2, 256), work(2, 256), work(2, 256), work(2, 256)
    SBIAS, SMASK, PS4, SCS = work(2, NK_S), work(NK_S), work(4, NK_S), work(NK_S + PADS_S)
    AC = work(C_END - C_STAY)
    TAB, RB = work(TABLE_W), work(17)
    MX, SUM, RIN = work(32), work(32), work(32)
    SMX, SSUM, SRIN, MX8, WVT, WV, WM, PGT, PN = work(4), work(4), work(4), work(8), work(8), work(2), work(2, 32), work(16), work(4, 32)
    REP, PAT, HM, NEW, OH = (AC[:, a - C_STAY:b - C_STAY] for a, b in (
        (C_REP, C_PAT), (C_PAT, C_HM), (C_HM, C_NEW), (C_NEW, C_OH), (C_OH, C_END)))

    moe = region(WORK, S0)
    XG, XGT, SG, HT, YO = moe(2, D), moe(2, DC, CAP), moe(2, FC, CAP), moe(2, FC, CAP), moe(2, D)
    YG = region(WORK, S0)(2, D)
    WC = [slots[1 + k // 3][:, 4096 * (k % 3):4096 * (k % 3 + 1)].rearrange("p (c n) -> p c n", c=DC) for k in range(6)]
    WCO = region(S0 + SLOT, TOTAL)(DC, D)
    ULT = region(S0 + SLOT + 8192, TOTAL)(D)
    cv = region(WORK, S0)
    ZT, UB, HSB, CB, SCW, SCT, UL = cv(DC, NTOK), cv(2, SEQ + 2 + DEC_B * 6), cv(2, NTOK), cv(2, NTOK), cv(D), cv(DC, 19), cv(DC, 18)

    bank = [ctx.enter_context(nc.psum_tensor(f"bank{i}", [128, 512], F32)) for i in range(8)]

    table_d = nc.dram_tensor("bias_table", [128, 17, TABLE_W], F32).ap()
    xrows_d = [nc.dram_tensor(f"x_rows{i}", [NTOK, D], F32).ap() for i in range(DEPTH)]
    slot_tok_d = [nc.dram_tensor(f"slot_token{i}", [SLOTS, 1], I32).ap() for i in range(DEPTH)]
    yslot_d = [nc.dram_tensor(f"slot_out{i}", [NE * CAP, D], F32).ap() for i in range(DEPTH)]
    ymore_d = [nc.dram_tensor(f"slot_more{i}", [SLOTS - NE * CAP, D], F32).ap() for i in range(DEPTH)]

    ld_const, ld_x, ld_small, ld_rb, ld_ln, ld_pt, ld_wout = (sem("ld_" + n) for n in ("const", "x", "small", "rb", "ln", "pt", "wout"))
    ld_win = [sem(f"ld_win{k}") for k in range(3)]
    st_rows, st_out, st_state, st_tab, ld_bias, ld_state, ld_wco = (sem(n) for n in ("st_rows", "st_out", "st_state", "st_tab", "ld_bias", "ld_state", "ld_wco"))
    act_own, dve_own, pool_own = sem("act_own"), sem("dve_own"), sem("pool_own")
    rb_zero, rb_set, tab_psum, tab_sb = (sem(n) for n in ("rb_zero", "rb_set", "tab_psum", "tab_sb"))
    xT_psum, xT_evac, proj_psum, proj_evac = (sem(n) for n in ("xT_psum", "xT_evac", "proj_psum", "proj_evac"))
    ktok_psum, ktok_evac = sem("ktok_psum"), sem("ktok_evac")
    idx_psum, idx_relu, idx_acc, sel_ready, comb_ready = (sem(n) for n in ("idx_psum", "idx_relu", "idx_acc", "sel_ready", "comb_ready"))
    att_S, att_scored, att_exp, att_p, att_T, att_Tevac, att_O, att_Oevac = (
        sem("att_" + n) for n in ("S", "scored", "exp", "p", "T", "Tevac", "O", "Oevac"))
    ld_k = [sem(f"ld_k{k}") for k in range(2)]
    ld_v = [sem(f"ld_v{k}") for k in range(2)]
    kt_psum, kt_evac, k_new, q_zero, q_cut, smp_S, smp_Sevac, smp_relu = (
        sem(n) for n in ("kt_psum", "kt_evac", "k_new", "q_zero", "q_cut", "smp_S", "smp_Sevac", "smp_relu"))
    w_psum, w_mat, sc_psum, sc_mask, rep_psum = (sem(n) for n in ("w_psum", "w_mat", "sc_psum", "sc_mask", "rep_psum"))
    smp_scored, smp_exp, smp_p, smp_T, smp_Tevac, smp_O, smp_y = (
        sem("smp_" + n) for n in ("scored", "exp", "p", "T", "Tevac", "O", "y"))
    op_psum, op_added, ln_stat, ln_rstd, ln_done = (sem(n) for n in ("op_psum", "op_added", "ln_stat", "ln_rstd", "ln_done"))
    ro_psum, ro_top, ro_exp, ro_hot, ro_rank, ro_slot = (sem("ro_" + n) for n in ("psum", "top", "exp", "hot", "rank", "slot"))
    st_x, zero_set, st_zero, scattered, ld_tok, tok_f, tok_T, tok_idx = (
        sem(n) for n in ("st_x", "zero_set", "st_zero", "scattered", "ld_tok", "tok_f", "tok_T", "tok_idx"))
    ld_wg = [sem(f"ld_wg{k}") for k in range(3)]
    ld_wu = [sem(f"ld_wu{k}") for k in range(3)]
    ld_wd = [sem(f"ld_wd{k}") for k in range(3)]
    gath = [sem(f"gath{k}") for k in range(2)]
    idx_cur, xg_T, xg_evac, gu_psum, silu_done, h_done, dn_psum, y_evac = (
        sem(n) for n in ("idx_cur", "xg_T", "xg_evac", "gu_psum", "silu_done", "h_done", "dn_psum", "y_evac"))
    st_y = [sem(f"st_y{k}") for k in range(2)]
    ygath = [sem(f"ygath{k}") for k in range(2)]
    y_used, pe_passed, pool_passed = sem("y_used"), sem("pe_passed"), sem("pool_passed")
    ld_wc = [sem(f"ld_wc{k}") for k in range(2)]
    cv_in_T, cv_in, cv_psum, cv_h, cv_u, cv_z, cv_lT, cv_lsb = (
        sem("cv_" + n) for n in ("in_T", "in", "psum", "h", "u", "z", "lT", "lsb"))
    more = [{n: sem(f"more{i}_{n}") for n in ("w", "tok", "gath", "T", "Tevac", "gu", "silu", "h", "dn", "y", "st", "more")} for i in range(DEPTH)]

    def linker(eng, own):
        n = [0]

        def link(ins):
            n[0] += 1
            ins.then_inc(own, 1)
            eng.wait_ge(own, n[0])
        return link

    def wait(eng, s, value):
        if isinstance(value, int) and value <= 0:
            return
        eng.wait_ge(s, value)

    def number(i, u):
        return 6 * i + u

    def slot_loads(layer, i, u):
        return 16 * (layer * (-(-(NE - u % 3) // 3)) + 2 * i + u // 3 + 1)

    def pair_count(layer, i, u):
        return 16 * (layer * (NE // 2) + 3 * i + u // 2 + 1)

    tiled = "(t p) n -> p t n"
    flat = "l b t h d -> (l b t) (h d)"
    n_more = (PASSES - 1) * NE

    block = ctx.enter_context(nc.Block())

    @block.sync
    def _(sp):
        w_in = t["w_attn_in"][0].rearrange("(c p) n -> p c n", p=128)
        sp.dma_start(CST, t["consts"][:, 0:C_STAY]).then_inc(ld_const, 16)
        sp.dma_start(AC, t["consts"][:, C_STAY:C_END]).then_inc(ld_const, 16)
        sp.dma_start(X[:, 0:2, :], t["x_prompt"][0].rearrange("(t p) d -> p t d", p=128)).then_inc(ld_x, 16)
        sp.dma_start(X[0:NS, 2, :], t["x_sample"].rearrange("b t d -> (b t) d")).then_inc(ld_x, 16)
        for k, (lo, n) in enumerate(W_BLOCKS):
            if k >= 3:
                sp.wait_ge(proj_psum, PROJ_END[k - 3])
            sp.dma_start(WIN[k % 3][:, :, 0:n], w_in[:, :, lo:lo + n]).then_inc(ld_win[k % 3], 16)
        sp.dma_start(WOUT, t["w_attn_out"][0].rearrange("(c p) n -> p c n", p=128)).then_inc(ld_wout, 16)

        def load_ln(k):
            sp.dma_start(LNP[:, 0, :], t["ln_g"][k // 2, k % 2].partition_broadcast(128)).then_inc(ld_ln, 16)
            sp.dma_start(LNP[:, 1, :], t["ln_b"][k // 2, k % 2].partition_broadcast(128)).then_inc(ld_ln, 16)

        load_ln(0)
        sp.wait_ge(proj_evac, len(PROJ))
        sp.dma_start(t["new_v_a_prompt"].rearrange(flat).rearrange(tiled, p=128), V[:, 0:2, 0:512]).then_inc(st_rows, 16)
        sp.dma_start(t["new_v_b_prompt"].rearrange(flat).rearrange(tiled, p=128), V[:, 0:2, 512:640]).then_inc(st_rows, 16)
        sp.dma_start(t["new_v_a_sample"].rearrange(flat), V[0:NS, 2, 0:512]).then_inc(st_rows, 16)
        sp.dma_start(t["new_v_b_sample"].rearrange(flat), V[0:NS, 2, 512:640]).then_inc(st_rows, 16)
        sp.wait_ge(ktok_evac, 6)
        sp.dma_start(t["new_k_a_prompt"].rearrange(flat).rearrange(tiled, p=128), KTOK[:, 0:2, 0:512]).then_inc(st_rows, 16)
        sp.dma_start(t["new_k_b_prompt"].rearrange(flat).rearrange(tiled, p=128), KTOK[:, 0:2, 512:640]).then_inc(st_rows, 16)
        sp.dma_start(t["new_k_idx_prompt"].rearrange("l b t d -> (l b t) d").rearrange(tiled, p=128), KTOK[:, 0:2, 640:704]).then_inc(st_rows, 16)
        sp.dma_start(t["new_k_a_sample"].rearrange(flat), KTOK[0:NS, 2, 0:512]).then_inc(st_rows, 16)
        sp.dma_start(t["new_k_b_sample"].rearrange(flat), KTOK[0:NS, 2, 512:640]).then_inc(st_rows, 16)
        sp.dma_start(t["new_k_idx_sample"].rearrange("l b t d -> (l b t) d"), KTOK[0:NS, 2, 640:704]).then_inc(st_rows, 16)
        pages = "l p t h d -> (l p) t (h d)"
        k_caches = [(t["cache_k_a"].rearrange(pages), 0, 512), (t["cache_k_b"].rearrange(pages), 512, 128),
                    (t["cache_k_idx"].rearrange("l p t d -> (l p) t d"), 640, 64)]
        v_caches = [(t["cache_v_a"].rearrange(pages), 0, 512), (t["cache_v_b"].rearrange(pages), 512, 128)]
        n_phys = k_caches[0][0].shape[0]
        sp.wait_ge(ld_pt, 16)
        for caches, buf, ld, used, per in ((k_caches, KRAW, ld_k, kt_psum, 3), (v_caches, VRAW, ld_v, smp_O, 1)):
            for b in range(DEC_B):
                wait(sp, used, per * (b - 1))
                for pg in range(N_PAGES):
                    page = sp.value_load(PGT[0:1, b * N_PAGES + pg:b * N_PAGES + pg + 1].bitcast(I32), min_val=0, max_val=n_phys - 1)
                    for cache, lo, n in caches:
                        sp.dma_start(buf[b % 2][:, pg, lo:lo + n], cache[page]).then_inc(ld[b % 2], 16)
        sp.wait_ge(st_rows, 160)
        if stage < 6:
            return

        def load_expert(layer, i, u, free=None):
            e, k = number(i, u), u % 3
            if free is not None:
                wait(sp, gu_psum, free)
            sp.dma_start(WG[k], t["w_exp_gate"][layer, e].rearrange("(p c) f -> p c f", c=DC)).then_inc(ld_wg[k], 16)
            sp.dma_start(WU[k], t["w_exp_up"][layer, e].rearrange("(p c) f -> p c f", c=DC)).then_inc(ld_wu[k], 16)
            if free is not None:
                wait(sp, dn_psum, free)
            sp.dma_start(WD[k], t["w_exp_down"][layer, e].rearrange("(c p) n -> p c n", p=128)).then_inc(ld_wd[k], 16)

        def experts(layer):
            base = NE * layer
            sp.wait_ge(ln_done, 6 * layer + 3)
            sp.dma_start(xrows_d[layer][0:SEQ].rearrange(tiled, p=128), X[:, 0:2, :]).then_inc(st_x, 16)
            sp.dma_start(xrows_d[layer][SEQ:NTOK], X[0:NS, 2, :]).then_inc(st_x, 16)
            load_ln(2 * layer + 1)
            for u in (3, 4, 5):
                load_expert(layer, 0, u, base + u - 2)
            with sp.Fori(1, NE // 6) as i:
                for u in range(6):
                    load_expert(layer, i, u, base + number(i, u) - 2)
            for u in range(NE % 6):
                load_expert(layer, NE // 6, u, base + number(NE // 6, u) - 2)
            s = more[layer]
            full = sp.value_load(FLAG[0:1, layer:layer + 1].bitcast(I32), min_val=0, max_val=1)
            sp.wait_ge(dn_psum, base + NE)
            with sp.If(full > 0):
                with sp.Fori(1, PASSES) as r:
                    with sp.Fori(0, NE) as e:
                        sp.wait_ge(s["dn"], (r - 1) * NE + e)
                        sp.dma_start(WG[0], t["w_exp_gate"][layer, e].rearrange("(p c) f -> p c f", c=DC)).then_inc(s["w"], 16)
                        sp.dma_start(WU[0], t["w_exp_up"][layer, e].rearrange("(p c) f -> p c f", c=DC)).then_inc(s["w"], 16)
                        sp.dma_start(WD[0], t["w_exp_down"][layer, e].rearrange("(c p) n -> p c n", p=128)).then_inc(s["w"], 16)
                sp.wait_ge(s["dn"], n_more)
                sp.wait_ge(s["st"], 16 * n_more)
            with sp.Else():
                sp.nop()

        sp.wait_ge(op_psum, 3)
        for u in range(3):
            load_expert(0, 0, u)
        experts(0)
        if stage < 8:
            return
        load_expert(1, 0, 0)
        w_cv = t["w_conv_in"][0].rearrange("(c p) n -> p c n", p=128)
        for k in range(6):
            half, part = k // 3, k % 3
            lo = part * D + half * 512
            sp.dma_start(WC[k], w_cv[:, :, lo:lo + 512]).then_inc(ld_wc[half], 16)
        sp.wait_ge(ln_done, 6)
        load_ln(2)
        sp.wait_ge(cv_psum, 12)
        sp.dma_start(WCO, t["w_conv_out"][0].rearrange("(c p) n -> p c n", p=128)).then_inc(ld_wco, 16)
        sp.wait_ge(cv_lsb, 1)
        sp.dma_start(t["new_conv_prompt"].rearrange("l b t d -> (l b t) d"), ULT[0:2, :]).then_inc(st_state, 16)
        sp.dma_start(t["new_conv_sample"].rearrange("l b t d -> (l b t) d"), ULT[2:18, :]).then_inc(st_state, 16)
        sp.wait_ge(st_state, 32)
        sp.wait_ge(op_psum, 6)
        for u in (1, 2):
            load_expert(1, 0, u)
        experts(1)
        sp.wait_ge(ln_done, 12)
        sp.dma_start(t["y_prompt"][0].rearrange("(t p) d -> p t d", p=128), X[:, 0:2, :]).then_inc(st_out, 16)
        sp.dma_start(t["y_sample"].rearrange("b t d -> (b t) d"), X[0:NS, 2, :]).then_inc(st_out, 16)
        sp.wait_ge(st_out, 32)

    @block.gpsimd
    def _(pool):
        link = linker(pool, pool_own)
        nc.gpsimd.memset(ZERO.bitcast(I32), 0).then_inc(zero_set, 1)
        nc.gpsimd.memset(NEGH, -0.5).then_inc(zero_set, 1)
        pool.wait_ge(zero_set, 2)
        for layer in range(DEPTH):
            pool.dma_start(slot_tok_d[layer].rearrange("(p n) o -> p (n o)", p=128), ZERO.bitcast(I32)).then_inc(st_zero, 16)
        pool.wait_ge(proj_evac, len(PROJ))
        for u in range(2 * HB):
            h, qt = HA + u // 2, u % 2
            n = 128 * (qt + 1)
            if u == 0:
                pool.wait_ge(ld_bias, 16 * 10)
                pool.wait_ge(sel_ready, 2)
            wait(pool, att_scored, 2 * HA + u - 1)
            nc.gpsimd.tensor_tensor(COMB[:, u % 2, 0:n], BM[:, h, 256 - n:256] if qt == 0 else BM[:, h, 0:n],
                                    SELM[:, qt, 0:n], ALU.add).then_inc(comb_ready, 1)
        for b in range(DEC_B):
            lo = SEQ + DEC_T * b
            wait(pool, smp_S, b - 1)
            nc.gpsimd.tensor_copy(KTB[b % 2][:, 0:4, PAST:NK_S], QKVT[:, KA:KA + 4, lo:lo + DEC_T])
            nc.gpsimd.tensor_copy(KTB[b % 2][:, 4, PAST:NK_S], QKVT[:, KB, lo:lo + DEC_T])
            nc.gpsimd.tensor_copy(KTB[b % 2][0:64, 5, PAST:NK_S], QKVT[0:64, KI, lo:lo + DEC_T]).then_inc(k_new, 1)
        if stage < 5:
            return

        def rstd(k, tiles=range(3)):
            for i in tiles:
                n = TILES[i][1]
                pool.wait_ge(ln_stat, 3 * k + i + 1)
                nc.gpsimd.tensor_tensor(RSTD[0:n, i:i + 1], VE[0:n, i:i + 1], NEGH[0:n], ALU.pow).then_inc(ln_rstd, 1)

        def experts(layer):
            base = NE * layer
            pool.wait_ge(ro_slot, 2 * layer + 2)
            pool.wait_ge(st_zero, 16 * DEPTH)
            if layer == 0:
                nc.gpsimd.iota(TOKI.bitcast(I32), pattern=[[128, 3]], base=0, channel_multiplier=1).then_inc(zero_set, 1)
                pool.wait_ge(zero_set, 3)
            for i, (_, n) in enumerate(TILES):
                for k in range(2):
                    pool.indirect_dma_start(
                        out=slot_tok_d[layer], out_offset=bass.IndirectOffsetOnAxis(ap=SLOTI[0:n, 2 * i + k:2 * i + k + 1].bitcast(I32), axis=0),
                        in_=TOKI[0:n, i:i + 1].bitcast(I32), in_offset=None).then_inc(scattered, 16)
            pool.wait_ge(scattered, 96 * (layer + 1))
            pool.dma_start(TKI[0:NE, :].bitcast(I32), slot_tok_d[layer][0:NE * CAP].rearrange("(e j) o -> e (j o)", e=NE)).then_inc(ld_tok, 16)
            pool.wait_ge(tok_idx, layer + 1)
            pool.wait_ge(st_x, 32 * (layer + 1))

            def gather(i, u, free):
                e, k = number(i, u), u % 2
                wait(pool, xg_T, free)
                nc.gpsimd.tensor_copy(IDXC[0:CAP, k:k + 1].bitcast(I32), IDXI[0:CAP, bass.ds(e, 1)].bitcast(I32)).then_inc(idx_cur, 1)
                pool.wait_ge(idx_cur, base + e + 1)
                pool.sem_inc(pool_passed, 1)
                pool.indirect_dma_start(
                    out=XG[0:CAP, k, :], out_offset=None, in_=xrows_d[layer],
                    in_offset=bass.IndirectOffsetOnAxis(ap=IDXC[0:CAP, k:k + 1].bitcast(I32), axis=0)).then_inc(gath[k], 16)

            for u in range(6):
                gather(0, u, base + u - 1)
            with pool.Fori(1, NE // 6) as i:
                for u in range(6):
                    gather(i, u, base + number(i, u) - 1)
            for u in range(NE % 6):
                gather(NE // 6, u, base + number(NE // 6, u) - 1)
            s = more[layer]
            full = pool.value_load(FLAG[0:1, layer:layer + 1].bitcast(I32), min_val=0, max_val=1)
            pool.wait_ge(xg_T, base + NE)
            with pool.If(full > 0):
                with pool.Fori(1, PASSES) as r:
                    with pool.Fori(0, NE) as e:
                        n = (r - 1) * NE + e
                        pool.wait_ge(s["T"], n)
                        pool.dma_start(IDXC[0:CAP, 0:1].bitcast(I32), slot_tok_d[layer][bass.ds((r * NE + e) * CAP, CAP)]).then_inc(s["tok"], 16)
                        pool.wait_ge(s["tok"], 16 * (n + 1))
                        pool.sem_inc(pool_passed, 1)
                        pool.indirect_dma_start(
                            out=XG[0:CAP, 0, :], out_offset=None, in_=xrows_d[layer],
                            in_offset=bass.IndirectOffsetOnAxis(ap=IDXC[0:CAP, 0:1].bitcast(I32), axis=0)).then_inc(s["gath"], 16)
                pool.wait_ge(s["st"], 16 * n_more)
            with pool.Else():
                pool.nop()
            for k in range(2):
                pool.wait_ge(st_y[k], 16 * (NE // 2) * (layer + 1))
            for j in range(6):
                n = TILES[j // 2][1]
                wait(pool, y_used, 6 * layer + j - 1)
                with pool.If(full > 0):
                    pool.indirect_dma_start(
                        out=YG[0:n, j % 2, :], out_offset=None, in_=ymore_d[layer],
                        in_offset=bass.IndirectOffsetOnAxis(ap=SLOTM[0:n, j:j + 1].bitcast(I32), axis=0),
                        bounds_check=SLOTS - NE * CAP - 1, oob_is_err=False).then_inc(s["more"], 16)
                    pool.wait_ge(s["more"], 16 * (j + 1))
                with pool.Else():
                    pool.nop()
                pool.indirect_dma_start(
                    out=YG[0:n, j % 2, :], out_offset=None, in_=yslot_d[layer],
                    in_offset=bass.IndirectOffsetOnAxis(ap=SLOTI[0:n, j:j + 1].bitcast(I32), axis=0),
                    bounds_check=NE * CAP - 1, oob_is_err=False).then_inc(ygath[j % 2], 16)
                if j % 2 == 1 and j > 1:
                    rstd(2 * layer + 1, [j // 2 - 1])
            rstd(2 * layer + 1, [2])

        rstd(0)
        if stage < 6:
            return
        experts(0)
        if stage < 8:
            return
        rstd(2)
        experts(1)

    @block.scalar
    def _(act):
        link = linker(act, act_own)

        def copy(out, in_):
            return nc.scalar.copy(out, in_)

        def silu(out, in_):
            return nc.scalar.activation(out, in_, ACT.Silu)

        act.wait_ge(rb_zero, 1)
        act.dma_start(RB[0:32, 0:16], t["rel_bias"]).then_inc(ld_rb, 16)
        act.dma_start(PGT[0:1, :].bitcast(I32), t["page_table"].rearrange("(o b) n -> o (b n)", o=1)).then_inc(ld_pt, 16)
        for i in range(DEPTH):
            act.dma_start(WR[:, i, :, 0:NG], t["w_router_group"][i].rearrange("(c p) n -> p c n", p=128)).then_inc(ld_small, 16)
            act.dma_start(WR[:, i, :, NG:NG + NE], t["w_router_expert"][i].rearrange("(c p) n -> p c n", p=128)).then_inc(ld_small, 16)
            act.dma_start(RBI[:, i, 0:NG], t["b_router_group"][i].partition_broadcast(128)).then_inc(ld_small, 16)
            act.dma_start(RBI[:, i, NG:NG + NE], t["b_router_expert"][i].partition_broadcast(128)).then_inc(ld_small, 16)
        act.wait_ge(tab_psum, 1)
        copy(TAB[0:17, :], bank[7][0:17, 0:TABLE_W]).then_inc(tab_sb, 1)
        act.wait_ge(tab_sb, 1)
        act.dma_start(table_d.rearrange("p h n -> h p n"), TAB[0:17, :].unsqueeze(1).to_broadcast([17, 128, TABLE_W])).then_inc(st_tab, 16)
        act.wait_ge(st_tab, 16)

        def skew(offset, dims):
            return bass.AP(tensor=table_d.tensor, offset=offset, ap=dims)

        pitch = 17 * TABLE_W
        act.dma_start(BM, skew(DIST0 - 128, [[pitch - 1, 128], [TABLE_W, 17], [1, 256]])).then_inc(ld_bias, 16)
        for q in range(4):
            for g in range(2):
                act.dma_start(SBIAS[32 * q:32 * q + 32, g, :],
                              skew(DIST0 - PAST + 8 * g * TABLE_W, [[TABLE_W, 8], [pitch - 1, 4], [1, NK_S]])).then_inc(ld_bias, 16)
        act.dma_start(SMASK[0:NS, :], skew(DIST0 - PAST + 16 * TABLE_W, [[4 * pitch, 8], [pitch - 1, 4], [1, NK_S]])).then_inc(ld_bias, 16)

        def evac_xT(k):
            for c in range(DC):
                act.wait_ge(xT_psum, DC * k + c + 1)
                copy(XT[:, c, :], bank[c % 4][:, 0:NTOK]).then_inc(xT_evac, 1)

        evac_xT(0)
        for g, (_, _, n, chunk, tile, col) in enumerate(PROJ):
            act.wait_ge(proj_psum, g + 1)
            src = bank[4 + g % 4]
            if chunk is None:
                rows = TILES[tile][1]
                copy(V[0:rows, tile, col:col + n], src[0:rows, 0:n]).then_inc(proj_evac, 1)
            elif chunk == KB:
                copy(QKVT[:, KB, :], src[:, 0:NTOK])
                copy(QKVT[0:64, KBS, :], src[64:128, 0:NTOK])
                copy(QKVT[64:128, KBS, :], src[0:64, 0:NTOK]).then_inc(proj_evac, 1)
            elif chunk == KI:
                copy(QKVT[0:64, KI, :], src[0:64, 0:NTOK])
                copy(QKVT[64:128, KI, :], src[0:64, 0:NTOK]).then_inc(proj_evac, 1)
            else:
                copy(QKVT[:, chunk, :], src[:, 0:NTOK]).then_inc(proj_evac, 1)
        for i in range(2 * HI):
            n = 128 * (i // HI + 1)
            act.wait_ge(idx_psum, i + 1)
            wait(act, idx_acc, i - 1)
            nc.scalar.activation(RELU[:, i % 2, 0:n], bank[i % 2][:, 0:n], ACT.Relu).then_inc(idx_relu, 1)

        def exps(u):
            n = 128 * (u % 2 + 1)
            act.wait_ge(att_scored, u + 1)
            nc.scalar.activation(PB[:, u % 3, 0:n], PB[:, u % 3, 0:n], ACT.Exp, bias=MX[:, u:u + 1],
                                 accum_out=SUM[:, u:u + 1]).then_inc(att_exp, 1)

        def evac_T(u):
            act.wait_ge(att_T, u + 1)
            wait(act, att_O, u - 1)
            copy(PTB[:, u % 2, 0:u % 2 + 1, :], bank[2 + u % 2][:, 0:128 * (u % 2 + 1)].rearrange("p (a b) -> p a b", b=128)).then_inc(att_Tevac, 1)

        exps(0)
        for u in range(2 * HEADS):
            if u + 1 < 2 * HEADS:
                exps(u + 1)
            evac_T(u)
            if u % 4 == 3:
                act.wait_ge(att_O, u + 1)
                copy(YT[:, u // 4, 0:SEQ], bank[4 + (u // 4) % 2][:, 0:SEQ]).then_inc(att_Oevac, 1)
        if stage < 4:
            return
        for b in range(DEC_B):
            wait(act, smp_S, b - 1)
            for j in range(3):
                g = 3 * b + j
                act.wait_ge(kt_psum, g + 1)
                src = bank[g % 4][:, :].rearrange("p (a b) -> p a b", b=128)
                if j < 2:
                    copy(KTB[b % 2][:, 0:4, 128 * j:128 * j + 128], src).then_inc(kt_evac, 1)
                else:
                    copy(KTB[b % 2][:, 4, 0:PAST], src[:, 0:2, :])
                    copy(KTB[b % 2][0:64, 5, 0:PAST], src[0:64, 2:4, :]).then_inc(kt_evac, 1)
            if b % 4 == 3:
                act.wait_ge(smp_S, b + 1)
                nc.scalar.activation(RIS[b // 4], bank[6][:, 0:NK_S], ACT.Relu).then_inc(smp_relu, 1)
        for j in range(4):
            act.wait_ge(smp_scored, j + 1)
            nc.scalar.activation(PS4[:, j, :], PS4[:, j, :], ACT.Exp, bias=SMX[:, j:j + 1],
                                 accum_out=SSUM[:, j:j + 1]).then_inc(smp_exp, 1)
        for j in range(4):
            act.wait_ge(smp_T, j + 1)
            copy(PT[:, j, :, :], bank[j % 4][:, 0:384].rearrange("p (a b) -> p a b", b=128)).then_inc(smp_Tevac, 1)
        act.wait_ge(smp_O, DEC_B)
        oa = bank[4][:, 0:256].rearrange("p (b c x) -> p b c x", b=DEC_B, c=4)
        ob = bank[5][:, 0:128].rearrange("p (b k i q) -> p b k i q", b=DEC_B, k=2, i=2)
        for c in range(4):
            dst = YT[:, c, SEQ:NTOK].rearrange("p (b q) -> p b q", b=DEC_B)
            copy(dst[0:64], oa[0:64, :, c, 0:4])
            copy(dst[64:128], oa[64:128, :, c, 4:8])
            last = copy(YT[:, 4 + c, SEQ:NTOK].rearrange("p (b q) -> p b q", b=DEC_B), ob[:, :, c // 2, c % 2, :])
        last.then_inc(smp_y, 1)
        if stage < 6:
            return

        def experts(layer):
            base = NE * layer
            for i in range(3):
                act.wait_ge(ro_top, 2 * (3 * layer + i) + 1)
                nc.scalar.activation(L8[0:TILES[i][1], 0:NG], L8[0:TILES[i][1], 0:NG], ACT.Exp, bias=GT[0:TILES[i][1], 0:1],
                                     accum_out=GSUM[0:TILES[i][1], i:i + 1]).then_inc(ro_exp, 1)
                act.wait_ge(ro_top, 2 * (3 * layer + i) + 2)
                nc.scalar.activation(RR[0:TILES[i][1], i:i + 1], TOP8[0:TILES[i][1], 1:2], ACT.Exp,
                                     bias=GT[0:TILES[i][1], 1:2]).then_inc(ro_exp, 1)

            def gathered(i, u, last=False):
                E, k = base + number(i, u), u % 2
                act.wait_ge(xg_T, E + 1)
                wait(act, gu_psum, E - 1)
                copy(XGT[:, k, :, :], bank[k][:, 0:DC * CAP].rearrange("p (c n) -> p c n", c=DC)).then_inc(xg_evac, 1)

            def rest(i, u, nxt):
                E, k = base + number(i, u), u % 2
                act.wait_ge(gu_psum, E + 1)
                wait(act, h_done, E - 1)
                silu(SG[:, k, :, :], bank[2 + k][:, 0:FC * CAP].rearrange("p (f n) -> p f n", f=FC)).then_inc(silu_done, 1)
                if nxt is not None:
                    gathered(*nxt)
                act.wait_ge(dn_psum, E + 1)
                wait(act, st_y[k], pair_count(layer, i, u) - 16)
                copy(YO[0:CAP, k, 0:512], bank[4 + 2 * k][0:CAP, :])
                copy(YO[0:CAP, k, 512:D], bank[5 + 2 * k][0:CAP, :]).then_inc(y_evac, 1)
                act.wait_ge(y_evac, E + 1)
                act.dma_start(yslot_d[layer][bass.ds(number(i, u) * CAP, CAP)], YO[0:CAP, k, :]).then_inc(st_y[k], 16)

            gathered(0, 0)
            for u in range(6):
                rest(0, u, (0, u + 1) if u < 5 else (1, 0))
            with act.Fori(1, NE // 6) as i:
                for u in range(6):
                    rest(i, u, (i, u + 1) if u < 5 else (i + 1, 0))
            for u in range(NE % 6):
                rest(NE // 6, u, (NE // 6, u + 1) if u + 1 < NE % 6 else None)
            s = more[layer]
            full = act.value_load(FLAG[0:1, layer:layer + 1].bitcast(I32), min_val=0, max_val=1)
            for k in range(2):
                act.wait_ge(st_y[k], 16 * (NE // 2) * (layer + 1))
            with act.If(full > 0):
                with act.Fori(1, PASSES) as r:
                    with act.Fori(0, NE) as e:
                        n = (r - 1) * NE + e
                        act.wait_ge(s["T"], n + 1)
                        copy(XGT[:, 0, :, :], bank[0][:, 0:DC * CAP].rearrange("p (c n) -> p c n", c=DC)).then_inc(s["Tevac"], 1)
                        act.wait_ge(s["gu"], n + 1)
                        silu(SG[:, 0, :, :], bank[2][:, 0:FC * CAP].rearrange("p (f n) -> p f n", f=FC)).then_inc(s["silu"], 1)
                        act.wait_ge(s["dn"], n + 1)
                        act.wait_ge(s["st"], 16 * n)
                        copy(YO[0:CAP, 0, 0:512], bank[4][0:CAP, :])
                        copy(YO[0:CAP, 0, 512:D], bank[5][0:CAP, :]).then_inc(s["y"], 1)
                        act.wait_ge(s["y"], n + 1)
                        act.dma_start(ymore_d[layer][bass.ds(n * CAP, CAP)], YO[0:CAP, 0, :]).then_inc(s["st"], 16)
                act.wait_ge(s["st"], 16 * n_more)
            with act.Else():
                act.nop()

        evac_xT(1)
        experts(0)
        if stage < 8:
            return
        act.dma_start(SCW[0:16, :], t["state_conv"].rearrange("l b w d -> (l b w) d")).then_inc(ld_state, 16)
        act.dma_start(SCW[16:19, :], t["conv_w"][0]).then_inc(ld_state, 16)
        evac_xT(2)
        act.wait_ge(cv_in_T, 1)
        copy(SCT, bank[6][:, 0:DC * 19].rearrange("p (c n) -> p c n", c=DC)).then_inc(cv_in, 1)
        for j in range(DC):
            k = j % 2
            act.wait_ge(cv_psum, 3 * j + 1)
            wait(act, cv_u, j - 1)
            copy(HSB[:, k, :], bank[3 * k][:, 0:NTOK]).then_inc(cv_h, 1)
        act.wait_ge(cv_lT, 1)
        copy(ULT[0:18, 0:512], bank[6][0:18, :])
        copy(ULT[0:18, 512:D], bank[7][0:18, :]).then_inc(cv_lsb, 1)
        evac_xT(3)
        experts(1)

    @block.vector
    def _(dve):
        link = linker(dve, dve_own)
        V_ = nc.vector
        V_.memset(RB[0:33, :], 0.0).then_inc(rb_set, 1)
        dve.wait_ge(rb_set, 1)
        V_.memset(RB[32:33, :], NEG).then_inc(rb_zero, 1)
        for g in range(6):
            dve.wait_ge(ktok_psum, g + 1)
            i, part = g // 2, g % 2
            n = TILES[i][1]
            lo, cols = (0, 512) if part == 0 else (512, 192)
            V_.tensor_copy(KTOK[0:n, i, lo:lo + cols], bank[g % 4][0:n, 0:cols]).then_inc(ktok_evac, 1)
        for i in range(2 * HI):
            qt, h = i // HI, i % HI
            n = 128 * (qt + 1)
            acc, w = ACC[:, qt, 0:n], V[:, qt, 640 + h:641 + h]
            dve.wait_ge(idx_relu, i + 1)
            if h == 0:
                V_.tensor_scalar(acc, RELU[:, i % 2, 0:n], w, None, ALU.mult).then_inc(idx_acc, 1)
            else:
                V_.scalar_tensor_tensor(acc, RELU[:, i % 2, 0:n], w, acc, ALU.mult, ALU.add).then_inc(idx_acc, 1)
            dve.wait_ge(idx_acc, i + 1)
        dve.wait_ge(ld_bias, 16 * 10)

        def select_top(scores, rounds, rows):
            for _ in range(rounds):
                link(V_.max(MX8[0:rows, :], scores))
                link(V_.match_replace(scores, MX8[0:rows, :], scores, TAKEN))

        for qt in range(2):
            n = 128 * (qt + 1)
            acc = ACC[:, qt, 0:n]
            link(V_.scalar_tensor_tensor(acc, acc, IDX_SCALE, BM[:, 16, 128:256] if qt == 0 else BM[:, 16, :], ALU.mult, ALU.add))
            select_top(acc, ROUNDS_P, 128)
            V_.tensor_scalar(SELM[:, qt, 0:n], acc, TAKEN / 2, NEG, ALU.is_ge, ALU.mult).then_inc(sel_ready, 1)

        def score(u):
            h, qt = u // 2, u % 2
            n = 128 * (qt + 1)
            dve.wait_ge(att_S, u + 1)
            wait(dve, att_T, u - 2)
            if h < HA:
                bias = BM[:, h, 128:256] if qt == 0 else BM[:, h, :]
            else:
                dve.wait_ge(comb_ready, u - 2 * HA + 1)
                bias = COMB[:, u % 2, 0:n]
            link(V_.tensor_tensor_reduce(PB[:, u % 3, 0:n], bank[u % 2][:, 0:n], bias, QK_SCALE, -3e38,
                                         ALU.add, ALU.max, MX[:, u:u + 1]))
            V_.tensor_scalar(MX[:, u:u + 1], MX[:, u:u + 1], -1.0, None, ALU.mult).then_inc(att_scored, 1)

        def norm(u):
            n = 128 * (u % 2 + 1)
            dve.wait_ge(att_exp, u + 1)
            link(V_.reciprocal(RIN[:, u:u + 1], SUM[:, u:u + 1]))
            V_.tensor_scalar(PB[:, u % 3, 0:n], PB[:, u % 3, 0:n], RIN[:, u:u + 1], None, ALU.mult).then_inc(att_p, 1)

        score(0)
        for u in range(2 * HEADS):
            if u + 1 < 2 * HEADS:
                score(u + 1)
            norm(u)
        if stage < 4:
            return
        V_.memset(QAS, 0.0)
        V_.memset(QBS, 0.0).then_inc(q_zero, 1)
        dve.wait_ge(q_zero, 1)
        for h in range(HA):
            p, c = 64 * (h % 2), h // 2
            kv = 64 * (h // (HB // KVB))

            def cut(lo, chunk):
                return QKVT[lo:lo + 64, chunk, SEQ:NTOK].rearrange("p (b q) -> p b q", b=DEC_B)
            V_.tensor_copy(QAS[p:p + 64, c, :, 4 * h:4 * h + 4], cut(p, QA + c))
            V_.tensor_copy(QBS[kv:kv + 64, :, 4 * h:4 * h + 4], cut(p, QB + c))
            last = V_.tensor_copy(QIS[0:64, :, 4 * h:4 * h + 4], cut(p, QI + c))
        last.then_inc(q_cut, 1)
        dve.wait_ge(w_psum, 1)
        for g in range(2):
            link(V_.tensor_tensor(WVT, bank[7][:, 8 * g:8 * g + 8], HM, ALU.mult))
            link(V_.tensor_reduce(WV[:, g:g + 1], WVT, AX.X, ALU.add))
            V_.tensor_scalar(WM[:, g, :], PAT[:, 32 * g:32 * g + 32], WV[:, g:g + 1], None, ALU.mult).then_inc(w_mat, 1)
        for g in range(2):
            dve.wait_ge(smp_S, 4 * g + 4)
            link(V_.tensor_tensor_reduce(PS4[:, g, :], bank[4][:, 0:NK_S], SBIAS[:, 0, :], QK_SCALE, -3e38,
                                         ALU.add, ALU.max, SMX[:, g:g + 1]))
            V_.tensor_scalar(SMX[:, g:g + 1], SMX[:, g:g + 1], -1.0, None, ALU.mult).then_inc(smp_scored, 1)
            V_.tensor_tensor(PS4[:, 2 + g, :], bank[5][:, 0:NK_S], SBIAS[:, 1, :], ALU.add).then_inc(smp_Sevac, 1)
        dve.wait_ge(sc_psum, 1)
        V_.memset(SCS[0:NS, NK_S:NK_S + PADS_S], -TAKEN)
        link(V_.scalar_tensor_tensor(SCS[0:NS, 0:NK_S], bank[7][0:NS, 0:NK_S], IDX_SCALE, SMASK[0:NS, :], ALU.mult, ALU.add))
        select_top(SCS[0:NS, :], ROUNDS_S, NS)
        V_.tensor_scalar(SMASK[0:NS, :], SCS[0:NS, 0:NK_S], TAKEN / 2, NEG, ALU.is_ge, ALU.mult).then_inc(sc_mask, 1)
        dve.wait_ge(smp_Sevac, 2)
        for g in range(2):
            dve.wait_ge(rep_psum, g + 1)
            link(V_.tensor_tensor_reduce(PS4[:, 2 + g, :], bank[g][:, 0:NK_S], PS4[:, 2 + g, :], QK_SCALE, -3e38,
                                         ALU.add, ALU.max, SMX[:, 2 + g:3 + g]))
            V_.tensor_scalar(SMX[:, 2 + g:3 + g], SMX[:, 2 + g:3 + g], -1.0, None, ALU.mult).then_inc(smp_scored, 1)
        for j in range(4):
            g = j % 2
            dve.wait_ge(smp_exp, j + 1)
            link(V_.reciprocal(SRIN[:, j:j + 1], SSUM[:, j:j + 1]))
            link(V_.tensor_scalar(PS4[:, j, :], PS4[:, j, :], SRIN[:, j:j + 1], None, ALU.mult))
            V_.tensor_tensor(PN[:, j, :].rearrange("p (b q) -> p b q", b=DEC_B),
                             PS4[:, j, PAST:NK_S].unsqueeze(1).to_broadcast([128, DEC_B, DEC_T]),
                             NEW[:, 32 * g:32 * g + 32].rearrange("p (b q) -> p b q", b=DEC_B), ALU.mult).then_inc(smp_p, 1)
        if stage < 5:
            return

        def norm_rows(k, i):
            n = TILES[i][1]
            x = X[0:n, i, :]
            V_.bn_stats(STATS[0:n, 0:6], X[0:n, i, 0:512])
            link(V_.bn_stats(STATS[0:n, 6:12], X[0:n, i, 512:D]))
            link(V_.bn_aggr(MV[0:n, i, :], STATS[0:n, :]))
            V_.tensor_scalar(VE[0:n, i:i + 1], MV[0:n, i, 1:2], EPS, None, ALU.add).then_inc(ln_stat, 1)
            dve.wait_ge(ln_rstd, 3 * k + i + 1)
            link(V_.tensor_scalar(x, x, MV[0:n, i, 0:1], RSTD[0:n, i:i + 1], ALU.subtract, ALU.mult))
            dve.wait_ge(ld_ln, 32 * (k + 1))
            link(V_.tensor_tensor(x, x, LNP[0:n, 0, :], ALU.mult))
            V_.tensor_tensor(x, x, LNP[0:n, 1, :], ALU.add).then_inc(ln_done, 1)

        def mixed(k, first):
            for i, (_, n) in enumerate(TILES):
                dve.wait_ge(op_psum, first + i + 1)
                for half in range(2):
                    x = X[0:n, i, 512 * half:512 * half + 512]
                    link(V_.scalar_tensor_tensor(x, x, ALPHA, bank[2 * i + half][0:n, :], ALU.mult, ALU.add))
                norm_rows(k, i)

        def route(layer):
            link(V_.memset(L8, NEG))
            link(V_.memset(RK, 0.0))
            link(V_.memset(EF, 0.0))
            dve.wait_ge(ld_small, 8 * 16)
            for i, (_, n) in enumerate(TILES):
                m = 3 * layer + i
                dve.wait_ge(ro_psum, m + 1)
                link(V_.tensor_tensor(LG[0:n, :], bank[4 + i][0:n, 0:NG + NE], RBI[0:n, layer, :], ALU.add))
                link(V_.tensor_copy(L8[0:n, 0:NG], LG[0:n, 0:NG]))
                link(V_.max(TOP8[0:n, :], L8[0:n, :]))
                link(V_.max_index(GIX[0:n, :].bitcast(U32), TOP8[0:n, :], L8[0:n, :]))
                V_.tensor_scalar(GT[0:n, 0:1], TOP8[0:n, 0:1], -1.0, None, ALU.mult).then_inc(ro_top, 1)
                link(V_.tensor_copy(GT[0:n, 2:3], GIX[0:n, 0:1].bitcast(U32)))
                link(V_.tensor_scalar(PEN[0:n, :], IOTA[0:n, 0:NG], GT[0:n, 2:3], None, ALU.is_equal))
                link(V_.tensor_scalar(PEN[0:n, :], PEN[0:n, :], -1.0, -NEG, ALU.add, ALU.mult))
                le = LG[0:n, NG:NG + NE]
                link(V_.tensor_tensor(le.rearrange("p (g e) -> p g e", g=NG), le.rearrange("p (g e) -> p g e", g=NG),
                                      PEN[0:n, :].unsqueeze(2).to_broadcast([n, NG, EPG]), ALU.add))
                link(V_.max(TOP8[0:n, :], le))
                link(V_.max_index(EIX[0:n, :].bitcast(U32), TOP8[0:n, :], le))
                V_.tensor_scalar(GT[0:n, 1:2], TOP8[0:n, 0:1], -1.0, None, ALU.mult).then_inc(ro_top, 1)
                link(V_.tensor_copy(EF[0:n, 2 * i:2 * i + 2], EIX[0:n, 0:2].bitcast(U32)))
                for k in range(2):
                    link(V_.tensor_scalar(HOTK[0:n, 2 * i + k, :], IOTA[0:n, :], EF[0:n, 2 * i + k:2 * i + k + 1], None, ALU.is_equal))
                V_.tensor_tensor(HOT[0:n, i, :], HOTK[0:n, 2 * i, :], HOTK[0:n, 2 * i + 1, :], ALU.add).then_inc(ro_hot, 1)
                dve.wait_ge(ro_exp, 2 * m + 2)
                link(V_.tensor_scalar(DEN[0:n, i:i + 1], RR[0:n, i:i + 1], 1.0, GSUM[0:n, i:i + 1], ALU.add, ALU.mult))
                link(V_.reciprocal(GATE[0:n, 2 * i:2 * i + 1], DEN[0:n, i:i + 1]))
                link(V_.tensor_tensor(GATE[0:n, 2 * i + 1:2 * i + 2], GATE[0:n, 2 * i:2 * i + 1], RR[0:n, i:i + 1], ALU.mult))
            dve.wait_ge(ro_rank, 4 * layer + 4)
            for i, (_, n) in enumerate(TILES):
                for k in range(2):
                    link(V_.tensor_tensor(RANKT[0:n, :], bank[7][0:n, 32 * i:32 * i + 32], HOTK[0:n, 2 * i + k, :], ALU.mult))
                    link(V_.tensor_reduce(RK[0:n, 2 * i + k:2 * i + k + 1], RANKT[0:n, :], AX.X, ALU.add))
            link(V_.scalar_tensor_tensor(SLOTF, EF, float(CAP), RK, ALU.mult, ALU.add))
            for r in range(1, PASSES):
                link(V_.tensor_scalar(QQ, RK, float(r * CAP), float(NE * CAP - CAP), ALU.is_ge, ALU.mult))
                link(V_.tensor_tensor(SLOTF, SLOTF, QQ, ALU.add))
            link(V_.tensor_copy(SLOTI.bitcast(I32), SLOTF))
            link(V_.tensor_scalar(QQ, RK, float(CAP), -float(SLOTS + NE * CAP), ALU.is_lt, ALU.mult))
            link(V_.tensor_scalar(QQ, QQ, -1.0, -float(NE * CAP), ALU.mult, ALU.add))
            link(V_.tensor_tensor(SLOTF, SLOTF, QQ, ALU.add))
            V_.tensor_copy(SLOTM.bitcast(I32), SLOTF).then_inc(ro_slot, 1)
            link(V_.tensor_reduce(GT[0:1, 3:4], bank[7][0:1, 96:128], AX.X, ALU.max))
            link(V_.tensor_scalar(GT[0:1, 4:5], GT[0:1, 3:4], float(CAP), None, ALU.is_gt))
            V_.tensor_copy(FLAG[0:1, layer:layer + 1].bitcast(I32), GT[0:1, 4:5]).then_inc(ro_slot, 1)
            dve.wait_ge(ld_tok, 16 * (layer + 1))
            V_.tensor_copy(TKF[0:NE, :], TKI[0:NE, :].bitcast(I32)).then_inc(tok_f, 1)
            dve.wait_ge(tok_T, layer + 1)
            V_.tensor_copy(IDXI[0:CAP, :].bitcast(I32), bank[6][0:CAP, 0:NE]).then_inc(tok_idx, 1)

        def experts(layer):
            base = NE * layer

            def hidden(i, u):
                E, k = base + number(i, u), u % 2
                dve.wait_ge(silu_done, E + 1)
                wait(dve, dn_psum, E - 1)
                V_.tensor_tensor(HT[:, k, :, :], SG[:, k, :, :],
                                 bank[2 + k][:, FC * CAP:2 * FC * CAP].rearrange("p (f n) -> p f n", f=FC), ALU.mult).then_inc(h_done, 1)

            for u in range(6):
                hidden(0, u)
            with dve.Fori(1, NE // 6) as i:
                for u in range(6):
                    hidden(i, u)
            for u in range(NE % 6):
                hidden(NE // 6, u)
            s = more[layer]
            full = dve.value_load(FLAG[0:1, layer:layer + 1].bitcast(I32), min_val=0, max_val=1)
            with dve.If(full > 0):
                with dve.Fori(1, PASSES) as r:
                    with dve.Fori(0, NE) as e:
                        n = (r - 1) * NE + e
                        dve.wait_ge(s["silu"], n + 1)
                        V_.tensor_tensor(HT[:, 0, :, :], SG[:, 0, :, :],
                                         bank[2][:, FC * CAP:2 * FC * CAP].rearrange("p (f n) -> p f n", f=FC), ALU.mult).then_inc(s["h"], 1)
                dve.wait_ge(s["st"], 16 * n_more)
            with dve.Else():
                dve.nop()
            for i, (_, n) in enumerate(TILES):
                x, y0, y1 = X[0:n, i, :], YG[0:n, 0, :], YG[0:n, 1, :]
                done = 6 * layer + 2 * i
                dve.wait_ge(ygath[0], 16 * (3 * layer + i + 1))
                link(V_.tensor_scalar(y0, y0, GATE[0:n, 2 * i:2 * i + 1], None, ALU.mult))
                dve.wait_ge(ygath[1], 16 * (3 * layer + i + 1))
                V_.scalar_tensor_tensor(y1, y1, GATE[0:n, 2 * i + 1:2 * i + 2], y0, ALU.mult, ALU.add).then_inc(y_used, 1)
                dve.wait_ge(y_used, done + 1)
                V_.scalar_tensor_tensor(x, x, ALPHA, y1, ALU.mult, ALU.add).then_inc(y_used, 1)
                dve.wait_ge(y_used, done + 2)
                norm_rows(2 * layer + 1, i)

        mixed(0, 0)
        if stage < 6:
            return
        route(0)
        experts(0)
        if stage < 8:
            return
        for k in range(2):
            link(V_.memset(UB[:, k, 0:2], 0.0))
        dve.wait_ge(cv_in, 1)
        for j in range(DC):
            k = j % 2
            up, us = UB[:, k, 0:SEQ + 2], UB[:, k, SEQ + 2:].rearrange("p (b w) -> p b w", b=DEC_B)
            cp, cs = CB[:, k, 0:SEQ], CB[:, k, SEQ:NTOK].rearrange("p (b q) -> p b q", b=DEC_B)
            gate_c = bank[3 * k + 2]
            V_.tensor_copy(us[:, :, 0:2], SCT[:, j, 0:16].rearrange("p (b w) -> p b w", b=DEC_B))
            dve.wait_ge(cv_h, j + 1)
            dve.wait_ge(cv_psum, 3 * j + 3)
            V_.tensor_tensor(up[:, 2:], HSB[:, k, 0:SEQ], gate_c[:, 0:SEQ], ALU.mult)
            V_.tensor_tensor(us[:, :, 2:6], HSB[:, k, SEQ:NTOK].rearrange("p (b q) -> p b q", b=DEC_B),
                             gate_c[:, SEQ:NTOK].rearrange("p (b q) -> p b q", b=DEC_B), ALU.mult).then_inc(cv_u, 1)
            dve.wait_ge(cv_u, j + 1)
            w = [SCT[:, j, 16 + i:17 + i] for i in range(3)]
            V_.tensor_copy(UL[:, j, 0:2], up[:, SEQ:SEQ + 2])
            V_.tensor_copy(UL[:, j, 2:18].rearrange("p (b w) -> p b w", b=DEC_B), us[:, :, 4:6])
            link(V_.tensor_scalar(cp, up[:, 0:SEQ], w[0], None, ALU.mult))
            link(V_.tensor_scalar(cs, us[:, :, 0:4], w[0], None, ALU.mult))
            for i in (1, 2):
                link(V_.scalar_tensor_tensor(cp, up[:, i:i + SEQ], w[i], cp, ALU.mult, ALU.add))
                link(V_.scalar_tensor_tensor(cs, us[:, :, i:i + 4], w[i], cs, ALU.mult, ALU.add))
            V_.tensor_tensor(ZT[:, j, :], CB[:, k, :], bank[3 * k + 1][:, 0:NTOK], ALU.mult).then_inc(cv_z, 1)
        mixed(2, 3)
        route(1)
        experts(1)

    @block.tensor
    def _(pe):
        mm = nc.tensor.matmul

        def tr(out, in_, n):
            return nc.tensor.transpose(out, in_, ID[0:n, 0:n])

        pe.wait_ge(ld_const, 32)
        pe.wait_ge(ld_rb, 16)
        mm(bank[7][0:17, 0:TABLE_W], RB[0:33, :], OH[0:33, :], start=True, stop=True).then_inc(tab_psum, 1)

        def transpose_x(k):
            for c in range(DC):
                wait(pe, xT_evac, DC * k + c - 3)
                for lo, n in TILES:
                    last = tr(bank[c % 4][:, lo:lo + n], X[0:n, lo // 128, 128 * c:128 * c + 128], n)
                last.then_inc(xT_psum, 1)

        pe.wait_ge(ld_x, 32)
        transpose_x(0)
        pe.wait_ge(xT_evac, DC)
        pe.wait_ge(tab_sb, 1)
        for g, (load, lo, n, chunk, tile, _) in enumerate(PROJ):
            if g == 0 or PROJ[g - 1][0] != load:
                pe.wait_ge(ld_win[load % 3], 16 * (load // 3 + 1))
            wait(pe, proj_evac, g - 3)
            w = WIN[load % 3][:, :, lo:lo + n]
            out = bank[4 + g % 4]
            for c in range(DC):
                if chunk is None:
                    tok, rows = TILES[tile]
                    last = mm(out[0:rows, 0:n], XT[:, c, tok:tok + rows], w[:, c, :], start=c == 0, stop=c == DC - 1)
                else:
                    last = mm(out[0:n, 0:NTOK], w[:, c, :], XT[:, c, :], start=c == 0, stop=c == DC - 1)
            last.then_inc(proj_psum, 1)
        pe.wait_ge(proj_evac, len(PROJ))
        for g in range(6):
            (lo, n), part = TILES[g // 2], g % 2
            wait(pe, ktok_evac, g - 3)
            out = bank[g % 4]
            if part == 0:
                for c in range(4):
                    last = tr(out[0:n, 128 * c:128 * c + 128], QKVT[:, KA + c, lo:lo + n], 128)
            else:
                tr(out[0:n, 0:128], QKVT[:, KB, lo:lo + n], 128)
                last = tr(out[0:n, 128:192], QKVT[0:64, KI, lo:lo + n], 64)
            last.then_inc(ktok_psum, 1)
        pe.wait_ge(ktok_evac, 6)
        for i in range(2 * HI):
            qt, h = i // HI, i % HI
            p, n = 64 * (h % 2), 128 * (qt + 1)
            wait(pe, idx_relu, i - 1)
            mm(bank[i % 2][:, 0:n], QKVT[p:p + 64, QI + h // 2, 128 * qt:128 * qt + 128], QKVT[p:p + 64, KI, 0:n],
               start=True, stop=True).then_inc(idx_psum, 1)
        pe.wait_ge(idx_relu, 2 * HI)

        def scores(u):
            h, qt = u // 2, u % 2
            n, p = 128 * (qt + 1), 64 * (h % 2)
            if h < HA:
                q, k = QA + h // 2, KA + h // 2
            else:
                b = h - HA
                q, k = QB + b // 2, KB if b % 2 == b // (HB // KVB) else KBS
            wait(pe, att_scored, u - 1)
            mm(bank[u % 2][:, 0:n], QKVT[p:p + 64, q, 128 * qt:128 * qt + 128], QKVT[p:p + 64, k, 0:n],
               start=True, stop=True).then_inc(att_S, 1)

        def transpose_p(u):
            pe.wait_ge(att_p, u + 1)
            wait(pe, att_Tevac, u - 1)
            for kt in range(u % 2 + 1):
                last = tr(bank[2 + u % 2][:, 128 * kt:128 * kt + 128], PB[:, u % 3, 128 * kt:128 * kt + 128], 128)
            last.then_inc(att_T, 1)

        def values(u):
            h, qt = u // 2, u % 2
            pe.wait_ge(att_Tevac, u + 1)
            if u % 4 == 0:
                wait(pe, att_Oevac, u // 4 - 1)
            col = 64 * h if h < HA else 512 + 64 * ((h - HA) // (HB // KVB))
            out = bank[4 + (h // 2) % 2][64 * (h % 2):64 * (h % 2) + 64, 128 * qt:128 * qt + 128]
            for kt in range(qt + 1):
                last = mm(out, V[:, kt, col:col + 64], PTB[:, u % 2, kt, :], start=kt == 0, stop=kt == qt)
            last.then_inc(att_O, 1)

        scores(0)
        for u in range(2 * HEADS):
            if u + 1 < 2 * HEADS:
                scores(u + 1)
            transpose_p(u)
            if u >= 1:
                values(u - 1)
        values(2 * HEADS - 1)
        if stage < 4:
            return
        pe.wait_ge(att_Oevac, HEADS // 2)
        for g in range(2):
            last = mm(bank[7][:, 8 * g:8 * g + 8], REP[0:NS, 128 * g:128 * g + 128], V[0:NS, 2, 640:648], start=True, stop=True)
        last.then_inc(w_psum, 1)
        pe.wait_ge(q_cut, 1)
        for b in range(DEC_B):
            pe.wait_ge(ld_k[b % 2], 16 * 6 * (b // 2 + 1))
            for j in range(3):
                g = 3 * b + j
                wait(pe, kt_evac, g - 3)
                if j < 2:
                    for c in range(4):
                        last = tr(bank[g % 4][:, 128 * c:128 * c + 128], KRAW[b % 2][:, j, 128 * c:128 * c + 128], 128)
                else:
                    for pg in range(N_PAGES):
                        tr(bank[g % 4][:, 128 * pg:128 * pg + 128], KRAW[b % 2][:, pg, 512:640], 128)
                        last = tr(bank[g % 4][0:64, 256 + 128 * pg:384 + 128 * pg], KRAW[b % 2][:, pg, 640:704], 128)
                last.then_inc(kt_psum, 1)
            pe.wait_ge(kt_evac, 3 * b + 3)
            pe.wait_ge(k_new, b + 1)
            if b == 4:
                pe.wait_ge(smp_Sevac, 1)
                pe.wait_ge(smp_relu, 1)
            rows = slice(32 * (b % 4), 32 * (b % 4) + 32)
            for c in range(4):
                mm(bank[4][rows, 0:NK_S], QAS[:, c, b, :], KTB[b % 2][:, c, :], start=c == 0, stop=c == 3)
            mm(bank[5][rows, 0:NK_S], QBS[:, b, :], KTB[b % 2][:, 4, :], start=True, stop=True)
            mm(bank[6][rows, 0:NK_S], QIS[0:64, b, :], KTB[b % 2][0:64, 5, :], start=True, stop=True).then_inc(smp_S, 1)
        pe.wait_ge(smp_relu, 2)
        pe.wait_ge(w_mat, 2)
        for g in range(2):
            last = mm(bank[7][0:NS, 0:NK_S], WM[:, g, :], RIS[g], start=g == 0, stop=g == 1)
        last.then_inc(sc_psum, 1)
        pe.wait_ge(sc_mask, 1)
        for g in range(2):
            mm(bank[g][:, 0:NK_S], REP[0:NS, 128 * g:128 * g + 128], SMASK[0:NS, :], start=True, stop=True).then_inc(rep_psum, 1)
        pe.wait_ge(smp_scored, 4)
        for j in range(4):
            pe.wait_ge(smp_p, j + 1)
            for kt in range(2):
                tr(bank[j][:, 128 * kt:128 * kt + 128], PS4[:, j, 128 * kt:128 * kt + 128], 128)
            tr(bank[j][0:NS, 256:384], PN[:, j, :], 128).then_inc(smp_T, 1)
        pe.wait_ge(smp_Tevac, 4)
        for b in range(DEC_B):
            g, r0 = b // 4, 32 * (b % 4)
            pe.wait_ge(ld_v[b % 2], 16 * 4 * (b // 2 + 1))
            for c in range(4):
                out = bank[4][:, 32 * b + 8 * c:32 * b + 8 * c + 8]
                for kt in range(3):
                    v = VRAW[b % 2][:, kt, 128 * c:128 * c + 128] if kt < 2 else V[0:NS, 2, 128 * c:128 * c + 128]
                    p = PT[:, g, kt, r0 + 8 * c:r0 + 8 * c + 8] if kt < 2 else PT[0:NS, g, 2, r0 + 8 * c:r0 + 8 * c + 8]
                    mm(out, v, p, start=kt == 0, stop=kt == 2)
            for kv in range(2):
                for odd in range(2):
                    out = bank[5][64 * odd:64 * odd + 64, 16 * b + 8 * kv:16 * b + 8 * kv + 8].rearrange("p (i q) -> p i q", i=2)
                    for kt in range(3):
                        k_rows = 128 if kt < 2 else NS
                        v = (VRAW[b % 2][:, kt, 512 + 64 * kv:576 + 64 * kv] if kt < 2
                             else V[0:NS, 2, 512 + 64 * kv:576 + 64 * kv])
                        p = PT[0:k_rows, 2 + g, kt, r0 + 16 * kv:r0 + 16 * kv + 16].rearrange("p (i o q) -> p i o q", i=2, o=2)[:, :, odd, :]
                        last = mm(out, v, p, start=kt == 0, stop=kt == 2)
            last.then_inc(smp_O, 1)
        if stage < 5:
            return

        def project(feat, w):
            for i, (lo, n) in enumerate(TILES):
                for half in range(2):
                    for c in range(DC):
                        last = mm(bank[2 * i + half][0:n, :], feat[:, c, lo:lo + n], w[:, c, 512 * half:512 * half + 512],
                                  start=c == 0, stop=c == DC - 1)
                last.then_inc(op_psum, 1)

        def route(layer):
            k = 2 * layer + 1
            pe.wait_ge(ln_done, 6 * layer + 3)
            transpose_x(k)
            pe.wait_ge(xT_evac, DC * (k + 1))
            pe.wait_ge(ld_small, 8 * 16)
            for i, (lo, n) in enumerate(TILES):
                for c in range(DC):
                    last = mm(bank[4 + i][0:n, 0:NG + NE], XT[:, c, lo:lo + n], WR[:, layer, c, :], start=c == 0, stop=c == DC - 1)
                last.then_inc(ro_psum, 1)
            for i, (_, n) in enumerate(TILES):
                pe.wait_ge(ro_hot, 3 * layer + i + 1)
                for j in range(i):
                    mm(bank[7][0:n, 32 * i:32 * i + 32], ONE[:, 0:n], HOT[:, j, :], start=j == 0, stop=False)
                mm(bank[7][0:n, 32 * i:32 * i + 32], TRI[0:n, 0:n], HOT[0:n, i, :], start=i == 0, stop=True).then_inc(ro_rank, 1)
            for i, (_, n) in enumerate(TILES):
                last = mm(bank[7][0:1, 96:128], ONE[0:n, 0:1], HOT[0:n, i, :], start=i == 0, stop=i == 2)
            last.then_inc(ro_rank, 1)
            pe.wait_ge(tok_f, layer + 1)
            tr(bank[6][0:CAP, 0:NE], TKF[0:NE, :], NE).then_inc(tok_T, 1)
            pe.wait_ge(tok_idx, layer + 1)

        def experts(layer):
            base = NE * layer

            def transpose_rows(x, out):
                for c in range(DC):
                    last = tr(out[:, CAP * c:CAP * c + CAP], x.rearrange("n (p c) -> n p c", c=DC)[:, :, c], CAP)
                return last

            def gate_up(x, wg, wu, out, up_ready=None):
                for part, w in ((0, wg), (1, wu)):
                    if part == 1 and up_ready is not None:
                        pe.wait_ge(*up_ready)
                    for f in range(FC):
                        for c in range(DC):
                            lo = CAP * (FC * part + f)
                            last = mm(out[:, lo:lo + CAP], w[:, c, 128 * f:128 * f + 128], x[:, c, :], start=c == 0, stop=c == DC - 1)
                return last

            def down(h, wd, outs):
                for half in range(2):
                    for f in range(FC):
                        last = mm(outs[half][0:CAP, :], h[:, f, :], wd[:, f, 512 * half:512 * half + 512], start=f == 0, stop=f == FC - 1)
                return last

            def gathered(i, u):
                E, k = base + number(i, u), u % 2
                pe.wait_ge(gath[k], pair_count(layer, i, u))
                wait(pe, xg_evac, E - 1)
                pe.sem_inc(pe_passed, 1)
                transpose_rows(XG[0:CAP, k, :], bank[k]).then_inc(xg_T, 1)

            def rest(i, u, nxt):
                E, k, s = base + number(i, u), u % 2, u % 3
                pe.wait_ge(xg_evac, E + 1)
                wait(pe, h_done, E - 1)
                pe.wait_ge(ld_wg[s], slot_loads(layer, i, u))
                gate_up(XGT[:, k, :, :], WG[s], WU[s], bank[2 + k], (ld_wu[s], slot_loads(layer, i, u))).then_inc(gu_psum, 1)
                if nxt is not None:
                    gathered(*nxt)
                pe.wait_ge(h_done, E + 1)
                wait(pe, y_evac, E - 1)
                pe.wait_ge(ld_wd[s], slot_loads(layer, i, u))
                down(HT[:, k, :, :], WD[s], (bank[4 + 2 * k], bank[5 + 2 * k])).then_inc(dn_psum, 1)

            gathered(0, 0)
            for u in range(6):
                rest(0, u, (0, u + 1) if u < 5 else (1, 0))
            with pe.Fori(1, NE // 6) as i:
                for u in range(6):
                    rest(i, u, (i, u + 1) if u < 5 else (i + 1, 0))
            for u in range(NE % 6):
                rest(NE // 6, u, (NE // 6, u + 1) if u + 1 < NE % 6 else None)
            s = more[layer]
            full = pe.value_load(FLAG[0:1, layer:layer + 1].bitcast(I32), min_val=0, max_val=1)
            pe.wait_ge(y_evac, base + NE)
            with pe.If(full > 0):
                with pe.Fori(1, PASSES) as r:
                    with pe.Fori(0, NE) as e:
                        n = (r - 1) * NE + e
                        pe.wait_ge(s["gath"], 16 * (n + 1))
                        pe.sem_inc(pe_passed, 1)
                        transpose_rows(XG[0:CAP, 0, :], bank[0]).then_inc(s["T"], 1)
                        pe.wait_ge(s["Tevac"], n + 1)
                        pe.wait_ge(s["w"], 48 * (n + 1))
                        gate_up(XGT[:, 0, :, :], WG[0], WU[0], bank[2]).then_inc(s["gu"], 1)
                        pe.wait_ge(s["h"], n + 1)
                        pe.wait_ge(s["y"], n)
                        down(HT[:, 0, :, :], WD[0], (bank[4], bank[5])).then_inc(s["dn"], 1)
                pe.wait_ge(s["st"], 16 * n_more)
            with pe.Else():
                pe.nop()

        pe.wait_ge(smp_y, 1)
        pe.wait_ge(ld_wout, 16)
        project(YT, WOUT)
        if stage < 6:
            return
        route(0)
        experts(0)
        if stage < 8:
            return
        pe.wait_ge(ln_done, 6)
        transpose_x(2)
        pe.wait_ge(ld_state, 32)
        for c in range(DC):
            last = tr(bank[6][:, 19 * c:19 * c + 19], SCW[0:19, 128 * c:128 * c + 128], 19)
        last.then_inc(cv_in_T, 1)
        pe.wait_ge(xT_evac, 3 * DC)
        for j in range(DC):
            half = j // 4
            if j % 4 == 0:
                pe.wait_ge(ld_wc[half], 48)
            wait(pe, cv_z, j - 1)
            for part in range(3):
                w = WC[3 * half + part]
                for c in range(DC):
                    last = mm(bank[3 * (j % 2) + part][:, 0:NTOK], w[:, c, 128 * (j % 4):128 * (j % 4) + 128], XT[:, c, :],
                              start=c == 0, stop=c == DC - 1)
                last.then_inc(cv_psum, 1)
        pe.wait_ge(cv_z, DC)
        pe.wait_ge(cv_in, 1)
        for c in range(DC):
            last = tr(bank[6 + c // 4][0:18, 128 * (c % 4):128 * (c % 4) + 128], UL[:, c, :], 128)
        last.then_inc(cv_lT, 1)
        pe.wait_ge(ld_wco, 16)
        project(ZT, WCO)
        route(1)
        experts(1)


_INS = ["x_prompt", "x_sample", "cache_k_a", "cache_v_a", "cache_k_b", "cache_v_b", "cache_k_idx", "state_conv", "page_table",
        "rel_bias", "w_attn_in", "w_attn_out", "w_conv_in", "conv_w", "w_conv_out", "w_router_group", "b_router_group",
        "w_router_expert", "b_router_expert", "w_exp_gate", "w_exp_up", "w_exp_down", "ln_g", "ln_b"]
_OUTS = [("y_prompt", (1, SEQ, D)), ("y_sample", (DEC_B, DEC_T, D)),
         ("new_k_a_prompt", (1, 1, SEQ, HA, HD)), ("new_v_a_prompt", (1, 1, SEQ, HA, HD)),
         ("new_k_b_prompt", (1, 1, SEQ, KVB, HD)), ("new_v_b_prompt", (1, 1, SEQ, KVB, HD)),
         ("new_k_idx_prompt", (1, 1, SEQ, HD)), ("new_conv_prompt", (1, 1, 2, D)),
         ("new_k_a_sample", (1, DEC_B, DEC_T, HA, HD)), ("new_v_a_sample", (1, DEC_B, DEC_T, HA, HD)),
         ("new_k_b_sample", (1, DEC_B, DEC_T, KVB, HD)), ("new_v_b_sample", (1, DEC_B, DEC_T, KVB, HD)),
         ("new_k_idx_sample", (1, DEC_B, DEC_T, HD)), ("new_conv_sample", (1, DEC_B, 2, D))]


def kernel(**inputs):
    import concourse.bacc as bacc
    from concourse.bass_utils import run_bass_kernel_spmd as run

    nc = bacc.Bacc("TRN2", target_bir_lowering=False, num_devices=1)
    arrays, t = {}, {}
    arrays["consts"] = constants()
    for name in _INS:
        arrays[name] = np.ascontiguousarray(inputs[name])
    for name, a in arrays.items():
        t[name] = nc.dram_tensor(name, a.shape, mybir.dt.from_np(a.dtype), kind="ExternalInput").ap()
    for name, shape in _OUTS:
        t[name] = nc.dram_tensor(name, shape, F32, kind="ExternalOutput").ap()
    build(nc, t)
    r = run(nc, [arrays], core_ids=[0])
    return tuple(r.results[0][name] for name, _ in _OUTS)
```

```python
import math
from contextlib import ExitStack

import numpy as np
import concourse.bass as bass
from concourse import mybir

F32 = mybir.dt.float32
I32 = mybir.dt.int32
U32 = mybir.dt.uint32
ALU = mybir.AluOpType
ACT = mybir.ActivationFunctionType
AX = mybir.AxisListType

D = 1024
DC = D // 128
SEQ = 256
DEC_B, DEC_T = 8, 4
NS = DEC_B * DEC_T
NTOK = SEQ + NS
TILES = [(0, 128), (128, 128), (256, NS)]
DEPTH = 2
ALPHA = (2 * DEPTH) ** 0.25
EPS = 1e-5
PAST, PAGE = 256, 128
N_PAGES = PAST // PAGE
NK_S = PAST + DEC_T
HD, HA, HB, KVB, HI = 64, 8, 8, 2, 8
HEADS = HA + HB
TOPK_P = 64
TOPK_S = 65
ROUNDS_P = TOPK_P // 8
ROUNDS_S = -(-TOPK_S // 8)
PADS_S = ROUNDS_S * 8 - TOPK_S
IDX_SCALE = 1.0 / math.sqrt(64 * HI)
QK_SCALE = 1.0 / math.sqrt(HD)
NEG, TAKEN = -1e30, -3e38
ATTN_IN = 2888
NE, NG, EPG, FE = 32, 4, 8, 512
FC = FE // 128
CAP = 64
PASSES = -(-NTOK // CAP)
SLOTS = PASSES * NE * CAP
DIST0 = PAST + DEC_T - 1
TABLE_W = 388
W_BLOCKS = [(0, 512), (512, 512), (1024, 512), (1536, 512), (2048, 256), (2304, 512), (2816, 72)]
QA, KA, QB, KB, QI, KI, KBS = 0, 4, 8, 12, 13, 17, 18
PROJ = ([(0, 128 * c, 128, QA + c, None, None) for c in range(4)]
        + [(1, 128 * c, 128, KA + c, None, None) for c in range(4)]
        + [(2, 0, 512, None, t, 0) for t in range(3)]
        + [(3, 128 * c, 128, QB + c, None, None) for c in range(4)]
        + [(4, 0, 128, KB, None, None)] + [(4, 128, 128, None, t, 512) for t in range(3)]
        + [(5, 128 * c, 128, QI + c, None, None) for c in range(4)]
        + [(6, 0, 64, KI, None, None)] + [(6, 64, 8, None, t, 640) for t in range(3)])
PROJ_END = [sum(1 for p in PROJ if p[0] <= k) for k in range(len(W_BLOCKS))]
C_ID, C_TRI, C_ONE, C_IOTA, C_TOK, C_STAY = 0, 128, 256, 384, 416, 419
C_REP, C_PAT, C_HM, C_NEW, C_OH = 419, 675, 739, 747, 811
C_END = C_OH + TABLE_W


def constants():
    c = np.zeros((128, C_END), np.float32)
    i = np.arange(128)
    c[:, C_ID:C_ID + 128] = np.eye(128)
    c[:, C_TRI:C_TRI + 128] = i[:, None] < i[None, :]
    c[:, C_ONE:C_ONE + 128] = 1.0
    b, h, q = i // 32, (i // 4) % 8, i % 4
    for g in range(2):
        tok = (4 * g + b) * DEC_T + q
        c[tok, C_REP + 128 * g + i] = 1.0
        c[i, C_PAT + 32 * g + tok] = 1.0
        for j in range(DEC_T):
            c[i, C_NEW + 32 * g + (4 * g + b) * DEC_T + j] = 1.0
    c[i, C_HM + h] = 1.0
    c[:, C_IOTA:C_IOTA + 32] = np.arange(32)
    c[:, C_TOK:C_TOK + 3] = i[:, None] + 128 * np.arange(3)[None, :]
    dist = DIST0 - np.arange(TABLE_W)
    n = np.maximum(dist, 0)
    nf = np.maximum(n, 1).astype(np.float32)
    large = 16 + (np.log(nf / np.float32(16)) / np.float32(math.log(8.0)) * np.float32(16)).astype(np.int32)
    bucket = np.where(n < 16, n, np.minimum(large, 31))
    for k in range(TABLE_W):
        if dist[k] >= 0:
            c[bucket[k], C_OH + k] = 1.0 / QK_SCALE
        else:
            c[32, C_OH + k] = 1.0
    return c



def build(nc, t, stage=99):
    with ExitStack() as ctx:
        build_in(nc, t, ctx, stage)


def build_in(nc, t, ctx, stage):
    def sem(name):
        return ctx.enter_context(nc.semaphore(name))

    TOTAL = 53200
    mem = ctx.enter_context(nc.sbuf_tensor("mem", [128, TOTAL], F32))

    def region(lo, hi):
        at = [lo]

        def take(*dims):
            n = int(np.prod(dims))
            a = mem[:, at[0]:at[0] + n]
            at[0] += n + n % 2
            assert at[0] <= hi, (lo, hi, at[0])
            names = "abcd"[:len(dims)]
            if len(dims) > 1:
                sizes = {x: d for x, d in zip(names[:-1], dims)}
                a = a.rearrange("p (" + " ".join(names) + ") -> p " + " ".join(names), **sizes)
            return a
        return take

    SLOT = 3 * DC * FE
    S0 = TOTAL - 3 * SLOT
    WORK = 9350
    common = region(0, WORK)
    CST = common(C_STAY)
    X = common(3, D)
    XT = common(DC, NTOK)
    LNP = common(2, D)
    WR = common(DEPTH, DC, NG + NE)
    RBI = common(DEPTH, NG + NE)
    SLOTI, SLOTM, TOKI, IDXI, IDXC, FLAG = common(6), common(6), common(3), common(NE // 2), common(4), common(2)
    ZERO = common(SLOTS // 128)
    NEGH, L8, GT, GATE, EF, RK, QQ, SLOTF = common(1), common(8), common(6), common(6), common(6), common(6), common(6), common(6)
    TOP8, GIX, EIX, GSUM, RR, DEN = common(8), common(8), common(8), common(3), common(3), common(3)
    HOT, HOTK, LG, PEN, RANKT, TKI, TKF = common(3, NE), common(6, NE), common(NG + NE), common(NG), common(NE), common(2 * CAP), common(2 * CAP)
    STATS, MV, VE, RSTD = common(12), common(3, 2), common(3), common(3)
    ID, TRI, ONE = CST[:, C_ID:C_ID + 128], CST[:, C_TRI:C_TRI + 128], CST[:, C_ONE:C_ONE + 128]
    IOTA = CST[:, C_IOTA:C_IOTA + NE]

    slots = [mem[:, S0 + k * SLOT:S0 + (k + 1) * SLOT] for k in range(3)]
    WG = [s[:, 0:4096].rearrange("p (c f) -> p c f", c=DC) for s in slots]
    WU = [s[:, 4096:8192].rearrange("p (c f) -> p c f", c=DC) for s in slots]
    WD = [s[:, 8192:12288].rearrange("p (c n) -> p c n", c=FC) for s in slots]

    slot0 = region(S0, S0 + SLOT)
    WOUT, V, KTOK = slot0(DC, D), slot0(3, 648), slot0(3, 704)
    att = region(S0 + SLOT, TOTAL)
    WIN = [att(DC, 512) for _ in range(3)]
    att_rest = region(S0 + 2 * SLOT, TOTAL)
    QKVT, BM = att_rest(19, NTOK), att_rest(17, 256)
    PB, COMB = att_rest(5, 256), att_rest(4, 256)
    YT = XT
    sample = region(S0 + SLOT, S0 + SLOT + 3 * 4096)
    KRAW = [sample(N_PAGES, 704) for _ in range(2)]
    VRAW = [None, None, *(a[:, :, 0:640] for a in KRAW)]
    KTB = [sample(6, NK_S) for _ in range(2)]
    VRAW[0:2] = [sample(N_PAGES, 640) for _ in range(2)]
    QAS, QBS, QIS, PT = sample(4, DEC_B, 32), sample(DEC_B, 32), sample(DEC_B, 32), sample(4, 3, 128)
    RIS = [sample(NK_S) for _ in range(2)]
    work = region(WORK, S0)
    PTB, SELM, ACC, RELU = work(2, 2, 128), work(2, 256), work(2, 256), work(2, 256)
    SBIAS, SMASK, PS4, SCS = work(2, NK_S), work(NK_S), work(4, NK_S), work(NK_S + PADS_S)
    AC = work(C_END - C_STAY)
    TAB, RB = work(TABLE_W), work(17)
    MX, SUM, RIN = work(32), work(32), work(32)
    SMX, SSUM, SRIN, MX8, WVT, WV, WM, PGT, PN = work(4), work(4), work(4), work(8), work(8), work(2), work(2, 32), work(16), work(4, 32)
    REP, PAT, HM, NEW, OH = (AC[:, a - C_STAY:b - C_STAY] for a, b in (
        (C_REP, C_PAT), (C_PAT, C_HM), (C_HM, C_NEW), (C_NEW, C_OH), (C_OH, C_END)))

    moe = region(WORK, S0)
    XG, HID, HT, YO = moe(3, D), moe(2, FE), moe(2, FC, CAP), moe(2, D // 2)
    XT2 = XT.rearrange("p c n -> p (c n)")
    XGT = [a.rearrange("p (c n) -> p c n", c=DC) for a in (XT2[:, 0:DC * 2 * CAP], XT2[:, DC * 2 * CAP:2 * DC * 2 * CAP], moe(DC * 2 * CAP))]
    YG = region(WORK, S0)(2, D)
    WC = [slots[2 * (k // 3)][:, 4096 * (k % 3):4096 * (k % 3 + 1)].rearrange("p (c n) -> p c n", c=DC) for k in range(6)]
    WCO = region(S0 + SLOT, TOTAL)(DC, D)
    ULT = region(S0 + SLOT + 8192, TOTAL)(D)
    cv = region(WORK, S0)
    ZT, UB, HSB, CB, SCW, SCT, UL = cv(DC, NTOK), cv(2, SEQ + 2 + DEC_B * 6), cv(2, NTOK), cv(2, NTOK), cv(D), cv(DC, 19), cv(DC, 18)

    bank = [ctx.enter_context(nc.psum_tensor(f"bank{i}", [128, 512], F32)) for i in range(8)]

    table_d = nc.dram_tensor("bias_table", [128, 17, TABLE_W], F32).ap()
    xrows_d = [nc.dram_tensor(f"x_rows{i}", [NTOK, D], F32).ap() for i in range(DEPTH)]
    slot_tok_d = [nc.dram_tensor(f"slot_token{i}", [SLOTS, 1], I32).ap() for i in range(DEPTH)]
    yslot_d = [nc.dram_tensor(f"slot_out{i}", [NE * CAP, D], F32).ap() for i in range(DEPTH)]
    ymore_d = [nc.dram_tensor(f"slot_more{i}", [SLOTS - NE * CAP, D], F32).ap() for i in range(DEPTH)]

    ld_const, ld_x, ld_small, ld_rb, ld_ln, ld_pt, ld_wout = (sem("ld_" + n) for n in ("const", "x", "small", "rb", "ln", "pt", "wout"))
    ld_win = [sem(f"ld_win{k}") for k in range(3)]
    st_rows, st_out, st_state, st_tab, ld_bias, ld_state, ld_wco = (sem(n) for n in ("st_rows", "st_out", "st_state", "st_tab", "ld_bias", "ld_state", "ld_wco"))
    act_own, dve_own, pool_own = sem("act_own"), sem("dve_own"), sem("pool_own")
    rb_zero, rb_set, tab_psum, tab_sb = (sem(n) for n in ("rb_zero", "rb_set", "tab_psum", "tab_sb"))
    xT_psum, xT_evac, proj_psum, proj_evac = (sem(n) for n in ("xT_psum", "xT_evac", "proj_psum", "proj_evac"))
    ktok_psum, ktok_evac = sem("ktok_psum"), sem("ktok_evac")
    idx_psum, idx_relu, idx_acc, sel_ready, comb_ready = (sem(n) for n in ("idx_psum", "idx_relu", "idx_acc", "sel_ready", "comb_ready"))
    att_S, att_scored, att_exp, att_p, att_T, att_Tevac, att_O, att_Oevac = (
        sem("att_" + n) for n in ("S", "scored", "exp", "p", "T", "Tevac", "O", "Oevac"))
    ld_k = [sem(f"ld_k{k}") for k in range(2)]
    ld_v = [sem(f"ld_v{k}") for k in range(4)]
    kt_psum, kt_evac, k_new, q_zero, q_cut, smp_S, smp_Sevac, smp_relu = (
        sem(n) for n in ("kt_psum", "kt_evac", "k_new", "q_zero", "q_cut", "smp_S", "smp_Sevac", "smp_relu"))
    w_psum, w_mat, sc_psum, sc_mask, rep_psum = (sem(n) for n in ("w_psum", "w_mat", "sc_psum", "sc_mask", "rep_psum"))
    smp_scored, smp_exp, smp_p, smp_T, smp_Tevac, smp_O, smp_y = (
        sem("smp_" + n) for n in ("scored", "exp", "p", "T", "Tevac", "O", "y"))
    op_psum, op_added, ln_stat, ln_rstd, ln_done = (sem(n) for n in ("op_psum", "op_added", "ln_stat", "ln_rstd", "ln_done"))
    ro_psum, ro_top, ro_exp, ro_hot, ro_rank, ro_slot = (sem("ro_" + n) for n in ("psum", "top", "exp", "hot", "rank", "slot"))
    st_x, zero_set, st_zero, scattered, ld_tok, tok_f, tok_T, tok_idx = (
        sem(n) for n in ("st_x", "zero_set", "st_zero", "scattered", "ld_tok", "tok_f", "tok_T", "tok_idx"))
    ld_wg = [sem(f"ld_wg{k}") for k in range(3)]
    ld_wu = [sem(f"ld_wu{k}") for k in range(3)]
    ld_wd = [sem(f"ld_wd{k}") for k in range(3)]
    gath = [sem(f"gath{k}") for k in range(3)]
    idx_cur, xg_zero, xg_T, xg_evac, gu_psum, silu_done, h_done, ht_T, ht_evac, dn_psum, y_evac = (
        sem(n) for n in ("idx_cur", "xg_zero", "xg_T", "xg_evac", "gu_psum", "silu_done", "h_done", "ht_T", "ht_evac", "dn_psum", "y_evac"))
    st_y = [sem(f"st_y{k}") for k in range(2)]
    ygath = [sem(f"ygath{k}") for k in range(2)]
    y_used, pe_passed, pool_passed = sem("y_used"), sem("pe_passed"), sem("pool_passed")
    ld_wc = [sem(f"ld_wc{k}") for k in range(2)]
    cv_in_T, cv_in, cv_psum, cv_h, cv_u, cv_z, cv_lT, cv_lsb = (
        sem("cv_" + n) for n in ("in_T", "in", "psum", "h", "u", "z", "lT", "lsb"))
    more = [{n: sem(f"more{i}_{n}") for n in ("w", "tok", "gath", "T", "Tevac", "gu", "silu", "h", "hT", "hTe", "dn", "y", "st", "more")} for i in range(DEPTH)]

    def linker(eng, own):
        n = [0]

        def link(ins):
            n[0] += 1
            ins.then_inc(own, 1)
            eng.wait_ge(own, n[0])
        return link

    def wait(eng, s, value):
        if isinstance(value, int) and value <= 0:
            return
        eng.wait_ge(s, value)

    def number(i, u):
        return 6 * i + u

    ORDER = [(2, 1, 0), (0, 2, 1)]

    def slot_of(layer, u):
        return ORDER[layer][u % 3]

    def slot_loads(layer, i, u):
        before = sum(1 for e in range(layer * NE) if slot_of(0, e) == slot_of(layer, u))
        return 16 * (before + 2 * i + u // 3 + 1)

    def store_count(layer, i, u):
        return 16 * (layer * (NE // 2) + 3 * i + u // 2 + 1)

    def gather_count(layer, i, v):
        before = layer * sum(1 for q in range(NE // 2) if q % 3 == v % 3)
        return 16 * (before + i + 1)

    AHEAD, NP, NSB = 3, 5, 4
    S_BANKS = (0, 1, 6, 7)
    tiled = "(t p) n -> p t n"
    flat = "l b t h d -> (l b t) (h d)"
    n_more = (PASSES - 1) * NE

    block = ctx.enter_context(nc.Block())

    @block.sync
    def _(sp):
        w_in = t["w_attn_in"][0].rearrange("(c p) n -> p c n", p=128)
        sp.dma_start(CST, t["consts"][:, 0:C_STAY]).then_inc(ld_const, 16)
        sp.dma_start(AC, t["consts"][:, C_STAY:C_END]).then_inc(ld_const, 16)
        sp.dma_start(X[:, 0:2, :], t["x_prompt"][0].rearrange("(t p) d -> p t d", p=128)).then_inc(ld_x, 16)
        sp.dma_start(X[0:NS, 2, :], t["x_sample"].rearrange("b t d -> (b t) d")).then_inc(ld_x, 16)
        for k, (lo, n) in enumerate(W_BLOCKS):
            if k >= 3:
                sp.wait_ge(proj_psum, PROJ_END[k - 3])
            sp.dma_start(WIN[k % 3][:, :, 0:n], w_in[:, :, lo:lo + n]).then_inc(ld_win[k % 3], 16)
        sp.dma_start(WOUT, t["w_attn_out"][0].rearrange("(c p) n -> p c n", p=128)).then_inc(ld_wout, 16)

        def load_ln(k):
            sp.dma_start(LNP[:, 0, :], t["ln_g"][k // 2, k % 2].partition_broadcast(128)).then_inc(ld_ln, 16)
            sp.dma_start(LNP[:, 1, :], t["ln_b"][k // 2, k % 2].partition_broadcast(128)).then_inc(ld_ln, 16)

        load_ln(0)
        sp.wait_ge(proj_evac, len(PROJ))
        sp.dma_start(t["new_v_a_prompt"].rearrange(flat).rearrange(tiled, p=128), V[:, 0:2, 0:512]).then_inc(st_rows, 16)
        sp.dma_start(t["new_v_b_prompt"].rearrange(flat).rearrange(tiled, p=128), V[:, 0:2, 512:640]).then_inc(st_rows, 16)
        sp.dma_start(t["new_v_a_sample"].rearrange(flat), V[0:NS, 2, 0:512]).then_inc(st_rows, 16)
        sp.dma_start(t["new_v_b_sample"].rearrange(flat), V[0:NS, 2, 512:640]).then_inc(st_rows, 16)
        sp.wait_ge(ktok_evac, 6)
        sp.dma_start(t["new_k_a_prompt"].rearrange(flat).rearrange(tiled, p=128), KTOK[:, 0:2, 0:512]).then_inc(st_rows, 16)
        sp.dma_start(t["new_k_b_prompt"].rearrange(flat).rearrange(tiled, p=128), KTOK[:, 0:2, 512:640]).then_inc(st_rows, 16)
        sp.dma_start(t["new_k_idx_prompt"].rearrange("l b t d -> (l b t) d").rearrange(tiled, p=128), KTOK[:, 0:2, 640:704]).then_inc(st_rows, 16)
        sp.dma_start(t["new_k_a_sample"].rearrange(flat), KTOK[0:NS, 2, 0:512]).then_inc(st_rows, 16)
        sp.dma_start(t["new_k_b_sample"].rearrange(flat), KTOK[0:NS, 2, 512:640]).then_inc(st_rows, 16)
        sp.dma_start(t["new_k_idx_sample"].rearrange("l b t d -> (l b t) d"), KTOK[0:NS, 2, 640:704]).then_inc(st_rows, 16)
        pages = "l p t h d -> (l p) t (h d)"
        k_caches = [(t["cache_k_a"].rearrange(pages), 0, 512), (t["cache_k_b"].rearrange(pages), 512, 128),
                    (t["cache_k_idx"].rearrange("l p t d -> (l p) t d"), 640, 64)]
        v_caches = [(t["cache_v_a"].rearrange(pages), 0, 512), (t["cache_v_b"].rearrange(pages), 512, 128)]
        n_phys = k_caches[0][0].shape[0]
        sp.wait_ge(ld_pt, 16)
        for caches, buf, ld in ((k_caches, KRAW, ld_k), (v_caches, VRAW, ld_v)):
            for b in range(DEC_B):
                if caches is k_caches:
                    wait(sp, kt_psum, 3 * (b - 1))
                elif b in (2, 3):
                    sp.wait_ge(kt_psum, 3 * (DEC_B - 3 + b))
                else:
                    wait(sp, smp_O, b - 3)
                for pg in range(N_PAGES):
                    page = sp.value_load(PGT[0:1, b * N_PAGES + pg:b * N_PAGES + pg + 1].bitcast(I32), min_val=0, max_val=n_phys - 1)
                    for cache, lo, n in caches:
                        sp.dma_start(buf[b % len(buf)][:, pg, lo:lo + n], cache[page]).then_inc(ld[b % len(buf)], 16)
        sp.wait_ge(st_rows, 160)
        if stage < 6:
            return

        def load_expert(layer, i, u, free=None):
            e, k = number(i, u), slot_of(layer, u)
            if free is not None:
                wait(sp, gu_psum, free)
            sp.dma_start(WG[k], t["w_exp_gate"][layer, e].rearrange("(p c) f -> p c f", c=DC)).then_inc(ld_wg[k], 16)
            sp.dma_start(WU[k], t["w_exp_up"][layer, e].rearrange("(p c) f -> p c f", c=DC)).then_inc(ld_wu[k], 16)
            if free is not None:
                wait(sp, dn_psum, free)
            sp.dma_start(WD[k], t["w_exp_down"][layer, e].rearrange("(c p) n -> p c n", p=128)).then_inc(ld_wd[k], 16)

        def experts(layer):
            base = NE * layer
            sp.wait_ge(ln_done, 6 * layer + 3)
            sp.dma_start(xrows_d[layer][0:SEQ].rearrange(tiled, p=128), X[:, 0:2, :]).then_inc(st_x, 16)
            sp.dma_start(xrows_d[layer][SEQ:NTOK], X[0:NS, 2, :]).then_inc(st_x, 16)
            load_ln(2 * layer + 1)
            sp.wait_ge(gath[1], gather_count(layer, 0, 1))
            load_expert(layer, 0, 2)
            for u in (3, 4, 5):
                load_expert(layer, 0, u, base + u - 2)
            with sp.Fori(1, NE // 6) as i:
                for u in range(6):
                    load_expert(layer, i, u, base + number(i, u) - 2)
            for u in range(NE % 6):
                load_expert(layer, NE // 6, u, base + number(NE // 6, u) - 2)
            s = more[layer]
            full = sp.value_load(FLAG[0:1, layer:layer + 1].bitcast(I32), min_val=0, max_val=1)
            with sp.If(full > 0):
                sp.wait_ge(dn_psum, base + NE)
                with sp.Fori(1, PASSES) as r:
                    with sp.Fori(0, NE) as e:
                        sp.wait_ge(s["dn"], (r - 1) * NE + e)
                        sp.dma_start(WG[0], t["w_exp_gate"][layer, e].rearrange("(p c) f -> p c f", c=DC)).then_inc(s["w"], 16)
                        sp.dma_start(WU[0], t["w_exp_up"][layer, e].rearrange("(p c) f -> p c f", c=DC)).then_inc(s["w"], 16)
                        sp.dma_start(WD[0], t["w_exp_down"][layer, e].rearrange("(c p) n -> p c n", p=128)).then_inc(s["w"], 16)
                sp.wait_ge(s["dn"], n_more)
                sp.wait_ge(s["st"], 16 * n_more)
            with sp.Else():
                sp.nop()

        sp.wait_ge(smp_Tevac, 4)
        load_expert(0, 0, 0)
        sp.wait_ge(smp_y, 1)
        load_expert(0, 0, 1)
        sp.wait_ge(op_psum, 3)
        experts(0)
        if stage < 8:
            return
        w_cv = t["w_conv_in"][0].rearrange("(c p) n -> p c n", p=128)

        def load_conv(half):
            for part in range(3):
                lo = part * D + half * 512
                sp.dma_start(WC[3 * half + part], w_cv[:, :, lo:lo + 512]).then_inc(ld_wc[half], 16)

        sp.wait_ge(gu_psum, NE - 2)
        sp.wait_ge(dn_psum, NE - 2)
        load_conv(0)
        for k in range(2):
            sp.wait_ge(ygath[k], 48)
        load_conv(1)
        sp.wait_ge(ln_done, 6)
        load_ln(2)
        sp.dma_start(WCO, t["w_conv_out"][0].rearrange("(c p) n -> p c n", p=128)).then_inc(ld_wco, 16)
        sp.wait_ge(cv_psum, 12)
        load_expert(1, 0, 0)
        sp.wait_ge(cv_psum, 24)
        load_expert(1, 0, 1)
        sp.wait_ge(cv_lsb, 1)
        sp.dma_start(t["new_conv_prompt"].rearrange("l b t d -> (l b t) d"), ULT[0:2, :]).then_inc(st_state, 16)
        sp.dma_start(t["new_conv_sample"].rearrange("l b t d -> (l b t) d"), ULT[2:18, :]).then_inc(st_state, 16)
        sp.wait_ge(st_state, 32)
        sp.wait_ge(op_psum, 6)
        experts(1)
        sp.wait_ge(ln_done, 12)
        sp.dma_start(t["y_prompt"][0].rearrange("(t p) d -> p t d", p=128), X[:, 0:2, :]).then_inc(st_out, 16)
        sp.dma_start(t["y_sample"].rearrange("b t d -> (b t) d"), X[0:NS, 2, :]).then_inc(st_out, 16)
        sp.wait_ge(st_out, 32)

    @block.gpsimd
    def _(pool):
        link = linker(pool, pool_own)
        nc.gpsimd.memset(ZERO.bitcast(I32), NTOK).then_inc(zero_set, 1)
        nc.gpsimd.memset(NEGH, -0.5).then_inc(zero_set, 1)
        pool.wait_ge(zero_set, 2)
        for layer in range(DEPTH):
            pool.dma_start(slot_tok_d[layer].rearrange("(p n) o -> p (n o)", p=128), ZERO.bitcast(I32)).then_inc(st_zero, 16)
        pool.wait_ge(proj_evac, len(PROJ))
        for u in range(2 * HB):
            h, qt = HA + u // 2, u % 2
            n = 128 * (qt + 1)
            if u == 0:
                pool.wait_ge(ld_bias, 16 * 10)
                pool.wait_ge(sel_ready, 2)
            wait(pool, att_scored, 2 * HA + u - 3)
            nc.gpsimd.tensor_tensor(COMB[:, u % 4, 0:n], BM[:, h, 256 - n:256] if qt == 0 else BM[:, h, 0:n],
                                    SELM[:, qt, 0:n], ALU.add).then_inc(comb_ready, 1)
        for b in range(DEC_B):
            lo = SEQ + DEC_T * b
            wait(pool, smp_S, b - 1)
            nc.gpsimd.tensor_copy(KTB[b % 2][:, 0:4, PAST:NK_S], QKVT[:, KA:KA + 4, lo:lo + DEC_T])
            nc.gpsimd.tensor_copy(KTB[b % 2][:, 4, PAST:NK_S], QKVT[:, KB, lo:lo + DEC_T])
            nc.gpsimd.tensor_copy(KTB[b % 2][0:64, 5, PAST:NK_S], QKVT[0:64, KI, lo:lo + DEC_T]).then_inc(k_new, 1)
        if stage < 5:
            return

        def rstd(k, tiles=range(3)):
            for i in tiles:
                n = TILES[i][1]
                pool.wait_ge(ln_stat, 3 * k + i + 1)
                nc.gpsimd.tensor_tensor(RSTD[0:n, i:i + 1], VE[0:n, i:i + 1], NEGH[0:n], ALU.pow).then_inc(ln_rstd, 1)

        def experts(layer):
            base = NE * layer
            pool.wait_ge(ro_slot, 2 * layer + 2)
            pool.wait_ge(st_zero, 16 * DEPTH)
            if layer == 0:
                nc.gpsimd.iota(TOKI.bitcast(I32), pattern=[[128, 3]], base=0, channel_multiplier=1).then_inc(zero_set, 1)
                pool.wait_ge(zero_set, 3)
            for i, (_, n) in enumerate(TILES):
                for k in range(2):
                    pool.indirect_dma_start(
                        out=slot_tok_d[layer], out_offset=bass.IndirectOffsetOnAxis(ap=SLOTI[0:n, 2 * i + k:2 * i + k + 1].bitcast(I32), axis=0),
                        in_=TOKI[0:n, i:i + 1].bitcast(I32), in_offset=None).then_inc(scattered, 16)
            pool.wait_ge(scattered, 96 * (layer + 1))
            pool.dma_start(TKI[0:NE // 2, :].bitcast(I32), slot_tok_d[layer][0:NE * CAP].rearrange("(e j) o -> e (j o)", e=NE // 2)).then_inc(ld_tok, 16)
            nc.gpsimd.memset(XG, 0.0).then_inc(xg_zero, 1)
            pool.wait_ge(tok_idx, layer + 1)
            pool.wait_ge(st_x, 32 * (layer + 1))

            pool.wait_ge(xg_zero, layer + 1)

            def gather(i, v):
                q = 3 * i + v
                wait(pool, xg_T, base // 2 + q - 2)
                nc.gpsimd.tensor_copy(IDXC[0:2 * CAP, v:v + 1].bitcast(I32), IDXI[0:2 * CAP, bass.ds(q, 1)].bitcast(I32)).then_inc(idx_cur, 1)
                pool.wait_ge(idx_cur, base // 2 + q + 1)
                pool.sem_inc(pool_passed, 1)
                pool.indirect_dma_start(
                    out=XG[0:2 * CAP, v, :], out_offset=None, in_=xrows_d[layer],
                    in_offset=bass.IndirectOffsetOnAxis(ap=IDXC[0:2 * CAP, v:v + 1].bitcast(I32), axis=0),
                    bounds_check=NTOK - 1, oob_is_err=False).then_inc(gath[v], 16)

            for v in range(3):
                gather(0, v)
            with pool.Fori(1, NE // 6) as i:
                for v in range(3):
                    gather(i, v)
            gather(NE // 6, 0)
            s = more[layer]
            full = pool.value_load(FLAG[0:1, layer:layer + 1].bitcast(I32), min_val=0, max_val=1)
            pool.wait_ge(xg_T, (base + NE) // 2)
            with pool.If(full > 0):
                with pool.Fori(1, PASSES) as r:
                    with pool.Fori(0, NE) as e:
                        n = (r - 1) * NE + e
                        pool.wait_ge(s["T"], n)
                        pool.dma_start(IDXC[0:CAP, 0:1].bitcast(I32), slot_tok_d[layer][bass.ds((r * NE + e) * CAP, CAP)]).then_inc(s["tok"], 16)
                        pool.wait_ge(s["tok"], 16 * (n + 1))
                        pool.sem_inc(pool_passed, 1)
                        pool.indirect_dma_start(
                            out=XG[0:CAP, 0, :], out_offset=None, in_=xrows_d[layer],
                            in_offset=bass.IndirectOffsetOnAxis(ap=IDXC[0:CAP, 0:1].bitcast(I32), axis=0),
                            bounds_check=NTOK - 1, oob_is_err=False).then_inc(s["gath"], 16)
                pool.wait_ge(s["st"], 16 * n_more)
            with pool.Else():
                pool.nop()
            for k in range(2):
                pool.wait_ge(st_y[k], 16 * (NE // 2) * (layer + 1))
            for j in range(6):
                n = TILES[j // 2][1]
                wait(pool, y_used, 6 * layer + j - 1)
                with pool.If(full > 0):
                    pool.indirect_dma_start(
                        out=YG[0:n, j % 2, :], out_offset=None, in_=ymore_d[layer],
                        in_offset=bass.IndirectOffsetOnAxis(ap=SLOTM[0:n, j:j + 1].bitcast(I32), axis=0),
                        bounds_check=SLOTS - NE * CAP - 1, oob_is_err=False).then_inc(s["more"], 16)
                    pool.wait_ge(s["more"], 16 * (j + 1))
                with pool.Else():
                    pool.nop()
                pool.indirect_dma_start(
                    out=YG[0:n, j % 2, :], out_offset=None, in_=yslot_d[layer],
                    in_offset=bass.IndirectOffsetOnAxis(ap=SLOTI[0:n, j:j + 1].bitcast(I32), axis=0),
                    bounds_check=NE * CAP - 1, oob_is_err=False).then_inc(ygath[j % 2], 16)
                if j % 2 == 1 and j > 1:
                    rstd(2 * layer + 1, [j // 2 - 1])
            rstd(2 * layer + 1, [2])

        rstd(0)
        if stage < 6:
            return
        experts(0)
        if stage < 8:
            return
        rstd(2)
        experts(1)

    @block.scalar
    def _(act):
        link = linker(act, act_own)

        def copy(out, in_):
            return nc.scalar.copy(out, in_)

        def silu(out, in_):
            return nc.scalar.activation(out, in_, ACT.Silu)

        act.wait_ge(rb_zero, 1)
        act.dma_start(RB[0:32, 0:16], t["rel_bias"]).then_inc(ld_rb, 16)
        act.dma_start(PGT[0:1, :].bitcast(I32), t["page_table"].rearrange("(o b) n -> o (b n)", o=1)).then_inc(ld_pt, 16)
        for i in range(DEPTH):
            act.dma_start(WR[:, i, :, 0:NG], t["w_router_group"][i].rearrange("(c p) n -> p c n", p=128)).then_inc(ld_small, 16)
            act.dma_start(WR[:, i, :, NG:NG + NE], t["w_router_expert"][i].rearrange("(c p) n -> p c n", p=128)).then_inc(ld_small, 16)
            act.dma_start(RBI[:, i, 0:NG], t["b_router_group"][i].partition_broadcast(128)).then_inc(ld_small, 16)
            act.dma_start(RBI[:, i, NG:NG + NE], t["b_router_expert"][i].partition_broadcast(128)).then_inc(ld_small, 16)
        def load_biases():
            act.wait_ge(st_tab, 16)

            def skew(offset, dims):
                return bass.AP(tensor=table_d.tensor, offset=offset, ap=dims)

            pitch = 17 * TABLE_W
            act.dma_start(BM, skew(DIST0 - 128, [[pitch - 1, 128], [TABLE_W, 17], [1, 256]])).then_inc(ld_bias, 16)
            for q in range(4):
                for g in range(2):
                    act.dma_start(SBIAS[32 * q:32 * q + 32, g, :],
                                  skew(DIST0 - PAST + 8 * g * TABLE_W, [[TABLE_W, 8], [pitch - 1, 4], [1, NK_S]])).then_inc(ld_bias, 16)
            act.dma_start(SMASK[0:NS, :], skew(DIST0 - PAST + 16 * TABLE_W, [[4 * pitch, 8], [pitch - 1, 4], [1, NK_S]])).then_inc(ld_bias, 16)

        def evac_xT(k):
            for c in range(DC):
                act.wait_ge(xT_psum, DC * k + c + 1)
                copy(XT[:, c, :], bank[c % 4][:, 0:NTOK]).then_inc(xT_evac, 1)

        act.wait_ge(tab_psum, 1)
        copy(TAB[0:17, :], bank[7][0:17, 0:TABLE_W]).then_inc(tab_sb, 1)
        act.wait_ge(tab_sb, 1)
        act.dma_start(table_d.rearrange("p h n -> h p n"), TAB[0:17, :].unsqueeze(1).to_broadcast([17, 128, TABLE_W])).then_inc(st_tab, 16)
        evac_xT(0)
        for g, (_, _, n, chunk, tile, col) in enumerate(PROJ):
            if g == 12:
                load_biases()
            act.wait_ge(proj_psum, g + 1)
            src = bank[4 + g % 4]
            if chunk is None:
                rows = TILES[tile][1]
                copy(V[0:rows, tile, col:col + n], src[0:rows, 0:n]).then_inc(proj_evac, 1)
            elif chunk == KB:
                copy(QKVT[:, KB, :], src[:, 0:NTOK])
                copy(QKVT[0:64, KBS, :], src[64:128, 0:NTOK])
                copy(QKVT[64:128, KBS, :], src[0:64, 0:NTOK]).then_inc(proj_evac, 1)
            elif chunk == KI:
                copy(QKVT[0:64, KI, :], src[0:64, 0:NTOK])
                copy(QKVT[64:128, KI, :], src[0:64, 0:NTOK]).then_inc(proj_evac, 1)
            else:
                copy(QKVT[:, chunk, :], src[:, 0:NTOK]).then_inc(proj_evac, 1)
        for i in range(2 * HI):
            n = 128 * (i // HI + 1)
            act.wait_ge(idx_psum, i + 1)
            wait(act, idx_acc, i - 1)
            nc.scalar.activation(RELU[:, i % 2, 0:n], bank[i % 2][:, 0:n], ACT.Relu).then_inc(idx_relu, 1)

        def exps(u):
            n = 128 * (u % 2 + 1)
            act.wait_ge(att_scored, u + 1)
            nc.scalar.activation(PB[:, u % NP, 0:n], PB[:, u % NP, 0:n], ACT.Exp, bias=MX[:, u:u + 1], scale=-1.0,
                                 accum_out=SUM[:, u:u + 1]).then_inc(att_exp, 1)

        def evac_T(u):
            act.wait_ge(att_T, u + 1)
            wait(act, att_O, u - 1)
            copy(PTB[:, u % 2, 0:u % 2 + 1, :], bank[2 + u % 2][:, 0:128 * (u % 2 + 1)].rearrange("p (a b) -> p a b", b=128)).then_inc(att_Tevac, 1)

        for u in range(AHEAD):
            exps(u)
        for u in range(2 * HEADS):
            if u + AHEAD < 2 * HEADS:
                exps(u + AHEAD)
            evac_T(u)
            if u % 4 == 3:
                act.wait_ge(att_O, u + 1)
                copy(YT[:, u // 4, 0:SEQ], bank[4 + (u // 4) % 2][:, 0:SEQ]).then_inc(att_Oevac, 1)
        if stage < 4:
            return
        for b in range(DEC_B):
            wait(act, smp_S, b - 1)
            for j in range(3):
                g = 3 * b + j
                act.wait_ge(kt_psum, g + 1)
                src = bank[g % 4][:, :].rearrange("p (a b) -> p a b", b=128)
                if j < 2:
                    copy(KTB[b % 2][:, 0:4, 128 * j:128 * j + 128], src).then_inc(kt_evac, 1)
                else:
                    copy(KTB[b % 2][:, 4, 0:PAST], src[:, 0:2, :])
                    copy(KTB[b % 2][0:64, 5, 0:PAST], src[0:64, 2:4, :]).then_inc(kt_evac, 1)
            if b % 4 == 3:
                act.wait_ge(smp_S, b + 1)
                nc.scalar.activation(RIS[b // 4], bank[6][:, 0:NK_S], ACT.Relu).then_inc(smp_relu, 1)
        for j in range(4):
            act.wait_ge(smp_scored, j + 1)
            nc.scalar.activation(PS4[:, j, :], PS4[:, j, :], ACT.Exp, bias=SMX[:, j:j + 1],
                                 accum_out=SSUM[:, j:j + 1]).then_inc(smp_exp, 1)
        for j in range(4):
            act.wait_ge(smp_T, j + 1)
            copy(PT[:, j, :, :], bank[j % 4][:, 0:384].rearrange("p (a b) -> p a b", b=128)).then_inc(smp_Tevac, 1)
        act.wait_ge(smp_O, DEC_B)
        oa = bank[4][:, 0:256].rearrange("p (b c x) -> p b c x", b=DEC_B, c=4)
        ob = bank[5][:, 0:128].rearrange("p (b k i q) -> p b k i q", b=DEC_B, k=2, i=2)
        for c in range(4):
            dst = YT[:, c, SEQ:NTOK].rearrange("p (b q) -> p b q", b=DEC_B)
            copy(dst[0:64], oa[0:64, :, c, 0:4])
            copy(dst[64:128], oa[64:128, :, c, 4:8])
            last = copy(YT[:, 4 + c, SEQ:NTOK].rearrange("p (b q) -> p b q", b=DEC_B), ob[:, :, c // 2, c % 2, :])
        last.then_inc(smp_y, 1)
        if stage < 6:
            return

        def experts(layer):
            base = NE * layer
            for i in range(3):
                act.wait_ge(ro_top, 2 * (3 * layer + i) + 1)
                nc.scalar.activation(L8[0:TILES[i][1], 0:NG], L8[0:TILES[i][1], 0:NG], ACT.Exp, bias=GT[0:TILES[i][1], 0:1],
                                     accum_out=GSUM[0:TILES[i][1], i:i + 1]).then_inc(ro_exp, 1)
                act.wait_ge(ro_top, 2 * (3 * layer + i) + 2)
                nc.scalar.activation(RR[0:TILES[i][1], i:i + 1], TOP8[0:TILES[i][1], 1:2], ACT.Exp,
                                     bias=GT[0:TILES[i][1], 1:2]).then_inc(ro_exp, 1)

            def store(row0, table, y, done):
                return act.dma_start(table[bass.ds(row0, CAP)].rearrange("j (h n) -> h j n", h=2),
                                     y).then_inc(done, 16)

            def gathered(i, v):
                Q = base // 2 + 3 * i + v
                act.wait_ge(xg_T, Q + 1)
                wait(act, gu_psum, 2 * Q - 4)
                for half in range(2):
                    last = copy(XGT[v][:, 4 * half:4 * half + 4, :],
                                bank[half][:, 0:8 * CAP].rearrange("p (c n) -> p c n", c=4))
                last.then_inc(xg_evac, 1)

            def output(i, u):
                E, k = base + number(i, u), u % 2
                act.wait_ge(dn_psum, E + 1)
                wait(act, st_y[k], store_count(layer, i, u) - 16)
                copy(YO[0:2 * CAP, k, :], bank[6 + k][0:2 * CAP, :]).then_inc(y_evac, 1)
                act.wait_ge(y_evac, E + 1)
                store(number(i, u) * CAP, yslot_d[layer], YO[0:2 * CAP, k, :], st_y[k])

            def step(i, u, before, nxt):
                E, k = base + number(i, u), u % 2
                act.wait_ge(gu_psum, E + 1)
                wait(act, ht_T, E - 1)
                silu(HID[CAP:2 * CAP, k, :], bank[2 + k][0:CAP, :]).then_inc(silu_done, 1)
                if before is not None:
                    output(*before)
                if nxt is not None:
                    gathered(*nxt)

            gathered(0, 0)
            for u in range(6):
                step(0, u, (0, u - 1) if u else None, (0, u // 2 + 1) if u in (0, 2) else (1, 0) if u == 4 else None)
            with act.Fori(1, NE // 6) as i:
                for u in range(6):
                    step(i, u, (i, u - 1) if u else (i - 1, 5), (i, u // 2 + 1) if u in (0, 2) else (i + 1, 0) if u == 4 else None)
            for u in range(NE % 6):
                step(NE // 6, u, (NE // 6, u - 1) if u else (NE // 6 - 1, 5), None)
            output(NE // 6, NE % 6 - 1)
            s = more[layer]
            full = act.value_load(FLAG[0:1, layer:layer + 1].bitcast(I32), min_val=0, max_val=1)
            for k in range(2):
                act.wait_ge(st_y[k], 16 * (NE // 2) * (layer + 1))
            with act.If(full > 0):
                with act.Fori(1, PASSES) as r:
                    with act.Fori(0, NE) as e:
                        n = (r - 1) * NE + e
                        act.wait_ge(s["T"], n + 1)
                        copy(XGT[0][:, :, 0:CAP], bank[0][:, 0:DC * CAP].rearrange("p (c n) -> p c n", c=DC)).then_inc(s["Tevac"], 1)
                        act.wait_ge(s["gu"], n + 1)
                        silu(HID[CAP:2 * CAP, 0, :], bank[2][0:CAP, :]).then_inc(s["silu"], 1)
                        act.wait_ge(s["dn"], n + 1)
                        act.wait_ge(s["st"], 16 * n)
                        copy(YO[0:2 * CAP, 0, :], bank[6][0:2 * CAP, :]).then_inc(s["y"], 1)
                        act.wait_ge(s["y"], n + 1)
                        store(n * CAP, ymore_d[layer], YO[0:2 * CAP, 0, :], s["st"])
                act.wait_ge(s["st"], 16 * n_more)
            with act.Else():
                act.nop()

        evac_xT(1)
        experts(0)
        if stage < 8:
            return
        act.dma_start(SCW[0:16, :], t["state_conv"].rearrange("l b w d -> (l b w) d")).then_inc(ld_state, 16)
        act.dma_start(SCW[16:19, :], t["conv_w"][0]).then_inc(ld_state, 16)
        evac_xT(2)
        act.wait_ge(cv_in_T, 1)
        copy(SCT, bank[6][:, 0:DC * 19].rearrange("p (c n) -> p c n", c=DC)).then_inc(cv_in, 1)
        for j in range(DC):
            k = j % 2
            act.wait_ge(cv_psum, 3 * j + 1)
            wait(act, cv_u, j - 1)
            copy(HSB[:, k, :], bank[3 * k][:, 0:NTOK]).then_inc(cv_h, 1)
        act.wait_ge(cv_lT, 1)
        copy(ULT[0:18, 0:512], bank[6][0:18, :])
        copy(ULT[0:18, 512:D], bank[7][0:18, :]).then_inc(cv_lsb, 1)
        evac_xT(3)
        experts(1)

    @block.vector
    def _(dve):
        link = linker(dve, dve_own)
        V_ = nc.vector
        V_.memset(RB[0:33, :], 0.0).then_inc(rb_set, 1)
        dve.wait_ge(rb_set, 1)
        V_.memset(RB[32:33, :], NEG).then_inc(rb_zero, 1)
        for g in range(6):
            dve.wait_ge(ktok_psum, g + 1)
            i, part = g // 2, g % 2
            n = TILES[i][1]
            lo, cols = (0, 512) if part == 0 else (512, 192)
            V_.tensor_copy(KTOK[0:n, i, lo:lo + cols], bank[g % 4][0:n, 0:cols]).then_inc(ktok_evac, 1)
        for i in range(2 * HI):
            qt, h = i // HI, i % HI
            n = 128 * (qt + 1)
            acc, w = ACC[:, qt, 0:n], V[:, qt, 640 + h:641 + h]
            dve.wait_ge(idx_relu, i + 1)
            if h == 0:
                V_.tensor_scalar(acc, RELU[:, i % 2, 0:n], w, None, ALU.mult).then_inc(idx_acc, 1)
            else:
                V_.scalar_tensor_tensor(acc, RELU[:, i % 2, 0:n], w, acc, ALU.mult, ALU.add).then_inc(idx_acc, 1)
            dve.wait_ge(idx_acc, i + 1)
        dve.wait_ge(ld_bias, 16 * 10)

        def select_top(scores, rounds, rows):
            for _ in range(rounds):
                link(V_.max(MX8[0:rows, :], scores))
                link(V_.match_replace(scores, MX8[0:rows, :], scores, TAKEN))

        for qt in range(2):
            n = 128 * (qt + 1)
            acc = ACC[:, qt, 0:n]
            link(V_.scalar_tensor_tensor(acc, acc, IDX_SCALE, BM[:, 16, 128:256] if qt == 0 else BM[:, 16, :], ALU.mult, ALU.add))
            select_top(acc, ROUNDS_P, 128)
            V_.tensor_scalar(SELM[:, qt, 0:n], acc, TAKEN / 2, NEG, ALU.is_ge, ALU.mult).then_inc(sel_ready, 1)

        def score(u):
            h, qt = u // 2, u % 2
            n = 128 * (qt + 1)
            dve.wait_ge(att_S, u + 1)
            wait(dve, att_T, u - NP + 1)
            if h < HA:
                bias = BM[:, h, 128:256] if qt == 0 else BM[:, h, :]
            else:
                dve.wait_ge(comb_ready, u - 2 * HA + 1)
                bias = COMB[:, u % 4, 0:n]
            V_.tensor_tensor_reduce(PB[:, u % NP, 0:n], bank[S_BANKS[u % NSB]][:, 0:n], bias, -QK_SCALE, 3e38,
                                    ALU.add, ALU.min, MX[:, u:u + 1]).then_inc(att_scored, 1)

        def norm(u):
            n = 128 * (u % 2 + 1)
            dve.wait_ge(att_exp, u + 1)
            link(V_.reciprocal(RIN[:, u:u + 1], SUM[:, u:u + 1]))
            V_.tensor_scalar(PB[:, u % NP, 0:n], PB[:, u % NP, 0:n], RIN[:, u:u + 1], None, ALU.mult).then_inc(att_p, 1)

        for u in range(AHEAD):
            score(u)
        for u in range(2 * HEADS):
            if u + AHEAD < 2 * HEADS:
                score(u + AHEAD)
            norm(u)
        if stage < 4:
            return
        V_.memset(QAS, 0.0)
        V_.memset(QBS, 0.0).then_inc(q_zero, 1)
        dve.wait_ge(q_zero, 1)
        for h in range(HA):
            p, c = 64 * (h % 2), h // 2
            kv = 64 * (h // (HB // KVB))

            def cut(lo, chunk):
                return QKVT[lo:lo + 64, chunk, SEQ:NTOK].rearrange("p (b q) -> p b q", b=DEC_B)
            V_.tensor_copy(QAS[p:p + 64, c, :, 4 * h:4 * h + 4], cut(p, QA + c))
            V_.tensor_copy(QBS[kv:kv + 64, :, 4 * h:4 * h + 4], cut(p, QB + c))
            last = V_.tensor_copy(QIS[0:64, :, 4 * h:4 * h + 4], cut(p, QI + c))
        last.then_inc(q_cut, 1)
        dve.wait_ge(w_psum, 1)
        for g in range(2):
            link(V_.tensor_tensor(WVT, bank[7][:, 8 * g:8 * g + 8], HM, ALU.mult))
            link(V_.tensor_reduce(WV[:, g:g + 1], WVT, AX.X, ALU.add))
            V_.tensor_scalar(WM[:, g, :], PAT[:, 32 * g:32 * g + 32], WV[:, g:g + 1], None, ALU.mult).then_inc(w_mat, 1)
        for g in range(2):
            dve.wait_ge(smp_S, 4 * g + 4)
            link(V_.tensor_tensor_reduce(PS4[:, g, :], bank[4][:, 0:NK_S], SBIAS[:, 0, :], QK_SCALE, -3e38,
                                         ALU.add, ALU.max, SMX[:, g:g + 1]))
            V_.tensor_scalar(SMX[:, g:g + 1], SMX[:, g:g + 1], -1.0, None, ALU.mult).then_inc(smp_scored, 1)
            V_.tensor_tensor(PS4[:, 2 + g, :], bank[5][:, 0:NK_S], SBIAS[:, 1, :], ALU.add).then_inc(smp_Sevac, 1)
        dve.wait_ge(sc_psum, 1)
        V_.memset(SCS[0:NS, NK_S:NK_S + PADS_S], -TAKEN)
        link(V_.scalar_tensor_tensor(SCS[0:NS, 0:NK_S], bank[7][0:NS, 0:NK_S], IDX_SCALE, SMASK[0:NS, :], ALU.mult, ALU.add))
        select_top(SCS[0:NS, :], ROUNDS_S, NS)
        V_.tensor_scalar(SMASK[0:NS, :], SCS[0:NS, 0:NK_S], TAKEN / 2, NEG, ALU.is_ge, ALU.mult).then_inc(sc_mask, 1)
        dve.wait_ge(smp_Sevac, 2)
        for g in range(2):
            dve.wait_ge(rep_psum, g + 1)
            link(V_.tensor_tensor_reduce(PS4[:, 2 + g, :], bank[g][:, 0:NK_S], PS4[:, 2 + g, :], QK_SCALE, -3e38,
                                         ALU.add, ALU.max, SMX[:, 2 + g:3 + g]))
            V_.tensor_scalar(SMX[:, 2 + g:3 + g], SMX[:, 2 + g:3 + g], -1.0, None, ALU.mult).then_inc(smp_scored, 1)
        for j in range(4):
            g = j % 2
            dve.wait_ge(smp_exp, j + 1)
            link(V_.reciprocal(SRIN[:, j:j + 1], SSUM[:, j:j + 1]))
            link(V_.tensor_scalar(PS4[:, j, :], PS4[:, j, :], SRIN[:, j:j + 1], None, ALU.mult))
            V_.tensor_tensor(PN[:, j, :].rearrange("p (b q) -> p b q", b=DEC_B),
                             PS4[:, j, PAST:NK_S].unsqueeze(1).to_broadcast([128, DEC_B, DEC_T]),
                             NEW[:, 32 * g:32 * g + 32].rearrange("p (b q) -> p b q", b=DEC_B), ALU.mult).then_inc(smp_p, 1)
        if stage < 5:
            return

        def norm_rows(k, i):
            n = TILES[i][1]
            x = X[0:n, i, :]
            V_.bn_stats(STATS[0:n, 0:6], X[0:n, i, 0:512])
            link(V_.bn_stats(STATS[0:n, 6:12], X[0:n, i, 512:D]))
            link(V_.bn_aggr(MV[0:n, i, :], STATS[0:n, :]))
            V_.tensor_scalar(VE[0:n, i:i + 1], MV[0:n, i, 1:2], EPS, None, ALU.add).then_inc(ln_stat, 1)
            dve.wait_ge(ln_rstd, 3 * k + i + 1)
            link(V_.tensor_scalar(x, x, MV[0:n, i, 0:1], RSTD[0:n, i:i + 1], ALU.subtract, ALU.mult))
            dve.wait_ge(ld_ln, 32 * (k + 1))
            link(V_.tensor_tensor(x, x, LNP[0:n, 0, :], ALU.mult))
            V_.tensor_tensor(x, x, LNP[0:n, 1, :], ALU.add).then_inc(ln_done, 1)

        def mixed(k, first):
            for i, (_, n) in enumerate(TILES):
                dve.wait_ge(op_psum, first + i + 1)
                for half in range(2):
                    x = X[0:n, i, 512 * half:512 * half + 512]
                    link(V_.scalar_tensor_tensor(x, x, ALPHA, bank[2 * i + half][0:n, :], ALU.mult, ALU.add))
                norm_rows(k, i)

        def route(layer):
            link(V_.memset(L8, NEG))
            link(V_.memset(RK, 0.0))
            link(V_.memset(EF, 0.0))
            dve.wait_ge(ld_small, 8 * 16)
            for i, (_, n) in enumerate(TILES):
                m = 3 * layer + i
                dve.wait_ge(ro_psum, m + 1)
                link(V_.tensor_tensor(LG[0:n, :], bank[4 + i][0:n, 0:NG + NE], RBI[0:n, layer, :], ALU.add))
                link(V_.tensor_copy(L8[0:n, 0:NG], LG[0:n, 0:NG]))
                link(V_.max(TOP8[0:n, :], L8[0:n, :]))
                link(V_.max_index(GIX[0:n, :].bitcast(U32), TOP8[0:n, :], L8[0:n, :]))
                V_.tensor_scalar(GT[0:n, 0:1], TOP8[0:n, 0:1], -1.0, None, ALU.mult).then_inc(ro_top, 1)
                link(V_.tensor_copy(GT[0:n, 2:3], GIX[0:n, 0:1].bitcast(U32)))
                link(V_.tensor_scalar(PEN[0:n, :], IOTA[0:n, 0:NG], GT[0:n, 2:3], None, ALU.is_equal))
                link(V_.tensor_scalar(PEN[0:n, :], PEN[0:n, :], -1.0, -NEG, ALU.add, ALU.mult))
                le = LG[0:n, NG:NG + NE]
                link(V_.tensor_tensor(le.rearrange("p (g e) -> p g e", g=NG), le.rearrange("p (g e) -> p g e", g=NG),
                                      PEN[0:n, :].unsqueeze(2).to_broadcast([n, NG, EPG]), ALU.add))
                link(V_.max(TOP8[0:n, :], le))
                link(V_.max_index(EIX[0:n, :].bitcast(U32), TOP8[0:n, :], le))
                V_.tensor_scalar(GT[0:n, 1:2], TOP8[0:n, 0:1], -1.0, None, ALU.mult).then_inc(ro_top, 1)
                link(V_.tensor_copy(EF[0:n, 2 * i:2 * i + 2], EIX[0:n, 0:2].bitcast(U32)))
                for k in range(2):
                    link(V_.tensor_scalar(HOTK[0:n, 2 * i + k, :], IOTA[0:n, :], EF[0:n, 2 * i + k:2 * i + k + 1], None, ALU.is_equal))
                V_.tensor_tensor(HOT[0:n, i, :], HOTK[0:n, 2 * i, :], HOTK[0:n, 2 * i + 1, :], ALU.add).then_inc(ro_hot, 1)
                dve.wait_ge(ro_exp, 2 * m + 2)
                link(V_.tensor_scalar(DEN[0:n, i:i + 1], RR[0:n, i:i + 1], 1.0, GSUM[0:n, i:i + 1], ALU.add, ALU.mult))
                link(V_.reciprocal(GATE[0:n, 2 * i:2 * i + 1], DEN[0:n, i:i + 1]))
                link(V_.tensor_tensor(GATE[0:n, 2 * i + 1:2 * i + 2], GATE[0:n, 2 * i:2 * i + 1], RR[0:n, i:i + 1], ALU.mult))
            dve.wait_ge(ro_rank, 4 * layer + 4)
            for i, (_, n) in enumerate(TILES):
                for k in range(2):
                    link(V_.tensor_tensor(RANKT[0:n, :], bank[7][0:n, 32 * i:32 * i + 32], HOTK[0:n, 2 * i + k, :], ALU.mult))
                    link(V_.tensor_reduce(RK[0:n, 2 * i + k:2 * i + k + 1], RANKT[0:n, :], AX.X, ALU.add))
            link(V_.scalar_tensor_tensor(SLOTF, EF, float(CAP), RK, ALU.mult, ALU.add))
            for r in range(1, PASSES):
                link(V_.tensor_scalar(QQ, RK, float(r * CAP), float(NE * CAP - CAP), ALU.is_ge, ALU.mult))
                link(V_.tensor_tensor(SLOTF, SLOTF, QQ, ALU.add))
            link(V_.tensor_copy(SLOTI.bitcast(I32), SLOTF))
            link(V_.tensor_scalar(QQ, RK, float(CAP), -float(SLOTS + NE * CAP), ALU.is_lt, ALU.mult))
            link(V_.tensor_scalar(QQ, QQ, -1.0, -float(NE * CAP), ALU.mult, ALU.add))
            link(V_.tensor_tensor(SLOTF, SLOTF, QQ, ALU.add))
            V_.tensor_copy(SLOTM.bitcast(I32), SLOTF).then_inc(ro_slot, 1)
            link(V_.tensor_reduce(GT[0:1, 3:4], bank[7][0:1, 96:128], AX.X, ALU.max))
            link(V_.tensor_scalar(GT[0:1, 4:5], GT[0:1, 3:4], float(CAP), None, ALU.is_gt))
            V_.tensor_copy(FLAG[0:1, layer:layer + 1].bitcast(I32), GT[0:1, 4:5]).then_inc(ro_slot, 1)
            dve.wait_ge(ld_tok, 16 * (layer + 1))
            V_.tensor_copy(TKF[0:NE // 2, :], TKI[0:NE // 2, :].bitcast(I32)).then_inc(tok_f, 1)
            dve.wait_ge(tok_T, layer + 1)
            V_.tensor_copy(IDXI[0:2 * CAP, :].bitcast(I32), bank[6][0:2 * CAP, 0:NE // 2]).then_inc(tok_idx, 1)

        def experts(layer):
            base = NE * layer

            def hidden(i, u):
                E, k = base + number(i, u), u % 2
                dve.wait_ge(silu_done, E + 1)
                h = HID[CAP:2 * CAP, k, :]
                V_.tensor_tensor(h, h, bank[2 + k][CAP:2 * CAP, :], ALU.mult).then_inc(h_done, 1)
                dve.wait_ge(ht_T, E + 1)
                wait(dve, dn_psum, E - 1)
                V_.tensor_copy(HT[:, k, :, :], bank[4 + k][:, 0:FC * CAP].rearrange("p (f n) -> p f n", f=FC)).then_inc(ht_evac, 1)

            for u in range(6):
                hidden(0, u)
            with dve.Fori(1, NE // 6) as i:
                for u in range(6):
                    hidden(i, u)
            for u in range(NE % 6):
                hidden(NE // 6, u)
            s = more[layer]
            full = dve.value_load(FLAG[0:1, layer:layer + 1].bitcast(I32), min_val=0, max_val=1)
            with dve.If(full > 0):
                with dve.Fori(1, PASSES) as r:
                    with dve.Fori(0, NE) as e:
                        n = (r - 1) * NE + e
                        dve.wait_ge(s["silu"], n + 1)
                        V_.tensor_tensor(HID[CAP:2 * CAP, 0, :], HID[CAP:2 * CAP, 0, :], bank[2][CAP:2 * CAP, :], ALU.mult).then_inc(s["h"], 1)
                        dve.wait_ge(s["hT"], n + 1)
                        V_.tensor_copy(HT[:, 0, :, :], bank[4][:, 0:FC * CAP].rearrange("p (f n) -> p f n", f=FC)).then_inc(s["hTe"], 1)
                dve.wait_ge(s["st"], 16 * n_more)
            with dve.Else():
                dve.nop()
            for i, (_, n) in enumerate(TILES):
                x, y0, y1 = X[0:n, i, :], YG[0:n, 0, :], YG[0:n, 1, :]
                done = 6 * layer + 2 * i
                dve.wait_ge(ygath[0], 16 * (3 * layer + i + 1))
                link(V_.tensor_scalar(y0, y0, GATE[0:n, 2 * i:2 * i + 1], None, ALU.mult))
                dve.wait_ge(ygath[1], 16 * (3 * layer + i + 1))
                V_.scalar_tensor_tensor(y1, y1, GATE[0:n, 2 * i + 1:2 * i + 2], y0, ALU.mult, ALU.add).then_inc(y_used, 1)
                dve.wait_ge(y_used, done + 1)
                V_.scalar_tensor_tensor(x, x, ALPHA, y1, ALU.mult, ALU.add).then_inc(y_used, 1)
                dve.wait_ge(y_used, done + 2)
                norm_rows(2 * layer + 1, i)

        mixed(0, 0)
        if stage < 6:
            return
        route(0)
        experts(0)
        if stage < 8:
            return
        for k in range(2):
            link(V_.memset(UB[:, k, 0:2], 0.0))
        dve.wait_ge(cv_in, 1)
        for j in range(DC):
            k = j % 2
            up, us = UB[:, k, 0:SEQ + 2], UB[:, k, SEQ + 2:].rearrange("p (b w) -> p b w", b=DEC_B)
            cp, cs = CB[:, k, 0:SEQ], CB[:, k, SEQ:NTOK].rearrange("p (b q) -> p b q", b=DEC_B)
            gate_c = bank[3 * k + 2]
            V_.tensor_copy(us[:, :, 0:2], SCT[:, j, 0:16].rearrange("p (b w) -> p b w", b=DEC_B))
            dve.wait_ge(cv_h, j + 1)
            dve.wait_ge(cv_psum, 3 * j + 3)
            V_.tensor_tensor(up[:, 2:], HSB[:, k, 0:SEQ], gate_c[:, 0:SEQ], ALU.mult)
            V_.tensor_tensor(us[:, :, 2:6], HSB[:, k, SEQ:NTOK].rearrange("p (b q) -> p b q", b=DEC_B),
                             gate_c[:, SEQ:NTOK].rearrange("p (b q) -> p b q", b=DEC_B), ALU.mult).then_inc(cv_u, 1)
            dve.wait_ge(cv_u, j + 1)
            w = [SCT[:, j, 16 + i:17 + i] for i in range(3)]
            V_.tensor_copy(UL[:, j, 0:2], up[:, SEQ:SEQ + 2])
            V_.tensor_copy(UL[:, j, 2:18].rearrange("p (b w) -> p b w", b=DEC_B), us[:, :, 4:6])
            link(V_.tensor_scalar(cp, up[:, 0:SEQ], w[0], None, ALU.mult))
            link(V_.tensor_scalar(cs, us[:, :, 0:4], w[0], None, ALU.mult))
            for i in (1, 2):
                link(V_.scalar_tensor_tensor(cp, up[:, i:i + SEQ], w[i], cp, ALU.mult, ALU.add))
                link(V_.scalar_tensor_tensor(cs, us[:, :, i:i + 4], w[i], cs, ALU.mult, ALU.add))
            V_.tensor_tensor(ZT[:, j, :], CB[:, k, :], bank[3 * k + 1][:, 0:NTOK], ALU.mult).then_inc(cv_z, 1)
        mixed(2, 3)
        route(1)
        experts(1)

    @block.tensor
    def _(pe):
        mm = nc.tensor.matmul

        def tr(out, in_, n):
            return nc.tensor.transpose(out, in_, ID[0:n, 0:n] if n is not None else ID[CAP:2 * CAP, CAP:2 * CAP])

        pe.wait_ge(ld_const, 32)
        pe.wait_ge(ld_rb, 16)
        mm(bank[7][0:17, 0:TABLE_W], RB[0:33, :], OH[0:33, :], start=True, stop=True).then_inc(tab_psum, 1)

        def transpose_x(k):
            for c in range(DC):
                wait(pe, xT_evac, DC * k + c - 3)
                for lo, n in TILES:
                    last = tr(bank[c % 4][:, lo:lo + n], X[0:n, lo // 128, 128 * c:128 * c + 128], n)
                last.then_inc(xT_psum, 1)

        pe.wait_ge(ld_x, 32)
        transpose_x(0)
        pe.wait_ge(xT_evac, DC)
        pe.wait_ge(tab_sb, 1)
        for g, (load, lo, n, chunk, tile, _) in enumerate(PROJ):
            if g == 0 or PROJ[g - 1][0] != load:
                pe.wait_ge(ld_win[load % 3], 16 * (load // 3 + 1))
            wait(pe, proj_evac, g - 3)
            w = WIN[load % 3][:, :, lo:lo + n]
            out = bank[4 + g % 4]
            for c in range(DC):
                if chunk is None:
                    tok, rows = TILES[tile]
                    last = mm(out[0:rows, 0:n], XT[:, c, tok:tok + rows], w[:, c, :], start=c == 0, stop=c == DC - 1)
                else:
                    last = mm(out[0:n, 0:NTOK], w[:, c, :], XT[:, c, :], start=c == 0, stop=c == DC - 1)
            last.then_inc(proj_psum, 1)
        pe.wait_ge(proj_evac, len(PROJ))
        for g in range(6):
            (lo, n), part = TILES[g // 2], g % 2
            wait(pe, ktok_evac, g - 3)
            out = bank[g % 4]
            if part == 0:
                for c in range(4):
                    last = tr(out[0:n, 128 * c:128 * c + 128], QKVT[:, KA + c, lo:lo + n], 128)
            else:
                tr(out[0:n, 0:128], QKVT[:, KB, lo:lo + n], 128)
                last = tr(out[0:n, 128:192], QKVT[0:64, KI, lo:lo + n], 64)
            last.then_inc(ktok_psum, 1)
        pe.wait_ge(ktok_evac, 6)
        for i in range(2 * HI):
            qt, h = i // HI, i % HI
            p, n = 64 * (h % 2), 128 * (qt + 1)
            wait(pe, idx_relu, i - 1)
            mm(bank[i % 2][:, 0:n], QKVT[p:p + 64, QI + h // 2, 128 * qt:128 * qt + 128], QKVT[p:p + 64, KI, 0:n],
               start=True, stop=True).then_inc(idx_psum, 1)
        pe.wait_ge(idx_relu, 2 * HI)

        def scores(u):
            h, qt = u // 2, u % 2
            n, p = 128 * (qt + 1), 64 * (h % 2)
            if h < HA:
                q, k = QA + h // 2, KA + h // 2
            else:
                b = h - HA
                q, k = QB + b // 2, KB if b % 2 == b // (HB // KVB) else KBS
            wait(pe, att_scored, u - NSB + 1)
            mm(bank[S_BANKS[u % NSB]][:, 0:n], QKVT[p:p + 64, q, 128 * qt:128 * qt + 128], QKVT[p:p + 64, k, 0:n],
               start=True, stop=True).then_inc(att_S, 1)

        def transpose_p(u):
            pe.wait_ge(att_p, u + 1)
            wait(pe, att_Tevac, u - 1)
            for kt in range(u % 2 + 1):
                last = tr(bank[2 + u % 2][:, 128 * kt:128 * kt + 128], PB[:, u % NP, 128 * kt:128 * kt + 128], 128)
            last.then_inc(att_T, 1)

        def values(u):
            h, qt = u // 2, u % 2
            pe.wait_ge(att_Tevac, u + 1)
            if u % 4 == 0:
                wait(pe, att_Oevac, u // 4 - 1)
            col = 64 * h if h < HA else 512 + 64 * ((h - HA) // (HB // KVB))
            out = bank[4 + (h // 2) % 2][64 * (h % 2):64 * (h % 2) + 64, 128 * qt:128 * qt + 128]
            for kt in range(qt + 1):
                last = mm(out, V[:, kt, col:col + 64], PTB[:, u % 2, kt, :], start=kt == 0, stop=kt == qt)
            last.then_inc(att_O, 1)

        for u in range(AHEAD):
            scores(u)
        for u in range(2 * HEADS):
            if u + AHEAD < 2 * HEADS:
                scores(u + AHEAD)
            transpose_p(u)
            if u >= 1:
                values(u - 1)
        values(2 * HEADS - 1)
        if stage < 4:
            return
        pe.wait_ge(att_Oevac, HEADS // 2)
        for g in range(2):
            last = mm(bank[7][:, 8 * g:8 * g + 8], REP[0:NS, 128 * g:128 * g + 128], V[0:NS, 2, 640:648], start=True, stop=True)
        last.then_inc(w_psum, 1)
        pe.wait_ge(q_cut, 1)
        for b in range(DEC_B):
            pe.wait_ge(ld_k[b % 2], 16 * 6 * (b // 2 + 1))
            for j in range(3):
                g = 3 * b + j
                wait(pe, kt_evac, g - 3)
                if j < 2:
                    for c in range(4):
                        last = tr(bank[g % 4][:, 128 * c:128 * c + 128], KRAW[b % 2][:, j, 128 * c:128 * c + 128], 128)
                else:
                    for pg in range(N_PAGES):
                        tr(bank[g % 4][:, 128 * pg:128 * pg + 128], KRAW[b % 2][:, pg, 512:640], 128)
                        last = tr(bank[g % 4][0:64, 256 + 128 * pg:384 + 128 * pg], KRAW[b % 2][:, pg, 640:704], 128)
                last.then_inc(kt_psum, 1)
            pe.wait_ge(kt_evac, 3 * b + 3)
            pe.wait_ge(k_new, b + 1)
            if b == 4:
                pe.wait_ge(smp_Sevac, 1)
                pe.wait_ge(smp_relu, 1)
            rows = slice(32 * (b % 4), 32 * (b % 4) + 32)
            for c in range(4):
                mm(bank[4][rows, 0:NK_S], QAS[:, c, b, :], KTB[b % 2][:, c, :], start=c == 0, stop=c == 3)
            mm(bank[5][rows, 0:NK_S], QBS[:, b, :], KTB[b % 2][:, 4, :], start=True, stop=True)
            mm(bank[6][rows, 0:NK_S], QIS[0:64, b, :], KTB[b % 2][0:64, 5, :], start=True, stop=True).then_inc(smp_S, 1)
        pe.wait_ge(smp_relu, 2)
        pe.wait_ge(w_mat, 2)
        for g in range(2):
            last = mm(bank[7][0:NS, 0:NK_S], WM[:, g, :], RIS[g], start=g == 0, stop=g == 1)
        last.then_inc(sc_psum, 1)
        pe.wait_ge(sc_mask, 1)
        for g in range(2):
            mm(bank[g][:, 0:NK_S], REP[0:NS, 128 * g:128 * g + 128], SMASK[0:NS, :], start=True, stop=True).then_inc(rep_psum, 1)
        pe.wait_ge(smp_scored, 4)
        for j in range(4):
            pe.wait_ge(smp_p, j + 1)
            for kt in range(2):
                tr(bank[j][:, 128 * kt:128 * kt + 128], PS4[:, j, 128 * kt:128 * kt + 128], 128)
            tr(bank[j][0:NS, 256:384], PN[:, j, :], 128).then_inc(smp_T, 1)
        pe.wait_ge(smp_Tevac, 4)
        for b in range(DEC_B):
            g, r0 = b // 4, 32 * (b % 4)
            pe.wait_ge(ld_v[b % 4], 16 * 4 * (b // 4 + 1))
            for c in range(4):
                out = bank[4][:, 32 * b + 8 * c:32 * b + 8 * c + 8]
                for kt in range(3):
                    v = VRAW[b % 4][:, kt, 128 * c:128 * c + 128] if kt < 2 else V[0:NS, 2, 128 * c:128 * c + 128]
                    p = PT[:, g, kt, r0 + 8 * c:r0 + 8 * c + 8] if kt < 2 else PT[0:NS, g, 2, r0 + 8 * c:r0 + 8 * c + 8]
                    mm(out, v, p, start=kt == 0, stop=kt == 2)
            for kv in range(2):
                for odd in range(2):
                    out = bank[5][64 * odd:64 * odd + 64, 16 * b + 8 * kv:16 * b + 8 * kv + 8].rearrange("p (i q) -> p i q", i=2)
                    for kt in range(3):
                        k_rows = 128 if kt < 2 else NS
                        v = (VRAW[b % 4][:, kt, 512 + 64 * kv:576 + 64 * kv] if kt < 2
                             else V[0:NS, 2, 512 + 64 * kv:576 + 64 * kv])
                        p = PT[0:k_rows, 2 + g, kt, r0 + 16 * kv:r0 + 16 * kv + 16].rearrange("p (i o q) -> p i o q", i=2, o=2)[:, :, odd, :]
                        last = mm(out, v, p, start=kt == 0, stop=kt == 2)
            last.then_inc(smp_O, 1)
        if stage < 5:
            return

        def project(feat, w):
            for i, (lo, n) in enumerate(TILES):
                for half in range(2):
                    for c in range(DC):
                        last = mm(bank[2 * i + half][0:n, :], feat[:, c, lo:lo + n], w[:, c, 512 * half:512 * half + 512],
                                  start=c == 0, stop=c == DC - 1)
                last.then_inc(op_psum, 1)

        def route(layer):
            k = 2 * layer + 1
            pe.wait_ge(ln_done, 6 * layer + 3)
            transpose_x(k)
            pe.wait_ge(xT_evac, DC * (k + 1))
            pe.wait_ge(ld_small, 8 * 16)
            for i, (lo, n) in enumerate(TILES):
                for c in range(DC):
                    last = mm(bank[4 + i][0:n, 0:NG + NE], XT[:, c, lo:lo + n], WR[:, layer, c, :], start=c == 0, stop=c == DC - 1)
                last.then_inc(ro_psum, 1)
            for i, (_, n) in enumerate(TILES):
                pe.wait_ge(ro_hot, 3 * layer + i + 1)
                for j in range(i):
                    mm(bank[7][0:n, 32 * i:32 * i + 32], ONE[:, 0:n], HOT[:, j, :], start=j == 0, stop=False)
                mm(bank[7][0:n, 32 * i:32 * i + 32], TRI[0:n, 0:n], HOT[0:n, i, :], start=i == 0, stop=True).then_inc(ro_rank, 1)
            for i, (_, n) in enumerate(TILES):
                last = mm(bank[7][0:1, 96:128], ONE[0:n, 0:1], HOT[0:n, i, :], start=i == 0, stop=i == 2)
            last.then_inc(ro_rank, 1)
            pe.wait_ge(tok_f, layer + 1)
            tr(bank[6][0:2 * CAP, 0:NE // 2], TKF[0:NE // 2, :], NE // 2).then_inc(tok_T, 1)
            pe.wait_ge(tok_idx, layer + 1)

        def experts(layer):
            base = NE * layer

            def transpose_rows(x, n, outs):
                per = DC // len(outs)
                for c in range(DC):
                    last = tr(outs[c // per][:, n * (c % per):n * (c % per) + n], x.rearrange("n (p c) -> n p c", c=DC)[:, :, c], n)
                return last

            def gate_up(x, wg, wu, out, up_ready=None):
                for c in range(DC):
                    mm(out[0:CAP, :], x[:, c, :], wg[:, c, :], start=c == 0, stop=c == DC - 1)
                    if c == 0 and up_ready is not None:
                        pe.wait_ge(*up_ready)
                    last = mm(out[CAP:2 * CAP, :], x[:, c, :], wu[:, c, :], start=c == 0, stop=c == DC - 1)
                return last

            def transpose_h(h, out):
                for f in range(FC):
                    last = tr(out[:, CAP * f:CAP * f + CAP], h[:, 128 * f:128 * f + 128], None)
                return last

            def down(h, wd, out):
                for f in range(FC):
                    for half in range(2):
                        last = mm(out[CAP * half:CAP * half + CAP, :], h[:, f, :], wd[:, f, 512 * half:512 * half + 512],
                                  start=f == 0, stop=f == FC - 1)
                return last

            def gathered(i, v):
                Q = base // 2 + 3 * i + v
                pe.wait_ge(gath[v], gather_count(layer, i, v))
                wait(pe, xg_evac, Q)
                pe.sem_inc(pe_passed, 1)
                transpose_rows(XG[0:2 * CAP, v, :], 2 * CAP, (bank[0], bank[1])).then_inc(xg_T, 1)

            def output(i, u):
                E, k, s = base + number(i, u), u % 2, slot_of(layer, u)
                pe.wait_ge(ht_evac, E + 1)
                wait(pe, y_evac, E - 1)
                pe.wait_ge(ld_wd[s], slot_loads(layer, i, u))
                down(HT[:, k, :, :], WD[s], bank[6 + k]).then_inc(dn_psum, 1)

            def step(i, u, before, nxt):
                E, k, s, v = base + number(i, u), u % 2, slot_of(layer, u), u // 2
                pe.wait_ge(xg_evac, base // 2 + 3 * i + v + 1)
                wait(pe, h_done, E - 1)
                pe.wait_ge(ld_wg[s], slot_loads(layer, i, u))
                gate_up(XGT[v][:, :, CAP * k:CAP * k + CAP], WG[s], WU[s], bank[2 + k],
                        (ld_wu[s], slot_loads(layer, i, u))).then_inc(gu_psum, 1)
                if before is not None:
                    output(*before)
                pe.wait_ge(h_done, E + 1)
                wait(pe, ht_evac, E - 1)
                pe.sem_inc(pe_passed, 1)
                transpose_h(HID[CAP:2 * CAP, k, :], bank[4 + k]).then_inc(ht_T, 1)
                if nxt is not None:
                    gathered(*nxt)

            gathered(0, 0)
            for u in range(6):
                step(0, u, (0, u - 1) if u else None, (0, u // 2 + 1) if u in (0, 2) else (1, 0) if u == 4 else None)
            with pe.Fori(1, NE // 6) as i:
                for u in range(6):
                    step(i, u, (i, u - 1) if u else (i - 1, 5), (i, u // 2 + 1) if u in (0, 2) else (i + 1, 0) if u == 4 else None)
            for u in range(NE % 6):
                step(NE // 6, u, (NE // 6, u - 1) if u else (NE // 6 - 1, 5), None)
            output(NE // 6, NE % 6 - 1)
            s = more[layer]
            full = pe.value_load(FLAG[0:1, layer:layer + 1].bitcast(I32), min_val=0, max_val=1)
            pe.wait_ge(y_evac, base + NE)
            with pe.If(full > 0):
                with pe.Fori(1, PASSES) as r:
                    with pe.Fori(0, NE) as e:
                        n = (r - 1) * NE + e
                        pe.wait_ge(s["gath"], 16 * (n + 1))
                        pe.sem_inc(pe_passed, 1)
                        transpose_rows(XG[0:CAP, 0, :], CAP, (bank[0],)).then_inc(s["T"], 1)
                        pe.wait_ge(s["Tevac"], n + 1)
                        pe.wait_ge(s["w"], 48 * (n + 1))
                        gate_up(XGT[0][:, :, 0:CAP], WG[0], WU[0], bank[2]).then_inc(s["gu"], 1)
                        pe.wait_ge(s["h"], n + 1)
                        pe.sem_inc(pe_passed, 1)
                        transpose_h(HID[CAP:2 * CAP, 0, :], bank[4]).then_inc(s["hT"], 1)
                        pe.wait_ge(s["hTe"], n + 1)
                        pe.wait_ge(s["y"], n)
                        down(HT[:, 0, :, :], WD[0], bank[6]).then_inc(s["dn"], 1)
                pe.wait_ge(s["st"], 16 * n_more)
            with pe.Else():
                pe.nop()

        pe.wait_ge(smp_y, 1)
        pe.wait_ge(ld_wout, 16)
        project(YT, WOUT)
        if stage < 6:
            return
        route(0)
        experts(0)
        if stage < 8:
            return
        pe.wait_ge(ln_done, 6)
        transpose_x(2)
        pe.wait_ge(ld_state, 32)
        for c in range(DC):
            last = tr(bank[6][:, 19 * c:19 * c + 19], SCW[0:19, 128 * c:128 * c + 128], 19)
        last.then_inc(cv_in_T, 1)
        pe.wait_ge(xT_evac, 3 * DC)
        for j in range(DC):
            half = j // 4
            if j % 4 == 0:
                pe.wait_ge(ld_wc[half], 48)
            wait(pe, cv_z, j - 1)
            for part in range(3):
                w = WC[3 * half + part]
                for c in range(DC):
                    last = mm(bank[3 * (j % 2) + part][:, 0:NTOK], w[:, c, 128 * (j % 4):128 * (j % 4) + 128], XT[:, c, :],
                              start=c == 0, stop=c == DC - 1)
                last.then_inc(cv_psum, 1)
        pe.wait_ge(cv_z, DC)
        pe.wait_ge(cv_in, 1)
        for c in range(DC):
            last = tr(bank[6 + c // 4][0:18, 128 * (c % 4):128 * (c % 4) + 128], UL[:, c, :], 128)
        last.then_inc(cv_lT, 1)
        pe.wait_ge(ld_wco, 16)
        project(ZT, WCO)
        route(1)
        experts(1)


_INS = ["x_prompt", "x_sample", "cache_k_a", "cache_v_a", "cache_k_b", "cache_v_b", "cache_k_idx", "state_conv", "page_table",
        "rel_bias", "w_attn_in", "w_attn_out", "w_conv_in", "conv_w", "w_conv_out", "w_router_group", "b_router_group",
        "w_router_expert", "b_router_expert", "w_exp_gate", "w_exp_up", "w_exp_down", "ln_g", "ln_b"]
_OUTS = [("y_prompt", (1, SEQ, D)), ("y_sample", (DEC_B, DEC_T, D)),
         ("new_k_a_prompt", (1, 1, SEQ, HA, HD)), ("new_v_a_prompt", (1, 1, SEQ, HA, HD)),
         ("new_k_b_prompt", (1, 1, SEQ, KVB, HD)), ("new_v_b_prompt", (1, 1, SEQ, KVB, HD)),
         ("new_k_idx_prompt", (1, 1, SEQ, HD)), ("new_conv_prompt", (1, 1, 2, D)),
         ("new_k_a_sample", (1, DEC_B, DEC_T, HA, HD)), ("new_v_a_sample", (1, DEC_B, DEC_T, HA, HD)),
         ("new_k_b_sample", (1, DEC_B, DEC_T, KVB, HD)), ("new_v_b_sample", (1, DEC_B, DEC_T, KVB, HD)),
         ("new_k_idx_sample", (1, DEC_B, DEC_T, HD)), ("new_conv_sample", (1, DEC_B, 2, D))]


def kernel(**inputs):
    import concourse.bacc as bacc
    from concourse.bass_utils import run_bass_kernel_spmd as run

    nc = bacc.Bacc("TRN2", target_bir_lowering=False, num_devices=1)
    arrays, t = {}, {}
    arrays["consts"] = constants()
    for name in _INS:
        arrays[name] = np.ascontiguousarray(inputs[name])
    for name, a in arrays.items():
        t[name] = nc.dram_tensor(name, a.shape, mybir.dt.from_np(a.dtype), kind="ExternalInput").ap()
    for name, shape in _OUTS:
        t[name] = nc.dram_tensor(name, shape, F32, kind="ExternalOutput").ap()
    build(nc, t)
    r = run(nc, [arrays], core_ids=[0])
    return tuple(r.results[0][name] for name, _ in _OUTS)
```

```python
import math
from contextlib import ExitStack

import numpy as np
import concourse.bass as bass
from concourse import mybir

F32 = mybir.dt.float32
I32 = mybir.dt.int32
U32 = mybir.dt.uint32
ALU = mybir.AluOpType
ACT = mybir.ActivationFunctionType
AX = mybir.AxisListType

D = 1024
DC = D // 128
SEQ = 256
DEC_B, DEC_T = 8, 4
NS = DEC_B * DEC_T
NTOK = SEQ + NS
TILES = [(0, 128), (128, 128), (256, NS)]
STEPS = (0, 2, 1)
DEPTH = 2
ALPHA = (2 * DEPTH) ** 0.25
EPS = 1e-5
PAST, PAGE = 256, 128
N_PAGES = PAST // PAGE
NK_S = PAST + DEC_T
HD, HA, HB, KVB, HI = 64, 8, 8, 2, 8
HEADS = HA + HB
TOPK_P = 64
TOPK_S = 65
ROUNDS_P = TOPK_P // 8
ROUNDS_S = -(-TOPK_S // 8)
PADS_S = ROUNDS_S * 8 - TOPK_S
IDX_SCALE = 1.0 / math.sqrt(64 * HI)
QK_SCALE = 1.0 / math.sqrt(HD)
NEG, TAKEN = -1e30, -3e38
NE, NG, EPG, FE = 32, 4, 8, 512
FC = FE // 128
CAP = 64
PASSES = -(-NTOK // CAP)
SLOTS = PASSES * NE * CAP
DIST0 = PAST + DEC_T - 1
TABLE_W = 388
W_BLOCKS = [(0, 512), (512, 512), (1024, 512), (1536, 512), (2048, 256), (2304, 512), (2816, 72)]
QA, KA, QB, KB, QI, KI, KBS = 0, 4, 8, 12, 13, 17, 18
PROJ = ([(0, 128 * c, 128, QA + c, None, None) for c in range(4)]
        + [(1, 128 * c, 128, KA + c, None, None) for c in range(4)]
        + [(2, 0, 512, None, t, 0) for t in range(3)]
        + [(3, 128 * c, 128, QB + c, None, None) for c in range(4)]
        + [(4, 0, 128, KB, None, None)] + [(4, 128, 128, None, t, 512) for t in range(3)]
        + [(5, 128 * c, 128, QI + c, None, None) for c in range(4)]
        + [(6, 0, 64, KI, None, None)] + [(6, 64, 8, None, t, 640) for t in range(3)])
PROJ_END = [sum(1 for p in PROJ if p[0] <= k) for k in range(len(W_BLOCKS))]
C_ID, C_TRI, C_ONE, C_IOTA, C_STAY = 0, 128, 256, 384, 512
C_REP, C_PAT, C_HM, C_NEW, C_OH = 512, 768, 832, 840, 904
C_END = C_OH + TABLE_W


def constants():
    c = np.zeros((128, C_END), np.float32)
    i = np.arange(128)
    c[:, C_ID:C_ID + 128] = np.eye(128)
    c[:, C_TRI:C_TRI + 128] = i[:, None] < i[None, :]
    c[:, C_ONE:C_ONE + 128] = 1.0
    b, h, q = i // 32, (i // 4) % 8, i % 4
    for g in range(2):
        tok = (4 * g + b) * DEC_T + q
        c[tok, C_REP + 128 * g + i] = 1.0
        c[i, C_PAT + 32 * g + tok] = 1.0
        for j in range(DEC_T):
            c[i, C_NEW + 32 * g + (4 * g + b) * DEC_T + j] = 1.0
    c[i, C_HM + h] = 1.0
    c[:, C_IOTA:C_IOTA + 128] = np.arange(128)
    dist = DIST0 - np.arange(TABLE_W)
    n = np.maximum(dist, 0)
    nf = np.maximum(n, 1).astype(np.float32)
    large = 16 + (np.log(nf / np.float32(16)) / np.float32(math.log(8.0)) * np.float32(16)).astype(np.int32)
    bucket = np.where(n < 16, n, np.minimum(large, 31))
    for k in range(TABLE_W):
        if dist[k] >= 0:
            c[bucket[k], C_OH + k] = 1.0 / QK_SCALE
        else:
            c[32, C_OH + k] = 1.0
    return c


def build(nc, t):
    with ExitStack() as ctx:
        build_in(nc, t, ctx)


def build_in(nc, t, ctx):
    def sem(name):
        return ctx.enter_context(nc.semaphore(name))

    TOTAL = 53200
    mem = ctx.enter_context(nc.sbuf_tensor("mem", [128, TOTAL], F32))

    def region(lo, hi):
        at = [lo]

        def take(*dims):
            n = int(np.prod(dims))
            a = mem[:, at[0]:at[0] + n]
            at[0] += n + n % 2
            assert at[0] <= hi, (lo, hi, at[0])
            names = "abcd"[:len(dims)]
            if len(dims) > 1:
                sizes = {x: d for x, d in zip(names[:-1], dims)}
                a = a.rearrange("p (" + " ".join(names) + ") -> p " + " ".join(names), **sizes)
            return a
        return take

    SLOT = 3 * DC * FE
    S0 = TOTAL - 3 * SLOT
    WORK = 9390
    common = region(0, WORK)
    CST = common(C_STAY)
    X = common(3, D)
    XT = common(DC, NTOK)
    LNP = common(2, D)
    WR = common(DEPTH, DC, NG + NE)
    RBI = common(DEPTH, NG + NE)
    SLOTI, SLOTM, SLOTQ, TOKI, IDXC, FLAG = common(6), common(6), common(6), common(3), common(1), common(2)
    ZERO = common(SLOTS // 128)
    NEGH, L8, GT, GATE, EF, RK, QQ, SLOTF = common(1), common(8), common(6), common(6), common(6), common(6), common(6), common(6)
    TOP8, GIX, EIX, GSUM, RR, DEN = common(8), common(8), common(8), common(3), common(3), common(3)
    HOT, HOTK, LG, PEN, RANKT = common(3, NE), common(6, NE), common(NG + NE), common(NG), common(2, NE)
    STATS, MV, VE, RSTD = common(12), common(3, 2), common(3), common(3)
    XT_BANKS, LG_BANKS, RK_BANKS = (5, 6), (0, 4, 2), (7, 1, 3)
    ID, TRI, ONE = CST[:, C_ID:C_ID + 128], CST[:, C_TRI:C_TRI + 128], CST[:, C_ONE:C_ONE + 128]
    IOTA, IOTA_PAIR = CST[:, C_IOTA:C_IOTA + NE], CST[:, C_IOTA:C_IOTA + 2 * CAP]

    slots = [mem[:, S0 + k * SLOT:S0 + (k + 1) * SLOT] for k in range(3)]
    WG = [s[:, 0:4096].rearrange("p (c f) -> p c f", c=DC) for s in slots]
    WU = [s[:, 4096:8192].rearrange("p (c f) -> p c f", c=DC) for s in slots]
    WD = [s[:, 8192:12288].rearrange("p (c n) -> p c n", c=FC) for s in slots]

    slot0 = region(S0, S0 + SLOT)
    WOUT, V, KTOK = slot0(DC, D), slot0(3, 648), slot0(3, 704)
    att = region(S0 + SLOT, TOTAL)
    WIN = [att(DC, 512) for _ in range(3)]
    att_rest = region(S0 + 2 * SLOT, TOTAL)
    QKVT, BM = att_rest(19, NTOK), att_rest(17, 256)
    PB, COMB = att_rest(5, 256), att_rest(4, 256)
    YT = XT
    sample = region(S0 + SLOT, S0 + SLOT + 3 * 4096)
    KRAW = [sample(N_PAGES, 704) for _ in range(2)]
    KTB = [sample(6, NK_S) for _ in range(2)]
    over_bm = region(S0 + 2 * SLOT + 19 * NTOK, TOTAL)
    VRAW = [sample(N_PAGES, 640) for _ in range(2)] + [over_bm(N_PAGES, 640) for _ in range(4)] + [a[:, :, 0:640] for a in KRAW]
    KRAW.append(over_bm(N_PAGES, 704))
    OM = region(S0 + SLOT + 2 * N_PAGES * 704, S0 + 2 * SLOT)(2, 2, 512)
    QAS, QBS, QIS, PT = sample(4, DEC_B, 32), sample(DEC_B, 32), sample(DEC_B, 32), sample(4, 3, 128)
    RIS = [sample(NK_S) for _ in range(2)]
    work = region(WORK, S0)
    PTB, SELM, ACC, RELU = work(2, 2, 128), work(2, 256), work(2, 256), work(4, 256)
    SBIAS, SMASK, PS4, SCS = work(2, NK_S), work(NK_S), work(4, NK_S), work(NK_S + PADS_S)
    AC = work(C_END - C_STAY)
    TAB, RB = work(TABLE_W), work(17)
    MX, SUM, RIN = work(32), work(32), work(32)
    SMX, SSUM, SRIN, MX8, WVT, WV, WM, PGT, PN = work(4), work(4), work(4), work(8), work(8), work(2), work(2, 32), work(16), work(4, 32)
    REP, PAT, HM, NEW, OH = (AC[:, a - C_STAY:b - C_STAY] for a, b in (
        (C_REP, C_PAT), (C_PAT, C_HM), (C_HM, C_NEW), (C_NEW, C_OH), (C_OH, C_END)))

    moe = region(WORK, S0)
    HID, HT, YO, OHP, XG = moe(2, FE), moe(2, FC, CAP), moe(2, D // 2), moe(3, 3, 2 * CAP), moe(D)
    XT2 = XT.rearrange("p c n -> p (c n)")
    XGT = [a.rearrange("p (c n) -> p c n", c=DC) for a in (XT2[:, 0:DC * 2 * CAP], XT2[:, DC * 2 * CAP:2 * DC * 2 * CAP], moe(DC * 2 * CAP))]
    YG = region(WORK, S0)(4, D)
    WC = [slots[2 * (k // 3)][:, 4096 * (k % 3):4096 * (k % 3 + 1)].rearrange("p (c n) -> p c n", c=DC) for k in range(6)]
    WCO = region(S0 + SLOT, TOTAL)(DC, D)
    ULT = region(S0 + SLOT + 8192, TOTAL)(D)
    cv = region(WORK, S0)
    ZT, UB, HSB, CB = cv(DC, NTOK), cv(2, SEQ + 2 + DEC_B * 6), cv(2, NTOK), cv(2, NTOK)
    behind_yg = region(WORK + 4 * D, S0)
    SCW, SCT, UL = behind_yg(D), behind_yg(DC, 19), behind_yg(DC, 18)

    bank = [ctx.enter_context(nc.psum_tensor(f"bank{i}", [128, 512], F32)) for i in range(8)]

    table_d = nc.dram_tensor("bias_table", [128, 17, TABLE_W], F32).ap()
    xrows_d = [nc.dram_tensor(f"x_rows{i}", [NTOK, D], F32).ap() for i in range(DEPTH)]
    slot_tok_d = [nc.dram_tensor(f"slot_token{i}", [SLOTS, 1], I32).ap() for i in range(DEPTH)]
    yslot_d = [nc.dram_tensor(f"slot_out{i}", [NE * CAP, D], F32).ap() for i in range(DEPTH)]
    ymore_d = [nc.dram_tensor(f"slot_more{i}", [SLOTS - NE * CAP, D], F32).ap() for i in range(DEPTH)]

    ld_const, ld_x, ld_small, ld_rb, ld_ln, ld_pt, ld_wout = (sem("ld_" + n) for n in ("const", "x", "small", "rb", "ln", "pt", "wout"))
    ld_win = [sem(f"ld_win{k}") for k in range(3)]
    st_rows, st_out, st_tab, ld_bias, ld_state = (sem(n) for n in ("st_rows", "st_out", "st_tab", "ld_bias", "ld_state"))
    act_own, dve_own, pool_own = sem("act_own"), sem("dve_own"), sem("pool_own")
    rb_zero, rb_set, tab_psum, tab_sb = (sem(n) for n in ("rb_zero", "rb_set", "tab_psum", "tab_sb"))
    xT_psum, xT_evac, proj_psum, proj_evac = (sem(n) for n in ("xT_psum", "xT_evac", "proj_psum", "proj_evac"))
    ktok_psum, ktok_evac = sem("ktok_psum"), sem("ktok_evac")
    idx_psum, idx_relu, idx_acc, sel_ready, comb_ready = (sem(n) for n in ("idx_psum", "idx_relu", "idx_acc", "sel_ready", "comb_ready"))
    att_S, att_scored, att_exp, att_p, att_T, att_Tevac, att_O, att_Oevac = (
        sem("att_" + n) for n in ("S", "scored", "exp", "p", "T", "Tevac", "O", "Oevac"))
    ld_k = [sem(f"ld_k{k}") for k in range(3)]
    ld_v, ld_v_pool = sem("ld_v"), sem("ld_v_pool")
    kt_psum, kt_evac, k_new, q_zero, q_cut, smp_S, smp_Sevac, smp_relu = (
        sem(n) for n in ("kt_psum", "kt_evac", "k_new", "q_zero", "q_cut", "smp_S", "smp_Sevac", "smp_relu"))
    w_psum, w_mat, sc_psum, sc_mask, rep_psum = (sem(n) for n in ("w_psum", "w_mat", "sc_psum", "sc_mask", "rep_psum"))
    smp_scored, smp_exp, smp_p, smp_T, smp_Tevac, smp_O, smp_cut, smp_yT, smp_y = (
        sem("smp_" + n) for n in ("scored", "exp", "p", "T", "Tevac", "O", "cut", "yT", "y"))
    op_psum, ln_stat, ln_rstd, ln_done = (sem(n) for n in ("op_psum", "ln_stat", "ln_rstd", "ln_done"))
    ro_psum, ro_top, ro_exp, ro_hot, ro_rank, ro_slot = (sem("ro_" + n) for n in ("psum", "top", "exp", "hot", "rank", "slot"))
    st_x, zero_set, st_zero = (sem(n) for n in ("st_x", "zero_set", "st_zero"))
    ld_wg = [sem(f"ld_wg{k}") for k in range(3)]
    ld_wu = [sem(f"ld_wu{k}") for k in range(3)]
    ld_wd = [sem(f"ld_wd{k}") for k in range(3)]
    oh_slot, oh_half, oh_ready, xg_T, xg_evac, gu_psum, silu_done, h_done, ht_T, ht_evac, dn_psum, y_evac = (
        sem(n) for n in ("oh_slot", "oh_half", "oh_ready", "xg_T", "xg_evac", "gu_psum", "silu_done", "h_done", "ht_T", "ht_evac", "dn_psum", "y_evac"))
    st_y = [sem(f"st_y{k}") for k in range(2)]
    ygath = [sem(f"ygath{k}") for k in range(4)]
    y_gated, y_used, pe_passed, pool_passed = sem("y_gated"), sem("y_used"), sem("pe_passed"), sem("pool_passed")
    ld_wc = [sem(f"ld_wc{k}") for k in range(2)]
    cv_in_T, cv_in, cv_psum, cv_h, cv_u, cv_z, cv_lT, cv_lsb = (
        sem("cv_" + n) for n in ("in_T", "in", "psum", "h", "u", "z", "lT", "lsb"))
    more = [{n: sem(f"more{i}_{n}") for n in ("scat", "zero", "w", "tok", "gath", "T", "Tevac", "gu", "silu", "h", "hT", "hTe", "dn", "y", "st", "more")} for i in range(DEPTH)]

    def linker(eng, own):
        n = [0]

        def link(ins):
            n[0] += 1
            ins.then_inc(own, 1)
            eng.wait_ge(own, n[0])
        return link

    def wait(eng, s, value):
        if isinstance(value, int) and value <= 0:
            return
        eng.wait_ge(s, value)

    def number(i, u):
        return 6 * i + u

    ORDER = [(2, 1, 0), (0, 2, 1)]

    def slot_of(layer, u):
        return ORDER[layer][u % 3]

    def slot_loads(layer, i, u):
        before = sum(1 for e in range(layer * NE) if slot_of(0, e) == slot_of(layer, u))
        return 16 * (before + 2 * i + u // 3 + 1)

    def store_count(layer, i, u):
        return 16 * (layer * (NE // 2) + 3 * i + u // 2 + 1)

    def ygath_count(layer, j):
        return 16 * (layer * (2 if j % 4 < 2 else 1) + j // 4 + 1)

    AHEAD, NP, NSB, SELECT = 2, 5, 4, 2
    S_BANKS = (0, 1, 6, 7)
    pages = "l p t h d -> (l p) t (h d)"
    k_caches = [(t["cache_k_a"].rearrange(pages), 0, 512), (t["cache_k_b"].rearrange(pages), 512, 128),
                (t["cache_k_idx"].rearrange("l p t d -> (l p) t d"), 640, 64)]
    v_caches = [(t["cache_v_a"].rearrange(pages), 0, 512), (t["cache_v_b"].rearrange(pages), 512, 128)]
    n_phys = k_caches[0][0].shape[0]

    def load_batch(eng, b, caches, buf, done):
        for pg in range(N_PAGES):
            page = eng.value_load(PGT[0:1, b * N_PAGES + pg:b * N_PAGES + pg + 1].bitcast(I32), min_val=0, max_val=n_phys - 1)
            for cache, lo, n in caches:
                eng.dma_start(buf[:, pg, lo:lo + n], cache[page]).then_inc(done, 16)

    tiled = "(t p) n -> p t n"
    flat = "l b t h d -> (l b t) (h d)"
    n_more = (PASSES - 1) * NE

    block = ctx.enter_context(nc.Block())

    @block.sync
    def _(sp):
        w_in = t["w_attn_in"][0].rearrange("(c p) n -> p c n", p=128)
        sp.dma_start(CST, t["consts"][:, 0:C_STAY]).then_inc(ld_const, 16)
        sp.dma_start(AC, t["consts"][:, C_STAY:C_END]).then_inc(ld_const, 16)
        sp.dma_start(X[:, 0:2, :], t["x_prompt"][0].rearrange("(t p) d -> p t d", p=128)).then_inc(ld_x, 16)
        sp.dma_start(X[0:NS, 2, :], t["x_sample"].rearrange("b t d -> (b t) d")).then_inc(ld_x, 16)
        for k, (lo, n) in enumerate(W_BLOCKS):
            if k >= 3:
                sp.wait_ge(proj_psum, PROJ_END[k - 3])
            sp.dma_start(WIN[k % 3][:, :, 0:n], w_in[:, :, lo:lo + n]).then_inc(ld_win[k % 3], 16)
        sp.dma_start(WOUT, t["w_attn_out"][0].rearrange("(c p) n -> p c n", p=128)).then_inc(ld_wout, 16)

        def load_ln(k):
            sp.dma_start(LNP[:, 0, :], t["ln_g"][k // 2, k % 2].partition_broadcast(128)).then_inc(ld_ln, 16)
            sp.dma_start(LNP[:, 1, :], t["ln_b"][k // 2, k % 2].partition_broadcast(128)).then_inc(ld_ln, 16)

        load_ln(0)
        sp.wait_ge(proj_evac, len(PROJ))
        sp.dma_start(t["new_v_a_prompt"].rearrange(flat).rearrange(tiled, p=128), V[:, 0:2, 0:512]).then_inc(st_rows, 16)
        sp.dma_start(t["new_v_b_prompt"].rearrange(flat).rearrange(tiled, p=128), V[:, 0:2, 512:640]).then_inc(st_rows, 16)
        sp.dma_start(t["new_v_a_sample"].rearrange(flat), V[0:NS, 2, 0:512]).then_inc(st_rows, 16)
        sp.dma_start(t["new_v_b_sample"].rearrange(flat), V[0:NS, 2, 512:640]).then_inc(st_rows, 16)
        sp.wait_ge(ktok_evac, 6)
        sp.dma_start(t["new_k_a_prompt"].rearrange(flat).rearrange(tiled, p=128), KTOK[:, 0:2, 0:512]).then_inc(st_rows, 16)
        sp.dma_start(t["new_k_b_prompt"].rearrange(flat).rearrange(tiled, p=128), KTOK[:, 0:2, 512:640]).then_inc(st_rows, 16)
        sp.dma_start(t["new_k_idx_prompt"].rearrange("l b t d -> (l b t) d").rearrange(tiled, p=128), KTOK[:, 0:2, 640:704]).then_inc(st_rows, 16)
        sp.dma_start(t["new_k_a_sample"].rearrange(flat), KTOK[0:NS, 2, 0:512]).then_inc(st_rows, 16)
        sp.dma_start(t["new_k_b_sample"].rearrange(flat), KTOK[0:NS, 2, 512:640]).then_inc(st_rows, 16)
        sp.dma_start(t["new_k_idx_sample"].rearrange("l b t d -> (l b t) d"), KTOK[0:NS, 2, 640:704]).then_inc(st_rows, 16)
        sp.wait_ge(ld_pt, 16)
        for b in range(DEC_B):
            wait(sp, kt_psum, 3 * (b - 2))
            if b == 2:
                sp.wait_ge(att_Oevac, HEADS // 2)
            load_batch(sp, b, k_caches, KRAW[b % 3], ld_k[b % 3])
            if b < 2:
                load_batch(sp, b, v_caches, VRAW[b], ld_v)
        for b in range(6, DEC_B):
            sp.wait_ge(kt_psum, 3 * (b + 1))
            load_batch(sp, b, v_caches, VRAW[b], ld_v)
        sp.wait_ge(st_rows, 160)

        def load_expert(layer, i, u, free=None):
            e, k = number(i, u), slot_of(layer, u)
            if free is not None:
                wait(sp, gu_psum, free)
            sp.dma_start(WG[k], t["w_exp_gate"][layer, e].rearrange("(p c) f -> p c f", c=DC)).then_inc(ld_wg[k], 16)
            sp.dma_start(WU[k], t["w_exp_up"][layer, e].rearrange("(p c) f -> p c f", c=DC)).then_inc(ld_wu[k], 16)
            if free is not None:
                wait(sp, dn_psum, free)
            sp.dma_start(WD[k], t["w_exp_down"][layer, e].rearrange("(c p) n -> p c n", p=128)).then_inc(ld_wd[k], 16)

        def experts(layer):
            base = NE * layer
            load_expert(layer, 0, 2)
            for j, i in enumerate(STEPS):
                lo, n = TILES[i]
                sp.wait_ge(ln_done, 6 * layer + j + 1)
                sp.dma_start(xrows_d[layer][lo:lo + n], X[0:n, i, :]).then_inc(st_x, 16)
            load_ln(2 * layer + 1)
            for u in (3, 4, 5):
                load_expert(layer, 0, u, base + u - 2)
            with sp.Fori(1, NE // 6) as i:
                for u in range(6):
                    load_expert(layer, i, u, base + number(i, u) - 2)
            for u in range(NE % 6):
                load_expert(layer, NE // 6, u, base + number(NE // 6, u) - 2)
            s = more[layer]
            full = sp.value_load(FLAG[0:1, layer:layer + 1].bitcast(I32), min_val=0, max_val=1)
            with sp.If(full > 0):
                sp.wait_ge(dn_psum, base + NE)
                with sp.Fori(1, PASSES) as r:
                    with sp.Fori(0, NE) as e:
                        sp.wait_ge(s["dn"], (r - 1) * NE + e)
                        sp.dma_start(WG[0], t["w_exp_gate"][layer, e].rearrange("(p c) f -> p c f", c=DC)).then_inc(s["w"], 16)
                        sp.dma_start(WU[0], t["w_exp_up"][layer, e].rearrange("(p c) f -> p c f", c=DC)).then_inc(s["w"], 16)
                        sp.dma_start(WD[0], t["w_exp_down"][layer, e].rearrange("(c p) n -> p c n", p=128)).then_inc(s["w"], 16)
                sp.wait_ge(s["dn"], n_more)
                sp.wait_ge(s["st"], 16 * n_more)
            with sp.Else():
                sp.nop()

        sp.wait_ge(smp_O, 4)
        load_expert(0, 0, 0)
        sp.wait_ge(smp_y, 2)
        load_expert(0, 0, 1)
        sp.wait_ge(op_psum, 3)
        experts(0)
        w_cv = t["w_conv_in"][0].rearrange("(c p) n -> p c n", p=128)

        def load_conv(half, parts=range(3)):
            for part in parts:
                lo = part * D + half * 512
                sp.dma_start(WC[3 * half + part], w_cv[:, :, lo:lo + 512]).then_inc(ld_wc[half], 16)

        sp.wait_ge(gu_psum, NE - 2)
        sp.wait_ge(dn_psum, NE - 2)
        load_conv(0, (0, 1))
        for k in range(4):
            sp.wait_ge(ygath[k], ygath_count(0, k + 4 if k < 2 else k))
        load_conv(0, (2,))
        load_conv(1)
        sp.wait_ge(ln_done, 6)
        load_ln(2)
        sp.dma_start(WCO, t["w_conv_out"][0].rearrange("(c p) n -> p c n", p=128)).then_inc(ld_wout, 16)
        sp.wait_ge(cv_psum, 12)
        load_expert(1, 0, 0)
        sp.wait_ge(cv_psum, 24)
        load_expert(1, 0, 1)
        sp.wait_ge(cv_lsb, 1)
        sp.dma_start(t["new_conv_prompt"].rearrange("l b t d -> (l b t) d"), ULT[0:2, :]).then_inc(st_out, 16)
        sp.dma_start(t["new_conv_sample"].rearrange("l b t d -> (l b t) d"), ULT[2:18, :]).then_inc(st_out, 16)
        sp.wait_ge(st_out, 32)
        sp.wait_ge(op_psum, 6)
        experts(1)
        for j, i in enumerate(STEPS):
            lo, n = TILES[i]
            sp.wait_ge(ln_done, 9 + j + 1)
            out = t["y_prompt"][0, lo:lo + n] if n == 128 else t["y_sample"].rearrange("b t d -> (b t) d")
            sp.dma_start(out, X[0:n, i, :]).then_inc(st_out, 16)
        sp.wait_ge(st_out, 80)

    @block.gpsimd
    def _(pool):
        link = linker(pool, pool_own)
        nc.gpsimd.memset(ZERO.bitcast(I32), NTOK).then_inc(zero_set, 1)
        nc.gpsimd.memset(NEGH, -0.5).then_inc(zero_set, 1)
        pool.wait_ge(zero_set, 2)
        nc.gpsimd.iota(TOKI.bitcast(I32), pattern=[[128, 3]], base=0, channel_multiplier=1).then_inc(zero_set, 1)
        for layer in range(DEPTH):
            pool.dma_start(slot_tok_d[layer].rearrange("(p n) o -> p (n o)", p=128), ZERO.bitcast(I32)).then_inc(st_zero, 16)
        pool.wait_ge(proj_evac, len(PROJ))
        for u in range(2 * HB):
            h, qt = HA + u // 2, u % 2
            n = 128 * (qt + 1)
            if u == 0:
                pool.wait_ge(ld_bias, 16 * 10)
            pool.wait_ge(sel_ready, qt + 1)
            wait(pool, att_scored, 2 * HA + u - 3)
            nc.gpsimd.tensor_tensor(COMB[:, u % 4, 0:n], BM[:, h, 256 - n:256] if qt == 0 else BM[:, h, 0:n],
                                    SELM[:, qt, 0:n], ALU.add).then_inc(comb_ready, 1)
        for b in range(DEC_B):
            lo = SEQ + DEC_T * b
            wait(pool, smp_S, b - 1)
            nc.gpsimd.tensor_copy(KTB[b % 2][:, 0:4, PAST:NK_S], QKVT[:, KA:KA + 4, lo:lo + DEC_T])
            nc.gpsimd.tensor_copy(KTB[b % 2][:, 4, PAST:NK_S], QKVT[:, KB, lo:lo + DEC_T])
            nc.gpsimd.tensor_copy(KTB[b % 2][0:64, 5, PAST:NK_S], QKVT[0:64, KI, lo:lo + DEC_T]).then_inc(k_new, 1)
            if b == 1:
                pool.wait_ge(ld_pt, 16)
                pool.wait_ge(att_Oevac, HEADS // 2)
                for v in range(2, 6):
                    load_batch(pool, v, v_caches, VRAW[v], ld_v_pool)

        def rstd(k):
            for j, i in enumerate(STEPS):
                n = TILES[i][1]
                pool.wait_ge(ln_stat, 3 * k + j + 1)
                nc.gpsimd.tensor_tensor(RSTD[0:n, i:i + 1], VE[0:n, i:i + 1], NEGH[0:n], ALU.pow).then_inc(ln_rstd, 1)

        def experts(layer):
            base = NE * layer
            s = more[layer]
            pool.wait_ge(ro_slot, 2 * layer + 2)
            full = pool.value_load(FLAG[0:1, layer:layer + 1].bitcast(I32), min_val=0, max_val=1)
            pool.wait_ge(st_zero, 16 * DEPTH)
            pool.wait_ge(st_x, 48 * (layer + 1))
            with pool.If(full > 0):
                nc.gpsimd.memset(XG, 0.0).then_inc(s["zero"], 1)
                pool.wait_ge(s["zero"], 1)
                pool.wait_ge(zero_set, 3)
                for i, (_, n) in enumerate(TILES):
                    for k in range(2):
                        pool.indirect_dma_start(
                            out=slot_tok_d[layer], out_offset=bass.IndirectOffsetOnAxis(ap=SLOTI[0:n, 2 * i + k:2 * i + k + 1].bitcast(I32), axis=0),
                            in_=TOKI[0:n, i:i + 1].bitcast(I32), in_offset=None).then_inc(s["scat"], 16)
                pool.wait_ge(s["scat"], 96)
                with pool.Fori(1, PASSES) as r:
                    with pool.Fori(0, NE) as e:
                        n = (r - 1) * NE + e
                        pool.wait_ge(s["T"], n)
                        pool.dma_start(IDXC[0:CAP, 0:1].bitcast(I32), slot_tok_d[layer][bass.ds((r * NE + e) * CAP, CAP)]).then_inc(s["tok"], 16)
                        pool.wait_ge(s["tok"], 16 * (n + 1))
                        pool.sem_inc(pool_passed, 1)
                        pool.indirect_dma_start(
                            out=XG[0:CAP, :], out_offset=None, in_=xrows_d[layer],
                            in_offset=bass.IndirectOffsetOnAxis(ap=IDXC[0:CAP, 0:1].bitcast(I32), axis=0),
                            bounds_check=NTOK - 1, oob_is_err=False).then_inc(s["gath"], 16)
                pool.wait_ge(s["st"], 16 * n_more)
            with pool.Else():
                pool.nop()
            for k in range(2):
                pool.wait_ge(st_y[k], 16 * (NE // 2) * (layer + 1))
            for j in range(6):
                i = STEPS[j // 2]
                n, col = TILES[i][1], 2 * i + j % 2
                if j >= 4:
                    pool.wait_ge(y_used, 6 * layer + j - 3)
                with pool.If(full > 0):
                    pool.indirect_dma_start(
                        out=YG[0:n, j % 4, :], out_offset=None, in_=ymore_d[layer],
                        in_offset=bass.IndirectOffsetOnAxis(ap=SLOTM[0:n, col:col + 1].bitcast(I32), axis=0),
                        bounds_check=SLOTS - NE * CAP - 1, oob_is_err=False).then_inc(s["more"], 16)
                    pool.wait_ge(s["more"], 16 * (j + 1))
                with pool.Else():
                    pool.nop()
                pool.indirect_dma_start(
                    out=YG[0:n, j % 4, :], out_offset=None, in_=yslot_d[layer],
                    in_offset=bass.IndirectOffsetOnAxis(ap=SLOTI[0:n, col:col + 1].bitcast(I32), axis=0),
                    bounds_check=NE * CAP - 1, oob_is_err=False).then_inc(ygath[j % 4], 16)
            rstd(2 * layer + 1)

        rstd(0)
        experts(0)
        rstd(2)
        experts(1)

    @block.scalar
    def _(act):
        link = linker(act, act_own)

        def copy(out, in_):
            return nc.scalar.copy(out, in_)

        def silu(out, in_):
            return nc.scalar.activation(out, in_, ACT.Silu)

        act.wait_ge(rb_zero, 1)
        act.dma_start(RB[0:32, 0:16], t["rel_bias"]).then_inc(ld_rb, 16)
        act.dma_start(PGT[0:1, :].bitcast(I32), t["page_table"].rearrange("(o b) n -> o (b n)", o=1)).then_inc(ld_pt, 16)
        for i in range(DEPTH):
            act.dma_start(WR[:, i, :, 0:NG], t["w_router_group"][i].rearrange("(c p) n -> p c n", p=128)).then_inc(ld_small, 16)
            act.dma_start(WR[:, i, :, NG:NG + NE], t["w_router_expert"][i].rearrange("(c p) n -> p c n", p=128)).then_inc(ld_small, 16)
            act.dma_start(RBI[:, i, 0:NG], t["b_router_group"][i].partition_broadcast(128)).then_inc(ld_small, 16)
            act.dma_start(RBI[:, i, NG:NG + NE], t["b_router_expert"][i].partition_broadcast(128)).then_inc(ld_small, 16)

        def load_biases():
            act.wait_ge(st_tab, 16)

            def skew(offset, dims):
                return bass.AP(tensor=table_d.tensor, offset=offset, ap=dims)

            pitch = 17 * TABLE_W
            act.dma_start(BM, skew(DIST0 - 128, [[pitch - 1, 128], [TABLE_W, 17], [1, 256]])).then_inc(ld_bias, 16)
            for q in range(4):
                for g in range(2):
                    act.dma_start(SBIAS[32 * q:32 * q + 32, g, :],
                                  skew(DIST0 - PAST + 8 * g * TABLE_W, [[TABLE_W, 8], [pitch - 1, 4], [1, NK_S]])).then_inc(ld_bias, 16)
            act.dma_start(SMASK[0:NS, :], skew(DIST0 - PAST + 16 * TABLE_W, [[4 * pitch, 8], [pitch - 1, 4], [1, NK_S]])).then_inc(ld_bias, 16)

        def evac_xT(k, steps=range(3)):
            for j in steps:
                lo, n = TILES[STEPS[j]]
                for half in range(2):
                    act.wait_ge(xT_psum, 6 * k + 2 * j + half + 1)
                    copy(XT[:, 4 * half:4 * half + 4, lo:lo + n],
                         bank[XT_BANKS[half]][:, :].rearrange("p (c n) -> p c n", c=4)[:, :, 0:n]).then_inc(xT_evac, 1)

        def route(layer):
            for j, i in enumerate(STEPS):
                evac_xT(2 * layer + 1, [j])
                m, n = 3 * layer + j, TILES[i][1]
                act.wait_ge(ro_top, 2 * m + 1)
                nc.scalar.activation(L8[0:n, 0:NG], L8[0:n, 0:NG], ACT.Exp, bias=GT[0:n, 0:1],
                                     accum_out=GSUM[0:n, i:i + 1]).then_inc(ro_exp, 1)
                act.wait_ge(ro_top, 2 * m + 2)
                nc.scalar.activation(RR[0:n, i:i + 1], TOP8[0:n, 1:2], ACT.Exp, bias=GT[0:n, 1:2]).then_inc(ro_exp, 1)

        act.wait_ge(tab_psum, 1)
        copy(TAB[0:17, :], bank[7][0:17, 0:TABLE_W]).then_inc(tab_sb, 1)
        act.wait_ge(tab_sb, 1)
        act.dma_start(table_d.rearrange("p h n -> h p n"), TAB[0:17, :].unsqueeze(1).to_broadcast([17, 128, TABLE_W])).then_inc(st_tab, 16)
        evac_xT(0)
        for g, (_, _, n, chunk, tile, col) in enumerate(PROJ):
            if g == 12:
                load_biases()
            act.wait_ge(proj_psum, g + 1)
            src = bank[4 + g % 4]
            if (tile, n) == (2, 512):
                for r in range(4):
                    last = copy(V[0:NS, 2, n // 4 * r:n // 4 * (r + 1)], src[NS * r:NS * r + NS, 0:n // 4])
                last.then_inc(proj_evac, 1)
            elif chunk is None:
                rows = TILES[tile][1]
                copy(V[0:rows, tile, col:col + n], src[0:rows, 0:n]).then_inc(proj_evac, 1)
            elif chunk == KB:
                copy(QKVT[:, KB, :], src[:, 0:NTOK])
                copy(QKVT[0:64, KBS, :], src[64:128, 0:NTOK])
                copy(QKVT[64:128, KBS, :], src[0:64, 0:NTOK]).then_inc(proj_evac, 1)
            elif chunk == KI:
                copy(QKVT[0:64, KI, :], src[0:64, 0:NTOK])
                copy(QKVT[64:128, KI, :], src[0:64, 0:NTOK]).then_inc(proj_evac, 1)
            else:
                copy(QKVT[:, chunk, :], src[:, 0:NTOK]).then_inc(proj_evac, 1)
        for i in range(2 * HI):
            n = 128 * (i // HI + 1)
            act.wait_ge(idx_psum, i + 1)
            wait(act, idx_acc, i - 3)
            nc.scalar.activation(RELU[:, i % 4, 0:n], bank[i % 4][:, 0:n], ACT.Relu).then_inc(idx_relu, 1)

        def exps(u):
            n = 128 * (u % 2 + 1)
            act.wait_ge(att_scored, u + 1)
            nc.scalar.activation(PB[:, u % NP, 0:n], PB[:, u % NP, 0:n], ACT.Exp, bias=MX[:, u:u + 1], scale=-1.0,
                                 accum_out=SUM[:, u:u + 1]).then_inc(att_exp, 1)

        def evac_T(u):
            act.wait_ge(att_T, u + 1)
            wait(act, att_O, u - 1)
            copy(PTB[:, u % 2, 0:u % 2 + 1, :], bank[2 + u % 2][:, 0:128 * (u % 2 + 1)].rearrange("p (a b) -> p a b", b=128)).then_inc(att_Tevac, 1)

        for u in range(AHEAD):
            exps(u)
        for u in range(2 * HEADS):
            evac_T(u)
            if u + AHEAD < 2 * HEADS:
                exps(u + AHEAD)
            if u % 4 == 3:
                act.wait_ge(att_O, u + 1)
                copy(YT[:, u // 4, 0:SEQ], bank[4 + (u // 4) % 2][:, 0:SEQ]).then_inc(att_Oevac, 1)
        for b in range(DEC_B):
            wait(act, smp_S, b - 1)
            for j in range(3):
                g = 3 * b + j
                act.wait_ge(kt_psum, g + 1)
                src = bank[g % 4][:, :].rearrange("p (a b) -> p a b", b=128)
                if j < 2:
                    copy(KTB[b % 2][:, 0:4, 128 * j:128 * j + 128], src).then_inc(kt_evac, 1)
                else:
                    copy(KTB[b % 2][:, 4, 0:PAST], src[:, 0:2, :])
                    copy(KTB[b % 2][0:64, 5, 0:PAST], src[0:64, 2:4, :]).then_inc(kt_evac, 1)
            if b % 4 == 3:
                act.wait_ge(smp_S, b + 1)
                nc.scalar.activation(RIS[b // 4], bank[6][:, 0:NK_S], ACT.Relu).then_inc(smp_relu, 1)
        for js in ((0, 1), (2, 3)):
            for j in js:
                act.wait_ge(smp_scored, j + 1)
                nc.scalar.activation(PS4[:, j, :], PS4[:, j, :], ACT.Exp, bias=SMX[:, j:j + 1],
                                     accum_out=SSUM[:, j:j + 1]).then_inc(smp_exp, 1)
            for j in js:
                act.wait_ge(smp_T, j + 1)
                copy(PT[:, j, :, :], bank[2 + j % 2][:, 0:384].rearrange("p (a b) -> p a b", b=128)).then_inc(smp_Tevac, 1)
        for mixer in range(2):
            act.wait_ge(smp_yT, mixer + 1)
            copy(YT[:, 4 * mixer:4 * mixer + 4, SEQ:NTOK],
                 bank[4 + mixer][:, 0:4 * NS].rearrange("p (c n) -> p c n", c=4)).then_inc(smp_y, 1)

        def experts(layer):
            base = NE * layer
            def store(row0, table, y, done):
                return act.dma_start(table[bass.ds(row0, CAP)].rearrange("j (h n) -> h j n", h=2),
                                     y).then_inc(done, 16)

            def gathered(i, v):
                Q = base // 2 + 3 * i + v
                act.wait_ge(xg_T, Q + 1)
                wait(act, gu_psum, 2 * Q - 4)
                for half in range(2):
                    last = copy(XGT[v][:, 4 * half:4 * half + 4, :],
                                bank[half][:, 0:8 * CAP].rearrange("p (c n) -> p c n", c=4))
                last.then_inc(xg_evac, 1)

            def output(i, u):
                E, k = base + number(i, u), u % 2
                act.wait_ge(dn_psum, E + 1)
                wait(act, st_y[k], store_count(layer, i, u) - 16)
                copy(YO[0:2 * CAP, k, :], bank[6 + k][0:2 * CAP, :]).then_inc(y_evac, 1)
                act.wait_ge(y_evac, E + 1)
                store(number(i, u) * CAP, yslot_d[layer], YO[0:2 * CAP, k, :], st_y[k])

            def step(i, u, before, nxt):
                E, k = base + number(i, u), u % 2
                act.wait_ge(gu_psum, E + 1)
                wait(act, ht_T, E - 1)
                silu(HID[CAP:2 * CAP, k, :], bank[2 + k][0:CAP, :]).then_inc(silu_done, 1)
                if before is not None:
                    output(*before)
                if nxt is not None:
                    gathered(*nxt)

            gathered(0, 0)
            for u in range(6):
                step(0, u, (0, u - 1) if u else None, (0, u // 2 + 1) if u in (0, 2) else (1, 0) if u == 4 else None)
            with act.Fori(1, NE // 6) as i:
                for u in range(6):
                    step(i, u, (i, u - 1) if u else (i - 1, 5), (i, u // 2 + 1) if u in (0, 2) else (i + 1, 0) if u == 4 else None)
            for u in range(NE % 6):
                step(NE // 6, u, (NE // 6, u - 1) if u else (NE // 6 - 1, 5), None)
            output(NE // 6, NE % 6 - 1)
            s = more[layer]
            full = act.value_load(FLAG[0:1, layer:layer + 1].bitcast(I32), min_val=0, max_val=1)
            for k in range(2):
                act.wait_ge(st_y[k], 16 * (NE // 2) * (layer + 1))
            with act.If(full > 0):
                with act.Fori(1, PASSES) as r:
                    with act.Fori(0, NE) as e:
                        n = (r - 1) * NE + e
                        act.wait_ge(s["T"], n + 1)
                        copy(XGT[0][:, :, 0:CAP], bank[0][:, 0:DC * CAP].rearrange("p (c n) -> p c n", c=DC)).then_inc(s["Tevac"], 1)
                        act.wait_ge(s["gu"], n + 1)
                        silu(HID[CAP:2 * CAP, 0, :], bank[2][0:CAP, :]).then_inc(s["silu"], 1)
                        act.wait_ge(s["dn"], n + 1)
                        act.wait_ge(s["st"], 16 * n)
                        copy(YO[0:2 * CAP, 0, :], bank[6][0:2 * CAP, :]).then_inc(s["y"], 1)
                        act.wait_ge(s["y"], n + 1)
                        store(n * CAP, ymore_d[layer], YO[0:2 * CAP, 0, :], s["st"])
                act.wait_ge(s["st"], 16 * n_more)
            with act.Else():
                act.nop()
            for j, i in enumerate(STEPS):
                n = TILES[i][1]
                y0 = YG[0:n, 2 * j % 4, :]
                act.wait_ge(ygath[2 * j % 4], ygath_count(layer, 2 * j))
                nc.scalar.activation(y0, y0, ACT.Copy, scale=GATE[0:n, 2 * i:2 * i + 1]).then_inc(y_gated, 1)

        route(0)
        experts(0)
        act.dma_start(SCW[0:16, :], t["state_conv"].rearrange("l b w d -> (l b w) d")).then_inc(ld_state, 16)
        act.dma_start(SCW[16:19, :], t["conv_w"][0]).then_inc(ld_state, 16)
        act.wait_ge(cv_in_T, 1)
        copy(SCT, bank[7][:, 0:DC * 19].rearrange("p (c n) -> p c n", c=DC)).then_inc(cv_in, 1)
        evac_xT(2)
        for j in range(DC):
            k = j % 2
            act.wait_ge(cv_psum, 3 * j + 1)
            wait(act, cv_u, j - 1)
            copy(HSB[:, k, :], bank[3 * k][:, 0:NTOK]).then_inc(cv_h, 1)
        act.wait_ge(cv_lT, 1)
        copy(ULT[0:18, 0:512], bank[6][0:18, :])
        copy(ULT[0:18, 512:D], bank[7][0:18, :]).then_inc(cv_lsb, 1)
        route(1)
        experts(1)

    @block.vector
    def _(dve):
        link = linker(dve, dve_own)
        V_ = nc.vector
        V_.memset(RB[0:33, :], 0.0).then_inc(rb_set, 1)
        dve.wait_ge(rb_set, 1)
        V_.memset(RB[32:33, :], NEG).then_inc(rb_zero, 1)
        for g in range(6):
            dve.wait_ge(ktok_psum, g + 1)
            i, part = g // 2, g % 2
            n = TILES[i][1]
            lo, cols = (0, 512) if part == 0 else (512, 192)
            V_.tensor_copy(KTOK[0:n, i, lo:lo + cols], bank[g % 4][0:n, 0:cols]).then_inc(ktok_evac, 1)
        for i in range(2 * HI):
            qt, h = i // HI, i % HI
            n = 128 * (qt + 1)
            acc, w = ACC[:, qt, 0:n], V[:, qt, 640 + h:641 + h]
            dve.wait_ge(idx_relu, i + 1)
            if h == 0:
                V_.tensor_scalar(acc, RELU[:, i % 4, 0:n], w, None, ALU.mult).then_inc(idx_acc, 1)
            else:
                V_.scalar_tensor_tensor(acc, RELU[:, i % 4, 0:n], w, acc, ALU.mult, ALU.add).then_inc(idx_acc, 1)
            dve.wait_ge(idx_acc, i + 1)
        dve.wait_ge(ld_bias, 16 * 10)

        def select_top(scores, rounds, rows):
            for _ in range(rounds):
                link(V_.max(MX8[0:rows, :], scores))
                link(V_.match_replace(scores, MX8[0:rows, :], scores, TAKEN))

        def select_prompt(r):
            qt = r // ROUNDS_P
            n = 128 * (qt + 1)
            acc = ACC[:, qt, 0:n]
            if r % ROUNDS_P == 0:
                link(V_.scalar_tensor_tensor(acc, acc, IDX_SCALE, BM[:, 16, 128:256] if qt == 0 else BM[:, 16, :], ALU.mult, ALU.add))
            select_top(acc, 1, 128)
            if r % ROUNDS_P == ROUNDS_P - 1:
                V_.tensor_scalar(SELM[:, qt, 0:n], acc, TAKEN / 2, NEG, ALU.is_ge, ALU.mult).then_inc(sel_ready, 1)

        def score(u):
            h, qt = u // 2, u % 2
            n = 128 * (qt + 1)
            dve.wait_ge(att_S, u + 1)
            wait(dve, att_T, u - NP + 1)
            if h < HA:
                bias = BM[:, h, 128:256] if qt == 0 else BM[:, h, :]
            else:
                dve.wait_ge(comb_ready, u - 2 * HA + 1)
                bias = COMB[:, u % 4, 0:n]
            V_.tensor_tensor_reduce(PB[:, u % NP, 0:n], bank[S_BANKS[u % NSB]][:, 0:n], bias, -QK_SCALE, 3e38,
                                    ALU.add, ALU.min, MX[:, u:u + 1]).then_inc(att_scored, 1)

        def norm(u):
            n = 128 * (u % 2 + 1)
            dve.wait_ge(att_exp, u + 1)
            link(V_.reciprocal(RIN[:, u:u + 1], SUM[:, u:u + 1]))
            V_.tensor_scalar(PB[:, u % NP, 0:n], PB[:, u % NP, 0:n], RIN[:, u:u + 1], None, ALU.mult).then_inc(att_p, 1)

        for u in range(AHEAD):
            score(u)
        for u in range(2 * HEADS):
            norm(u)
            for r in range(SELECT * u, min(SELECT * (u + 1), 2 * ROUNDS_P)):
                select_prompt(r)
            if u + AHEAD < 2 * HEADS:
                score(u + AHEAD)
        V_.memset(QAS, 0.0)
        V_.memset(QBS, 0.0).then_inc(q_zero, 1)
        dve.wait_ge(q_zero, 1)
        for h in range(HA):
            p, c = 64 * (h % 2), h // 2
            kv = 64 * (h // (HB // KVB))

            def cut(lo, chunk):
                return QKVT[lo:lo + 64, chunk, SEQ:NTOK].rearrange("p (b q) -> p b q", b=DEC_B)
            V_.tensor_copy(QAS[p:p + 64, c, :, 4 * h:4 * h + 4], cut(p, QA + c))
            V_.tensor_copy(QBS[kv:kv + 64, :, 4 * h:4 * h + 4], cut(p, QB + c))
            last = V_.tensor_copy(QIS[0:64, :, 4 * h:4 * h + 4], cut(p, QI + c))
        last.then_inc(q_cut, 1)
        dve.wait_ge(w_psum, 1)
        for g in range(2):
            link(V_.tensor_tensor(WVT, bank[7][:, 8 * g:8 * g + 8], HM, ALU.mult))
            link(V_.tensor_reduce(WV[:, g:g + 1], WVT, AX.X, ALU.add))
            V_.tensor_scalar(WM[:, g, :], PAT[:, 32 * g:32 * g + 32], WV[:, g:g + 1], None, ALU.mult).then_inc(w_mat, 1)
        for g in range(2):
            dve.wait_ge(smp_S, 4 * g + 4)
            link(V_.tensor_tensor_reduce(PS4[:, g, :], bank[4][:, 0:NK_S], SBIAS[:, 0, :], QK_SCALE, -3e38,
                                         ALU.add, ALU.max, SMX[:, g:g + 1]))
            V_.tensor_scalar(SMX[:, g:g + 1], SMX[:, g:g + 1], -1.0, None, ALU.mult).then_inc(smp_scored, 1)
            V_.tensor_tensor(PS4[:, 2 + g, :], bank[5][:, 0:NK_S], SBIAS[:, 1, :], ALU.add).then_inc(smp_Sevac, 1)

        def norm_sample(j):
            g = j % 2
            dve.wait_ge(smp_exp, j + 1)
            link(V_.reciprocal(SRIN[:, j:j + 1], SSUM[:, j:j + 1]))
            link(V_.tensor_scalar(PS4[:, j, :], PS4[:, j, :], SRIN[:, j:j + 1], None, ALU.mult))
            V_.tensor_tensor(PN[:, j, :].rearrange("p (b q) -> p b q", b=DEC_B),
                             PS4[:, j, PAST:NK_S].unsqueeze(1).to_broadcast([128, DEC_B, DEC_T]),
                             NEW[:, 32 * g:32 * g + 32].rearrange("p (b q) -> p b q", b=DEC_B), ALU.mult).then_inc(smp_p, 1)

        norm_sample(0)
        norm_sample(1)
        dve.wait_ge(sc_psum, 1)
        V_.memset(SCS[0:NS, NK_S:NK_S + PADS_S], -TAKEN)
        link(V_.scalar_tensor_tensor(SCS[0:NS, 0:NK_S], bank[7][0:NS, 0:NK_S], IDX_SCALE, SMASK[0:NS, :], ALU.mult, ALU.add))
        select_top(SCS[0:NS, :], ROUNDS_S, NS)
        V_.tensor_scalar(SMASK[0:NS, :], SCS[0:NS, 0:NK_S], TAKEN / 2, NEG, ALU.is_ge, ALU.mult).then_inc(sc_mask, 1)
        mask = HM.unsqueeze(2).to_broadcast([128, 8, HD])
        for g in range(2):
            dve.wait_ge(smp_O, g + 1)
            V_.tensor_tensor(OM[:, 0, g, :].rearrange("p (h d) -> p h d", h=HA),
                             bank[4 + g][:, :].rearrange("p (h d) -> p h d", h=HA), mask, ALU.mult).then_inc(smp_cut, 1)
        dve.wait_ge(smp_Sevac, 2)
        for g in range(2):
            dve.wait_ge(rep_psum, g + 1)
            link(V_.tensor_tensor_reduce(PS4[:, 2 + g, :], bank[6 + g][:, 0:NK_S], PS4[:, 2 + g, :], QK_SCALE, -3e38,
                                         ALU.add, ALU.max, SMX[:, 2 + g:3 + g]))
            V_.tensor_scalar(SMX[:, 2 + g:3 + g], SMX[:, 2 + g:3 + g], -1.0, None, ALU.mult).then_inc(smp_scored, 1)
        norm_sample(2)
        norm_sample(3)
        for g in range(2):
            dve.wait_ge(smp_O, 2 + g + 1)
            for kv in range(KVB):
                heads = slice(HB // KVB * kv, HB // KVB * (kv + 1))
                last = V_.tensor_tensor(OM[:, 1, g, :].rearrange("p (h d) -> p h d", h=HB)[:, heads, :],
                                        bank[6 + g][:, HD * kv:HD * kv + HD].unsqueeze(1).to_broadcast([128, HB // KVB, HD]),
                                        mask[:, heads, :], ALU.mult)
            last.then_inc(smp_cut, 1)

        def norm_rows(k, j):
            i = STEPS[j]
            n = TILES[i][1]
            x = X[0:n, i, :]
            V_.bn_stats(STATS[0:n, 0:6], X[0:n, i, 0:512])
            link(V_.bn_stats(STATS[0:n, 6:12], X[0:n, i, 512:D]))
            link(V_.bn_aggr(MV[0:n, i, :], STATS[0:n, :]))
            V_.tensor_scalar(VE[0:n, i:i + 1], MV[0:n, i, 1:2], EPS, None, ALU.add).then_inc(ln_stat, 1)
            dve.wait_ge(ld_ln, 32 * (k + 1))
            link(V_.scalar_tensor_tensor(x, x, MV[0:n, i, 0:1], LNP[0:n, 0, :], ALU.subtract, ALU.mult))
            dve.wait_ge(ln_rstd, 3 * k + j + 1)
            V_.scalar_tensor_tensor(x, x, RSTD[0:n, i:i + 1], LNP[0:n, 1, :], ALU.mult, ALU.add).then_inc(ln_done, 1)

        def mixed(layer, j):
            i = STEPS[j]
            n = TILES[i][1]
            dve.wait_ge(op_psum, 3 * layer + j + 1)
            parts = ([bank[2 * i + half][:, :] for half in range(2)] if n == 128
                     else [bank[4][NS * r:NS * r + NS, 0:D // 4] for r in range(4)])
            for r, y in enumerate(parts):
                w = D // len(parts)
                x = X[0:n, i, w * r:w * r + w]
                last = V_.scalar_tensor_tensor(x, x, ALPHA, y, ALU.mult, ALU.add)
            link(last)
            norm_rows(2 * layer, j)

        def choose(layer, j):
            i, m = STEPS[j], 3 * layer + j
            n = TILES[i][1]
            if j > 0:
                dve.wait_ge(ro_exp, 2 * m)
            dve.wait_ge(ro_psum, m + 1)
            link(V_.tensor_tensor(LG[0:n, :], bank[LG_BANKS[j]][0:n, 0:NG + NE], RBI[0:n, layer, :], ALU.add))
            link(V_.tensor_copy(L8[0:n, 0:NG], LG[0:n, 0:NG]))
            link(V_.max(TOP8[0:n, :], L8[0:n, :]))
            link(V_.max_index(GIX[0:n, :].bitcast(U32), TOP8[0:n, :], L8[0:n, :]))
            V_.tensor_scalar(GT[0:n, 0:1], TOP8[0:n, 0:1], -1.0, None, ALU.mult).then_inc(ro_top, 1)
            link(V_.tensor_copy(GT[0:n, 2:3], GIX[0:n, 0:1].bitcast(U32)))
            link(V_.tensor_scalar(PEN[0:n, :], IOTA[0:n, 0:NG], GT[0:n, 2:3], None, ALU.is_equal))
            link(V_.tensor_scalar(PEN[0:n, :], PEN[0:n, :], -1.0, -NEG, ALU.add, ALU.mult))
            le = LG[0:n, NG:NG + NE]
            link(V_.tensor_tensor(le.rearrange("p (g e) -> p g e", g=NG), le.rearrange("p (g e) -> p g e", g=NG),
                                  PEN[0:n, :].unsqueeze(2).to_broadcast([n, NG, EPG]), ALU.add))
            link(V_.max(TOP8[0:n, :], le))
            link(V_.max_index(EIX[0:n, :].bitcast(U32), TOP8[0:n, :], le))
            V_.tensor_scalar(GT[0:n, 1:2], TOP8[0:n, 0:1], -1.0, None, ALU.mult).then_inc(ro_top, 1)
            link(V_.tensor_copy(EF[0:n, 2 * i:2 * i + 2], EIX[0:n, 0:2].bitcast(U32)))
            for k in range(2):
                link(V_.tensor_scalar(HOTK[0:n, 2 * i + k, :], IOTA[0:n, :], EF[0:n, 2 * i + k:2 * i + k + 1], None, ALU.is_equal))
            V_.tensor_tensor(HOT[0:n, i, :], HOTK[0:n, 2 * i, :], HOTK[0:n, 2 * i + 1, :], ALU.add).then_inc(ro_hot, 1)

        def rank(layer, j):
            i = STEPS[j]
            n = TILES[i][1]
            dve.wait_ge(ro_rank, 3 * layer + j + 1)
            link(V_.tensor_tensor(RANKT[0:n], bank[RK_BANKS[j]][0:n, 0:NE].unsqueeze(1).to_broadcast([n, 2, NE]),
                                  HOTK[0:n, 2 * i:2 * i + 2, :], ALU.mult))
            link(V_.tensor_reduce(RK[0:n, 2 * i:2 * i + 2], RANKT[0:n], AX.X, ALU.add))

        def choose_rows(layer, i, v):
            q = 3 * i + v
            Q = NE // 2 * layer + q
            if not (isinstance(q, int) and q == 0):
                dve.wait_ge(oh_ready, Q)
                V_.tensor_scalar(SLOTQ, SLOTQ, float(-2 * CAP), None, ALU.add).then_inc(oh_slot, 1)
            dve.wait_ge(oh_slot, Q + 1)
            wait(dve, xg_T, Q - 2)
            for j, (_, n) in enumerate(TILES):
                last = V_.tensor_scalar(OHP[0:n, v, j, :], IOTA_PAIR[0:n], SLOTQ[0:n, 2 * j:2 * j + 1], None, ALU.is_equal)
            last.then_inc(oh_half, 1)
            dve.wait_ge(oh_half, Q + 1)
            for j, (_, n) in enumerate(TILES):
                last = V_.scalar_tensor_tensor(OHP[0:n, v, j, :], IOTA_PAIR[0:n], SLOTQ[0:n, 2 * j + 1:2 * j + 2], OHP[0:n, v, j, :],
                                               ALU.is_equal, ALU.add)
            last.then_inc(oh_ready, 1)

        def route(layer):
            for buf, value in ((L8, NEG), (RK, 0.0), (EF, 0.0)):
                last = V_.memset(buf, value)
            link(last)
            dve.wait_ge(ld_small, 8 * 16)
            mixed(layer, 0)
            mixed(layer, 1)
            choose(layer, 0)
            choose(layer, 1)
            rank(layer, 0)
            mixed(layer, 2)
            choose(layer, 2)
            rank(layer, 1)
            rank(layer, 2)
            link(V_.scalar_tensor_tensor(SLOTF, EF, float(CAP), RK, ALU.mult, ALU.add))
            link(V_.tensor_scalar(QQ, RK, float(CAP), float(SLOTS), ALU.is_ge, ALU.mult))
            V_.tensor_tensor(SLOTQ, SLOTF, QQ, ALU.add).then_inc(oh_slot, 1)
            choose_rows(layer, 0, 0)
            link(V_.memset(QQ, 0.0))
            for r in range(1, PASSES):
                link(V_.scalar_tensor_tensor(QQ, RK, float(r * CAP), QQ, ALU.is_ge, ALU.add))
            link(V_.scalar_tensor_tensor(SLOTF, QQ, float(NE * CAP - CAP), SLOTF, ALU.mult, ALU.add))
            V_.tensor_copy(SLOTI.bitcast(I32), SLOTF).then_inc(ro_slot, 1)
            link(V_.tensor_scalar(QQ, RK, float(CAP), -float(SLOTS + NE * CAP), ALU.is_lt, ALU.mult))
            link(V_.tensor_scalar(QQ, QQ, -1.0, -float(NE * CAP), ALU.mult, ALU.add))
            link(V_.tensor_tensor(SLOTF, SLOTF, QQ, ALU.add))
            V_.tensor_copy(SLOTM.bitcast(I32), SLOTF)
            link(V_.tensor_reduce(GT[0:1, 3:4], bank[RK_BANKS[2]][0:1, NE:2 * NE], AX.X, ALU.max))
            link(V_.tensor_scalar(GT[0:1, 4:5], GT[0:1, 3:4], float(CAP), None, ALU.is_gt))
            V_.tensor_copy(FLAG[0:1, layer:layer + 1].bitcast(I32), GT[0:1, 4:5]).then_inc(ro_slot, 1)
            dve.wait_ge(ro_exp, 6 * (layer + 1))
            for i, (_, n) in enumerate(TILES):
                link(V_.tensor_scalar(DEN[0:n, i:i + 1], RR[0:n, i:i + 1], 1.0, GSUM[0:n, i:i + 1], ALU.add, ALU.mult))
                link(V_.reciprocal(GATE[0:n, 2 * i:2 * i + 1], DEN[0:n, i:i + 1]))
                link(V_.tensor_tensor(GATE[0:n, 2 * i + 1:2 * i + 2], GATE[0:n, 2 * i:2 * i + 1], RR[0:n, i:i + 1], ALU.mult))

        def experts(layer):
            base = NE * layer

            def hidden(i, u):
                E, k = base + number(i, u), u % 2
                dve.wait_ge(silu_done, E + 1)
                h = HID[CAP:2 * CAP, k, :]
                V_.tensor_tensor(h, h, bank[2 + k][CAP:2 * CAP, :], ALU.mult).then_inc(h_done, 1)
                dve.wait_ge(ht_T, E + 1)
                wait(dve, dn_psum, E - 1)
                V_.tensor_copy(HT[:, k, :, :], bank[4 + k][:, 0:FC * CAP].rearrange("p (f n) -> p f n", f=FC)).then_inc(ht_evac, 1)

            def step(i, u, nxt):
                if nxt is not None:
                    choose_rows(layer, *nxt)
                hidden(i, u)

            for u in range(6):
                step(0, u, (0, u // 2 + 1) if u in (0, 2) else (1, 0) if u == 4 else None)
            with dve.Fori(1, NE // 6) as i:
                for u in range(6):
                    step(i, u, (i, u // 2 + 1) if u in (0, 2) else (i + 1, 0) if u == 4 else None)
            for u in range(NE % 6):
                step(NE // 6, u, None)
            s = more[layer]
            full = dve.value_load(FLAG[0:1, layer:layer + 1].bitcast(I32), min_val=0, max_val=1)
            with dve.If(full > 0):
                with dve.Fori(1, PASSES) as r:
                    with dve.Fori(0, NE) as e:
                        n = (r - 1) * NE + e
                        dve.wait_ge(s["silu"], n + 1)
                        V_.tensor_tensor(HID[CAP:2 * CAP, 0, :], HID[CAP:2 * CAP, 0, :], bank[2][CAP:2 * CAP, :], ALU.mult).then_inc(s["h"], 1)
                        dve.wait_ge(s["hT"], n + 1)
                        V_.tensor_copy(HT[:, 0, :, :], bank[4][:, 0:FC * CAP].rearrange("p (f n) -> p f n", f=FC)).then_inc(s["hTe"], 1)
                dve.wait_ge(s["st"], 16 * n_more)
            with dve.Else():
                dve.nop()
            for j, i in enumerate(STEPS):
                n = TILES[i][1]
                x, y0, y1 = X[0:n, i, :], YG[0:n, 2 * j % 4, :], YG[0:n, 2 * j % 4 + 1, :]
                done = 6 * layer + 2 * j
                dve.wait_ge(y_gated, 3 * layer + j + 1)
                dve.wait_ge(ygath[2 * j % 4 + 1], ygath_count(layer, 2 * j + 1))
                V_.scalar_tensor_tensor(y1, y1, GATE[0:n, 2 * i + 1:2 * i + 2], y0, ALU.mult, ALU.add).then_inc(y_used, 1)
                dve.wait_ge(y_used, done + 1)
                V_.scalar_tensor_tensor(x, x, ALPHA, y1, ALU.mult, ALU.add).then_inc(y_used, 1)
                dve.wait_ge(y_used, done + 2)
                norm_rows(2 * layer + 1, j)

        route(0)
        experts(0)
        for k in range(2):
            link(V_.memset(UB[:, k, 0:2], 0.0))
        dve.wait_ge(cv_in, 1)
        for j in range(DC):
            k = j % 2
            up, us = UB[:, k, 0:SEQ + 2], UB[:, k, SEQ + 2:].rearrange("p (b w) -> p b w", b=DEC_B)
            cp, cs = CB[:, k, 0:SEQ], CB[:, k, SEQ:NTOK].rearrange("p (b q) -> p b q", b=DEC_B)
            gate_c = bank[3 * k + 2]
            V_.tensor_copy(us[:, :, 0:2], SCT[:, j, 0:16].rearrange("p (b w) -> p b w", b=DEC_B))
            dve.wait_ge(cv_h, j + 1)
            dve.wait_ge(cv_psum, 3 * j + 3)
            V_.tensor_tensor(up[:, 2:], HSB[:, k, 0:SEQ], gate_c[:, 0:SEQ], ALU.mult)
            V_.tensor_tensor(us[:, :, 2:6], HSB[:, k, SEQ:NTOK].rearrange("p (b q) -> p b q", b=DEC_B),
                             gate_c[:, SEQ:NTOK].rearrange("p (b q) -> p b q", b=DEC_B), ALU.mult).then_inc(cv_u, 1)
            dve.wait_ge(cv_u, j + 1)
            w = [SCT[:, j, 16 + i:17 + i] for i in range(3)]
            V_.tensor_copy(UL[:, j, 0:2], up[:, SEQ:SEQ + 2])
            V_.tensor_copy(UL[:, j, 2:18].rearrange("p (b w) -> p b w", b=DEC_B), us[:, :, 4:6])
            link(V_.tensor_scalar(cp, up[:, 0:SEQ], w[0], None, ALU.mult))
            link(V_.tensor_scalar(cs, us[:, :, 0:4], w[0], None, ALU.mult))
            for i in (1, 2):
                link(V_.scalar_tensor_tensor(cp, up[:, i:i + SEQ], w[i], cp, ALU.mult, ALU.add))
                link(V_.scalar_tensor_tensor(cs, us[:, :, i:i + 4], w[i], cs, ALU.mult, ALU.add))
            V_.tensor_tensor(ZT[:, j, :], CB[:, k, :], bank[3 * k + 1][:, 0:NTOK], ALU.mult).then_inc(cv_z, 1)
        route(1)
        experts(1)

    @block.tensor
    def _(pe):
        mm = nc.tensor.matmul

        def tr(out, in_, n):
            return nc.tensor.transpose(out, in_, ID[0:n, 0:n] if n is not None else ID[CAP:2 * CAP, CAP:2 * CAP])

        pe.wait_ge(ld_const, 32)
        pe.wait_ge(ld_rb, 16)
        mm(bank[7][0:17, 0:TABLE_W], RB[0:33, :], OH[0:33, :], start=True, stop=True).then_inc(tab_psum, 1)

        def transpose_x(k, steps=range(3)):
            for j in steps:
                i = STEPS[j]
                n = TILES[i][1]
                for half in range(2):
                    m = 6 * k + 2 * j + half
                    wait(pe, xT_evac, m - 1)
                    for c in range(4):
                        last = tr(bank[XT_BANKS[half]][:, 128 * c:128 * c + n], X[0:n, i, 128 * (4 * half + c):128 * (4 * half + c + 1)], n)
                    last.then_inc(xT_psum, 1)

        pe.wait_ge(ld_x, 32)
        transpose_x(0)
        pe.wait_ge(xT_evac, 6)
        pe.wait_ge(tab_sb, 1)
        for g, (load, lo, n, chunk, tile, _) in enumerate(PROJ):
            if g == 0 or PROJ[g - 1][0] != load:
                pe.wait_ge(ld_win[load % 3], 16 * (load // 3 + 1))
            wait(pe, proj_evac, g - 3)
            w = WIN[load % 3][:, :, lo:lo + n]
            out = bank[4 + g % 4]
            for c in range(DC):
                if (tile, n) == (2, 512):
                    for r in range(4):
                        last = mm(out[NS * r:NS * r + NS, 0:n // 4], XT[:, c, SEQ:NTOK], w[:, c, n // 4 * r:n // 4 * (r + 1)],
                                  start=c == 0, stop=c == DC - 1)
                elif chunk is None:
                    tok, rows = TILES[tile]
                    last = mm(out[0:rows, 0:n], XT[:, c, tok:tok + rows], w[:, c, :], start=c == 0, stop=c == DC - 1)
                else:
                    last = mm(out[0:n, 0:NTOK], w[:, c, :], XT[:, c, :], start=c == 0, stop=c == DC - 1)
            last.then_inc(proj_psum, 1)
        pe.wait_ge(proj_evac, len(PROJ))
        for g in range(6):
            (lo, n), part = TILES[g // 2], g % 2
            wait(pe, ktok_evac, g - 3)
            out = bank[g % 4]
            if part == 0:
                for c in range(4):
                    last = tr(out[0:n, 128 * c:128 * c + 128], QKVT[:, KA + c, lo:lo + n], 128)
            else:
                tr(out[0:n, 0:128], QKVT[:, KB, lo:lo + n], 128)
                last = tr(out[0:n, 128:192], QKVT[0:64, KI, lo:lo + n], 64)
            last.then_inc(ktok_psum, 1)
        pe.wait_ge(ktok_evac, 6)
        for i in range(2 * HI):
            qt, h = i // HI, i % HI
            p, n = 64 * (h % 2), 128 * (qt + 1)
            wait(pe, idx_relu, i - 3)
            mm(bank[i % 4][:, 0:n], QKVT[p:p + 64, QI + h // 2, 128 * qt:128 * qt + 128], QKVT[p:p + 64, KI, 0:n],
               start=True, stop=True).then_inc(idx_psum, 1)
        pe.wait_ge(idx_relu, 2 * HI)

        def scores(u):
            h, qt = u // 2, u % 2
            n, p = 128 * (qt + 1), 64 * (h % 2)
            if h < HA:
                q, k = QA + h // 2, KA + h // 2
            else:
                b = h - HA
                q, k = QB + b // 2, KB if b % 2 == b // (HB // KVB) else KBS
            wait(pe, att_scored, u - NSB + 1)
            mm(bank[S_BANKS[u % NSB]][:, 0:n], QKVT[p:p + 64, q, 128 * qt:128 * qt + 128], QKVT[p:p + 64, k, 0:n],
               start=True, stop=True).then_inc(att_S, 1)

        def transpose_p(u):
            pe.wait_ge(att_p, u + 1)
            wait(pe, att_Tevac, u - 1)
            for kt in range(u % 2 + 1):
                last = tr(bank[2 + u % 2][:, 128 * kt:128 * kt + 128], PB[:, u % NP, 128 * kt:128 * kt + 128], 128)
            last.then_inc(att_T, 1)

        def values(u):
            h, qt = u // 2, u % 2
            pe.wait_ge(att_Tevac, u + 1)
            if u % 4 == 0:
                wait(pe, att_Oevac, u // 4 - 1)
            col = 64 * h if h < HA else 512 + 64 * ((h - HA) // (HB // KVB))
            out = bank[4 + (h // 2) % 2][64 * (h % 2):64 * (h % 2) + 64, 128 * qt:128 * qt + 128]
            for kt in range(qt + 1):
                last = mm(out, V[:, kt, col:col + 64], PTB[:, u % 2, kt, :], start=kt == 0, stop=kt == qt)
            last.then_inc(att_O, 1)

        for u in range(AHEAD):
            scores(u)
        for u in range(2 * HEADS):
            if u + AHEAD < 2 * HEADS:
                scores(u + AHEAD)
            transpose_p(u)
            if u >= 1:
                values(u - 1)
        values(2 * HEADS - 1)
        def project_small(feat, w):
            lo = TILES[2][0]
            for c in range(DC):
                for r in range(4):
                    last = mm(bank[4][NS * r:NS * r + NS, 0:D // 4], feat[:, c, lo:lo + NS],
                              w[:, c, D // 4 * r:D // 4 * (r + 1)], start=c == 0, stop=c == DC - 1)
            last.then_inc(op_psum, 1)

        def project(i, half, feat, w, chunks=range(DC)):
            lo, n = TILES[i]
            for c in chunks:
                last = mm(bank[2 * i + half][0:n, :], feat[:, c, lo:lo + n], w[:, c, 512 * half:512 * half + 512],
                          start=c == 0, stop=c == DC - 1)
            if half == 1 and chunks[-1] == DC - 1:
                last.then_inc(op_psum, 1)

        pe.wait_ge(att_Oevac, HEADS // 2)
        for g in range(2):
            last = mm(bank[7][:, 8 * g:8 * g + 8], REP[0:NS, 128 * g:128 * g + 128], V[0:NS, 2, 640:648], start=True, stop=True)
        last.then_inc(w_psum, 1)
        pe.wait_ge(q_cut, 1)

        def transpose_keys(b):
            pe.wait_ge(ld_k[b % 3], 16 * 3 * N_PAGES * (b // 3 + 1))
            for j in range(3):
                g = 3 * b + j
                wait(pe, kt_evac, g - 3)
                if j < 2:
                    for c in range(4):
                        last = tr(bank[g % 4][:, 128 * c:128 * c + 128], KRAW[b % 3][:, j, 128 * c:128 * c + 128], 128)
                else:
                    for pg in range(N_PAGES):
                        tr(bank[g % 4][:, 128 * pg:128 * pg + 128], KRAW[b % 3][:, pg, 512:640], 128)
                        last = tr(bank[g % 4][0:64, 256 + 128 * pg:384 + 128 * pg], KRAW[b % 3][:, pg, 640:704], 128)
                last.then_inc(kt_psum, 1)

        transpose_keys(0)
        for b in range(DEC_B):
            if b + 1 < DEC_B:
                transpose_keys(b + 1)
            pe.wait_ge(kt_evac, 3 * b + 3)
            pe.wait_ge(k_new, b + 1)
            if b == 4:
                pe.wait_ge(smp_Sevac, 1)
                pe.wait_ge(smp_relu, 1)
            rows = slice(32 * (b % 4), 32 * (b % 4) + 32)
            for c in range(4):
                mm(bank[4][rows, 0:NK_S], QAS[:, c, b, :], KTB[b % 2][:, c, :], start=c == 0, stop=c == 3)
            mm(bank[5][rows, 0:NK_S], QBS[:, b, :], KTB[b % 2][:, 4, :], start=True, stop=True)
            mm(bank[6][rows, 0:NK_S], QIS[0:64, b, :], KTB[b % 2][0:64, 5, :], start=True, stop=True).then_inc(smp_S, 1)
        pe.wait_ge(smp_relu, 2)
        pe.wait_ge(w_mat, 2)
        for g in range(2):
            last = mm(bank[7][0:NS, 0:NK_S], WM[:, g, :], RIS[g], start=g == 0, stop=g == 1)
        last.then_inc(sc_psum, 1)

        def transpose_sample(j):
            pe.wait_ge(smp_p, j + 1)
            for kt in range(2):
                tr(bank[2 + j % 2][:, 128 * kt:128 * kt + 128], PS4[:, j, 128 * kt:128 * kt + 128], 128)
            tr(bank[2 + j % 2][0:NS, 256:384], PN[:, j, :], 128).then_inc(smp_T, 1)

        def values_sample(mixer, g, lo, n):
            for kt in range(3):
                for r in range(4):
                    rows = slice(32 * r, 32 * r + 32)
                    v = VRAW[4 * g + r][:, kt, lo:lo + n] if kt < 2 else V[0:NS, 2, lo:lo + n]
                    p = PT[:, 2 * mixer + g, kt, rows] if kt < 2 else PT[0:NS, 2 * mixer + g, 2, rows]
                    last = mm(bank[4 + 2 * mixer + g][rows, 0:n], p, v, start=kt == 0, stop=kt == 2)
            last.then_inc(smp_O, 1)

        def to_tokens(mixer):
            pe.wait_ge(smp_cut, 2 * mixer + 2)
            for c in range(4):
                for g in range(2):
                    last = mm(bank[4 + mixer][:, NS * c:NS * c + NS], OM[:, mixer, g, 128 * c:128 * c + 128],
                              PAT[:, 32 * g:32 * g + 32], start=g == 0, stop=g == 1)
            last.then_inc(smp_yT, 1)

        for j in range(2):
            transpose_sample(j)
        pe.wait_ge(smp_Tevac, 2)
        for g in range(2):
            pe.wait_ge(ld_v, 16 * 2 * N_PAGES * 2 * (g + 1))
            pe.wait_ge(ld_v_pool, 16 * 2 * N_PAGES * 4)
            values_sample(0, g, 0, 512)
            if g == 0:
                pe.wait_ge(ld_wout, 16)
                project(0, 0, YT, WOUT)
        pe.wait_ge(sc_mask, 1)
        for g in range(2):
            mm(bank[6 + g][:, 0:NK_S], REP[0:NS, 128 * g:128 * g + 128], SMASK[0:NS, :], start=True, stop=True).then_inc(rep_psum, 1)
        to_tokens(0)
        project(0, 1, YT, WOUT, range(0, 4))
        for j in range(2, 4):
            transpose_sample(j)
        pe.wait_ge(smp_Tevac, 4)
        for g in range(2):
            values_sample(1, g, 512, 128)
        project(0, 1, YT, WOUT, range(4, DC))
        to_tokens(1)

        def logits(layer, j):
            k, (lo, n) = 2 * layer + 1, TILES[STEPS[j]]
            pe.wait_ge(ln_done, 6 * layer + j + 1)
            transpose_x(k, [j])
            pe.wait_ge(xT_evac, 6 * k + 2 * j + 2)
            for c in range(DC):
                last = mm(bank[LG_BANKS[j]][0:n, 0:NG + NE], XT[:, c, lo:lo + n], WR[:, layer, c, :], start=c == 0, stop=c == DC - 1)
            last.then_inc(ro_psum, 1)

        def ranks(layer, j):
            pe.wait_ge(ro_hot, 3 * layer + j + 1)
            out, (_, n) = bank[RK_BANKS[j]], TILES[STEPS[j]]
            for q in range(j):
                rows = TILES[STEPS[q]][1]
                mm(out[0:n, 0:NE], ONE[0:rows, 0:n], HOT[0:rows, STEPS[q], :], start=q == 0, stop=False)
            last = mm(out[0:n, 0:NE], TRI[0:n, 0:n], HOT[0:n, STEPS[j], :], start=j == 0, stop=True)
            if j == 2:
                for q in range(3):
                    rows = TILES[STEPS[q]][1]
                    last = mm(out[0:1, NE:2 * NE], ONE[0:rows, 0:1], HOT[0:rows, STEPS[q], :], start=q == 0, stop=q == 2)
            last.then_inc(ro_rank, 1)

        def mix_and_route(layer, feat, w):
            if layer == 1:
                project(0, 0, feat, w)
                project(0, 1, feat, w)
            project_small(feat, w)
            pe.wait_ge(ld_small, 8 * 16)
            if layer == 1:
                pe.wait_ge(cv_lsb, 1)
            logits(layer, 0)
            project(1, 0, feat, w)
            logits(layer, 1)
            ranks(layer, 0)
            project(1, 1, feat, w)
            logits(layer, 2)
            ranks(layer, 1)
            ranks(layer, 2)

        def experts(layer):
            base = NE * layer

            def chunk(x, c):
                return x.rearrange("n (p c) -> n p c", c=DC)[:, :, c]

            def choose_tokens(v):
                for c in range(DC):
                    for j, (_, n) in enumerate(TILES):
                        last = mm(bank[c // 4][:, 2 * CAP * (c % 4):2 * CAP * (c % 4 + 1)], chunk(X[0:n, j, :], c), OHP[0:n, v, j, :],
                                  start=j == 0, stop=j == 2)
                return last

            def gate_up(x, wg, wu, out, up_ready=None):
                for c in range(DC):
                    mm(out[0:CAP, :], x[:, c, :], wg[:, c, :], start=c == 0, stop=c == DC - 1)
                    if c == 0 and up_ready is not None:
                        pe.wait_ge(*up_ready)
                    last = mm(out[CAP:2 * CAP, :], x[:, c, :], wu[:, c, :], start=c == 0, stop=c == DC - 1)
                return last

            def transpose_h(h, out):
                for f in range(FC):
                    last = tr(out[:, CAP * f:CAP * f + CAP], h[:, 128 * f:128 * f + 128], None)
                return last

            def down(h, wd, out):
                for f in range(FC):
                    for half in range(2):
                        last = mm(out[CAP * half:CAP * half + CAP, :], h[:, f, :], wd[:, f, 512 * half:512 * half + 512],
                                  start=f == 0, stop=f == FC - 1)
                return last

            def gathered(i, v):
                Q = base // 2 + 3 * i + v
                pe.wait_ge(oh_ready, Q + 1)
                wait(pe, xg_evac, Q)
                choose_tokens(v).then_inc(xg_T, 1)

            def output(i, u):
                E, k, s = base + number(i, u), u % 2, slot_of(layer, u)
                pe.wait_ge(ht_evac, E + 1)
                wait(pe, y_evac, E - 1)
                pe.wait_ge(ld_wd[s], slot_loads(layer, i, u))
                down(HT[:, k, :, :], WD[s], bank[6 + k]).then_inc(dn_psum, 1)

            def step(i, u, before, nxt):
                E, k, s, v = base + number(i, u), u % 2, slot_of(layer, u), u // 2
                pe.wait_ge(xg_evac, base // 2 + 3 * i + v + 1)
                wait(pe, h_done, E - 1)
                pe.wait_ge(ld_wg[s], slot_loads(layer, i, u))
                gate_up(XGT[v][:, :, CAP * k:CAP * k + CAP], WG[s], WU[s], bank[2 + k],
                        (ld_wu[s], slot_loads(layer, i, u))).then_inc(gu_psum, 1)
                if before is not None:
                    output(*before)
                pe.wait_ge(h_done, E + 1)
                wait(pe, ht_evac, E - 1)
                pe.sem_inc(pe_passed, 1)
                transpose_h(HID[CAP:2 * CAP, k, :], bank[4 + k]).then_inc(ht_T, 1)
                if nxt is not None:
                    gathered(*nxt)

            gathered(0, 0)
            step(0, 0, None, (0, 1))
            output(0, 0)
            for u in range(1, 6):
                step(0, u, (0, u - 1) if u > 1 else None, (0, 2) if u == 2 else (1, 0) if u == 4 else None)
            with pe.Fori(1, NE // 6) as i:
                for u in range(6):
                    step(i, u, (i, u - 1) if u else (i - 1, 5), (i, u // 2 + 1) if u in (0, 2) else (i + 1, 0) if u == 4 else None)
            for u in range(NE % 6):
                step(NE // 6, u, (NE // 6, u - 1) if u else (NE // 6 - 1, 5), None)
            output(NE // 6, NE % 6 - 1)
            s = more[layer]
            full = pe.value_load(FLAG[0:1, layer:layer + 1].bitcast(I32), min_val=0, max_val=1)
            pe.wait_ge(y_evac, base + NE)
            with pe.If(full > 0):
                with pe.Fori(1, PASSES) as r:
                    with pe.Fori(0, NE) as e:
                        n = (r - 1) * NE + e
                        pe.wait_ge(s["gath"], 16 * (n + 1))
                        pe.sem_inc(pe_passed, 1)
                        for c in range(DC):
                            last = tr(bank[0][:, CAP * c:CAP * c + CAP], chunk(XG[0:CAP, :], c), CAP)
                        last.then_inc(s["T"], 1)
                        pe.wait_ge(s["Tevac"], n + 1)
                        pe.wait_ge(s["w"], 48 * (n + 1))
                        gate_up(XGT[0][:, :, 0:CAP], WG[0], WU[0], bank[2]).then_inc(s["gu"], 1)
                        pe.wait_ge(s["h"], n + 1)
                        pe.sem_inc(pe_passed, 1)
                        transpose_h(HID[CAP:2 * CAP, 0, :], bank[4]).then_inc(s["hT"], 1)
                        pe.wait_ge(s["hTe"], n + 1)
                        pe.wait_ge(s["y"], n)
                        down(HT[:, 0, :, :], WD[0], bank[6]).then_inc(s["dn"], 1)
                pe.wait_ge(s["st"], 16 * n_more)
            with pe.Else():
                pe.nop()

        pe.wait_ge(smp_y, 2)
        pe.wait_ge(ld_wout, 16)
        mix_and_route(0, YT, WOUT)
        experts(0)
        pe.wait_ge(ld_state, 32)
        for c in range(DC):
            last = tr(bank[7][:, 19 * c:19 * c + 19], SCW[0:19, 128 * c:128 * c + 128], 19)
        last.then_inc(cv_in_T, 1)
        for j in range(3):
            pe.wait_ge(ln_done, 3 + j + 1)
            transpose_x(2, [j])
        pe.wait_ge(xT_evac, 18)
        for j in range(DC):
            half = j // 4
            if j % 4 == 0:
                pe.wait_ge(ld_wc[half], 48)
            wait(pe, cv_z, j - 1)
            for part in range(3):
                w = WC[3 * half + part]
                for c in range(DC):
                    last = mm(bank[3 * (j % 2) + part][:, 0:NTOK], w[:, c, 128 * (j % 4):128 * (j % 4) + 128], XT[:, c, :],
                              start=c == 0, stop=c == DC - 1)
                last.then_inc(cv_psum, 1)
        pe.wait_ge(cv_z, DC)
        pe.wait_ge(cv_in, 1)
        for c in range(DC):
            last = tr(bank[6 + c // 4][0:18, 128 * (c % 4):128 * (c % 4) + 128], UL[:, c, :], 128)
        last.then_inc(cv_lT, 1)
        pe.wait_ge(ld_wout, 32)
        mix_and_route(1, ZT, WCO)
        experts(1)


_INS = ["x_prompt", "x_sample", "cache_k_a", "cache_v_a", "cache_k_b", "cache_v_b", "cache_k_idx", "state_conv", "page_table",
        "rel_bias", "w_attn_in", "w_attn_out", "w_conv_in", "conv_w", "w_conv_out", "w_router_group", "b_router_group",
        "w_router_expert", "b_router_expert", "w_exp_gate", "w_exp_up", "w_exp_down", "ln_g", "ln_b"]
_OUTS = [("y_prompt", (1, SEQ, D)), ("y_sample", (DEC_B, DEC_T, D)),
         ("new_k_a_prompt", (1, 1, SEQ, HA, HD)), ("new_v_a_prompt", (1, 1, SEQ, HA, HD)),
         ("new_k_b_prompt", (1, 1, SEQ, KVB, HD)), ("new_v_b_prompt", (1, 1, SEQ, KVB, HD)),
         ("new_k_idx_prompt", (1, 1, SEQ, HD)), ("new_conv_prompt", (1, 1, 2, D)),
         ("new_k_a_sample", (1, DEC_B, DEC_T, HA, HD)), ("new_v_a_sample", (1, DEC_B, DEC_T, HA, HD)),
         ("new_k_b_sample", (1, DEC_B, DEC_T, KVB, HD)), ("new_v_b_sample", (1, DEC_B, DEC_T, KVB, HD)),
         ("new_k_idx_sample", (1, DEC_B, DEC_T, HD)), ("new_conv_sample", (1, DEC_B, 2, D))]


def kernel(**inputs):
    import concourse.bacc as bacc
    from concourse.bass_utils import run_bass_kernel_spmd as run

    nc = bacc.Bacc("TRN2", target_bir_lowering=False, num_devices=1)
    arrays, t = {}, {}
    arrays["consts"] = constants()
    for name in _INS:
        arrays[name] = np.ascontiguousarray(inputs[name])
    for name, a in arrays.items():
        t[name] = nc.dram_tensor(name, a.shape, mybir.dt.from_np(a.dtype), kind="ExternalInput").ap()
    for name, shape in _OUTS:
        t[name] = nc.dram_tensor(name, shape, F32, kind="ExternalOutput").ap()
    build(nc, t)
    r = run(nc, [arrays], core_ids=[0])
    return tuple(r.results[0][name] for name, _ in _OUTS)
```
